# Optimizing a Trainium2 kernel written in Bass

```python
import math
import jax, jax.numpy as jnp
from jax import lax
import numpy as np

D_MODEL = 1024
BATCH = 1
SEQ = 2048
DEPTH = 1

D_MIX = D_MODEL
HG_WIDTH = D_MIX // 2
HG_HEAD_DIM = 128
HG_HEADS = HG_WIDTH // HG_HEAD_DIM
HG_CHUNK = 64
SW_WIDTH = D_MIX - HG_WIDTH
SW_HEAD_DIM = 64
SW_Q_HEADS = SW_WIDTH // SW_HEAD_DIM
SW_KV_HEADS = SW_Q_HEADS // 4
SW_KV_WIDTH = SW_KV_HEADS * SW_HEAD_DIM
WINDOW = 128
ROPE_THETA = 500000.0
ROPE_DIM = SW_HEAD_DIM // 4
DN_ALPHA = (2.0 * DEPTH) ** 0.25
DN_BETA = (8.0 * DEPTH) ** -0.25
LN_EPS = 1e-5
RMS_EPS = 1e-6
IN_SIZES = (HG_WIDTH, HG_WIDTH, HG_WIDTH, HG_WIDTH, SW_WIDTH, SW_KV_WIDTH, SW_KV_WIDTH, SW_WIDTH)
IN_WIDTH = sum(IN_SIZES)
IN_SPLITS = tuple(int(s) for s in np.cumsum(IN_SIZES)[:-1])


def hgrn2_chunk(q, k, v, log_f):
    B, T, H, K = q.shape
    V = v.shape[-1]
    C = HG_CHUNK
    N = T // C
    q = q.reshape(B, N, C, H, K)
    k = k.reshape(B, N, C, H, K)
    v = v.reshape(B, N, C, H, V)
    log_f = log_f.reshape(B, N, C, H, K)
    G = jnp.cumsum(log_f, axis=2)
    G_last = G[:, :, -1]
    q_dec = q * jnp.exp(G)
    k_dec = k * jnp.exp(-G)
    causal = jnp.tril(jnp.ones((C, C), dtype=bool))
    A = jnp.einsum('bnthk,bnshk->bnhts', q_dec, k_dec)
    A = jnp.where(causal, A, 0.0)
    o_intra = jnp.einsum('bnhts,bnshv->bnthv', A, v)
    inc = jnp.einsum('bnshk,bnshv->bnhkv', k * jnp.exp(G_last[:, :, None] - G), v)
    decay = jnp.exp(G_last)

    def step(S, xs):
        d, u = xs
        return d[..., None] * S + u, S

    S0 = jnp.zeros((B, H, K, V), q.dtype)
    _, S_prev = lax.scan(step, S0, (jnp.moveaxis(decay, 1, 0), jnp.moveaxis(inc, 1, 0)))
    S_prev = jnp.moveaxis(S_prev, 0, 1)
    o_inter = jnp.einsum('bnthk,bnhkv->bnthv', q_dec, S_prev)
    return (o_intra + o_inter).reshape(B, T, H, V)

def partial_rope(x, cos, sin):
    half = ROPE_DIM // 2
    x1 = x[..., :half]
    x2 = x[..., half:ROPE_DIM]
    rot = jnp.concatenate([x1 * cos - x2 * sin, x2 * cos + x1 * sin], axis=-1)
    return jnp.concatenate([rot, x[..., ROPE_DIM:]], axis=-1)

def swa_with_sinks(q, k, v, sinks):
    B, T, Hq, D = q.shape
    Hkv = k.shape[2]
    G = Hq // Hkv
    W = WINDOW
    nb = T // W
    qb = q.reshape(B, nb, W, Hkv, G, D)
    pad = jnp.zeros((B, W, Hkv, D), k.dtype)
    kb = jnp.concatenate([pad, k], axis=1).reshape(B, nb + 1, W, Hkv, D)
    vb = jnp.concatenate([pad, v], axis=1).reshape(B, nb + 1, W, Hkv, D)
    kw = jnp.concatenate([kb[:, :-1], kb[:, 1:]], axis=2)
    vw = jnp.concatenate([vb[:, :-1], vb[:, 1:]], axis=2)
    s = jnp.einsum('bnqhgd,bnkhd->bnhgqk', qb, kw).astype(jnp.float32) * (D ** -0.5)
    t = jnp.arange(W)[:, None]
    j = jnp.arange(2 * W)[None, :]
    band = (j > t) & (j <= t + W)
    valid = (jnp.arange(nb)[:, None, None] > 0) | (j[None] >= W)
    mask = band[None] & valid
    s = jnp.where(mask[None, :, None, None], s, -jnp.inf)
    sink = sinks.astype(jnp.float32).reshape(1, 1, Hkv, G, 1, 1)
    m = jnp.maximum(jnp.max(s, axis=-1, keepdims=True), sink)
    p = jnp.exp(s - m)
    denom = jnp.sum(p, axis=-1, keepdims=True) + jnp.exp(sink - m)
    p = (p / denom).astype(v.dtype)
    o = jnp.einsum('bnhgqk,bnkhd->bnqhgd', p, vw)
    return o.reshape(B, T, Hq * D)

def first_inputs(seed: int = 0) -> dict:
    key = jax.random.key(seed)
    ks = jax.random.split(key, 8)
    x = jax.random.normal(ks[0], (BATCH, SEQ, D_MODEL), jnp.float32)
    col_scale = jnp.concatenate([
        jnp.ones((HG_WIDTH,)), jnp.ones((HG_WIDTH,)), jnp.full((HG_WIDTH,), DN_BETA), jnp.ones((HG_WIDTH,)),
        jnp.ones((SW_WIDTH,)), jnp.ones((SW_KV_WIDTH,)), jnp.full((SW_KV_WIDTH,), DN_BETA), jnp.ones((SW_WIDTH,)),
    ]).astype(jnp.float32)
    w_in = jax.random.normal(ks[1], (DEPTH, D_MODEL, IN_WIDTH), jnp.float32) * (D_MODEL ** -0.5) * col_scale
    lb_logits = 0.1 * jax.random.normal(ks[2], (DEPTH + 1, HG_WIDTH), jnp.float32)
    hg_norm_w = 1.0 + 0.02 * jax.random.normal(ks[3], (DEPTH, HG_WIDTH), jnp.float32)
    sinks = 0.5 * jax.random.normal(ks[4], (DEPTH, SW_Q_HEADS), jnp.float32)
    w_out = jax.random.normal(ks[5], (DEPTH, D_MIX, D_MODEL), jnp.float32) * (D_MIX ** -0.5) * DN_BETA
    ln_g = 1.0 + 0.02 * jax.random.normal(ks[6], (DEPTH, D_MODEL), jnp.float32)
    ln_b = 0.02 * jax.random.normal(ks[7], (DEPTH, D_MODEL), jnp.float32)
    return {"x": x, "w_in": w_in, "lb_logits": lb_logits, "hg_norm_w": hg_norm_w,
            "sinks": sinks, "w_out": w_out, "ln_g": ln_g, "ln_b": ln_b}

def first_block(x, w_in, lb_logits, hg_norm_w, sinks, w_out, ln_g, ln_b):
    B, T, _ = x.shape
    f32 = jnp.float32
    dt = x.dtype
    pos = jnp.arange(T, dtype=f32)
    inv_freq = ROPE_THETA ** (-jnp.arange(0, ROPE_DIM, 2, dtype=f32) / ROPE_DIM)
    ang = pos[:, None] * inv_freq[None, :]
    cos = jnp.cos(ang)[:, None, :].astype(dt)
    sin = jnp.sin(ang)[:, None, :].astype(dt)
    lower_bounds = jnp.cumsum(jax.nn.softmax(lb_logits.astype(f32), axis=0), axis=0)
    h_res = x
    for layer in range(DEPTH):
        h = jnp.einsum('btd,de->bte', h_res, w_in[layer])
        hq, hf, hi, hg, aq, ak, av, ag = jnp.split(h, IN_SPLITS, axis=-1)
        lb = lower_bounds[layer]
        f = lb + (1.0 - lb) * jax.nn.sigmoid(hf.astype(f32))
        log_f = jnp.log(f)
        k_in = 1.0 - f
        q_h = jax.nn.silu(hq.astype(f32))
        rs = lambda a: a.reshape(B, T, HG_HEADS, HG_HEAD_DIM)
        o_h = hgrn2_chunk(rs(q_h), rs(k_in), rs(hi.astype(f32)), rs(log_f))
        o_h = o_h * lax.rsqrt(jnp.mean(o_h * o_h, axis=-1, keepdims=True) + RMS_EPS)
        o_h = o_h * hg_norm_w[layer].astype(f32).reshape(HG_HEADS, HG_HEAD_DIM)
        o_h = o_h.reshape(B, T, HG_WIDTH).astype(dt) * jax.nn.silu(hg)
        q_a = partial_rope(aq.reshape(B, T, SW_Q_HEADS, SW_HEAD_DIM), cos, sin)
        k_a = partial_rope(ak.reshape(B, T, SW_KV_HEADS, SW_HEAD_DIM), cos, sin)
        v_a = av.reshape(B, T, SW_KV_HEADS, SW_HEAD_DIM)
        o_a = swa_with_sinks(q_a, k_a, v_a, sinks[layer]) * jax.nn.silu(ag)
        mix = jnp.concatenate([o_h, o_a], axis=-1)
        out = jnp.einsum('bte,ed->btd', mix, w_out[layer])
        z = DN_ALPHA * h_res.astype(f32) + out.astype(f32)
        mu = jnp.mean(z, axis=-1, keepdims=True)
        var = jnp.mean(jnp.square(z - mu), axis=-1, keepdims=True)
        z = (z - mu) * lax.rsqrt(var + LN_EPS)
        h_res = (z * ln_g[layer].astype(f32) + ln_b[layer].astype(f32)).astype(dt)
    return h_res


_first_inputs = first_inputs


def first_inputs(seed=0):
    import zlib

    import numpy as np

    out = dict(_first_inputs(seed))
    spreads = {}
    factors = {'lb_logits': 8.0, 'hg_norm_w': 8.0, 'sinks': 8.0, 'ln_g': 2.741, 'ln_b': 2.868}
    for name, (base, spread) in spreads.items():
        noise = np.random.default_rng([zlib.crc32(name.encode()), seed]).standard_normal(out[name].shape)
        drawn = base * np.exp(spread * noise) if base else spread * noise
        out[name] = __import__('jax').numpy.asarray(drawn.astype(out[name].dtype))
    for name, factor in factors.items():
        out[name] = (out[name] * factor).astype(out[name].dtype)
    return out


_narrow_inputs = first_inputs


def first_inputs(seed=0):

    out = dict(_narrow_inputs(seed))
    wider = {'hg_norm_w': 4.01, 'sinks': 12.0, 'ln_g': 3.09, 'ln_b': 3.08}
    for name, times in wider.items():
        mean = out[name].mean()
        out[name] = (mean + times * (out[name] - mean)).astype(out[name].dtype)
    return out


HEAD_DIM = 64
D_MIX_2 = D_MODEL
D_RWKV = D_MIX_2 // 2
D_FOX = D_MIX_2 - D_RWKV
H_RWKV = D_RWKV // HEAD_DIM
H_FOX = D_FOX // HEAD_DIM
DECAY_LORA = 64
AAA_LORA = 64
Q_BLOCK = 128
NORM_EPS = 1e-6
GN_EPS = 64e-5

RW_COLS = 3 * D_RWKV + DECAY_LORA + AAA_LORA
FOX_COLS = 3 * D_FOX + H_FOX
GATE_COLS = D_MIX_2
D_IN_PROJ = RW_COLS + FOX_COLS + GATE_COLS


def rmsnorm(x, g, eps=NORM_EPS):
    xf = x.astype(jnp.float32)
    y = xf * lax.rsqrt(jnp.mean(xf * xf, axis=-1, keepdims=True) + eps)
    return (y * g.astype(jnp.float32)).astype(x.dtype)

def rwkv7_branch(p, mu, w_up, w0, a_up, a0, k_k, k_a, r_k, gn_g, gn_b):
    B, S, _ = p.shape
    dt = p.dtype
    prev = jnp.pad(p, ((0, 0), (1, 0), (0, 0)))[:, :-1]
    p = p + (prev - p) * mu
    r = p[..., 0:D_RWKV]
    k = p[..., D_RWKV:2 * D_RWKV]
    v = p[..., 2 * D_RWKV:3 * D_RWKV]
    wl = p[..., 3 * D_RWKV:3 * D_RWKV + DECAY_LORA]
    al = p[..., 3 * D_RWKV + DECAY_LORA:]
    w = w0 + jnp.tanh(wl) @ w_up
    w = (-jax.nn.softplus(-w) - 0.5).astype(jnp.float32)
    decay = jnp.exp(-jnp.exp(w))
    a = jax.nn.sigmoid(a0 + al @ a_up)

    hs = lambda t: t.reshape(B, S, H_RWKV, HEAD_DIM)
    kk = hs(k * k_k).astype(jnp.float32)
    kk = kk / jnp.maximum(jnp.sqrt(jnp.sum(kk * kk, axis=-1, keepdims=True)), 1e-12)
    k = k * (1.0 + (a - 1.0) * k_a)
    r_h, k_h, v_h, a_h, w_h = hs(r), hs(k), hs(v), hs(a), decay.reshape(B, S, H_RWKV, HEAD_DIM)

    to_time = lambda t: jnp.swapaxes(t.astype(jnp.float32), 0, 1)
    xs = (to_time(r_h), to_time(w_h), to_time(k_h), to_time(v_h), to_time(kk), to_time(a_h))

    def step(state, inp):
        rt, wt, kt, vt, kkt, at = inp
        sa = jnp.einsum('bhvk,bhk->bhv', state, -kkt)
        state = (state * wt[:, :, None, :]
                 + sa[..., :, None] * (kkt * at)[..., None, :]
                 + vt[..., :, None] * kt[..., None, :])
        yt = jnp.einsum('bhvk,bhk->bhv', state, rt)
        return state, yt

    s0 = jnp.zeros((B, H_RWKV, HEAD_DIM, HEAD_DIM), jnp.float32)
    _, y = lax.scan(step, s0, xs)
    y = jnp.swapaxes(y, 0, 1)
    mean = jnp.mean(y, axis=-1, keepdims=True)
    var = jnp.mean(jnp.square(y - mean), axis=-1, keepdims=True)
    y = ((y - mean) * lax.rsqrt(var + GN_EPS)).reshape(B, S, D_RWKV)
    y = y * gn_g.astype(jnp.float32) + gn_b.astype(jnp.float32)
    bonus = jnp.sum((r_h * k_h * r_k).astype(jnp.float32), axis=-1, keepdims=True) * v_h.astype(jnp.float32)
    y = y + bonus.reshape(B, S, D_RWKV)
    return y.astype(dt)

def fox_branch(p, b_f, q_g, k_g):
    B, S, _ = p.shape
    dt = p.dtype
    heads = lambda t: t.reshape(B, S, H_FOX, HEAD_DIM).transpose(0, 2, 1, 3)
    q = rmsnorm(heads(p[..., 0:D_FOX]), q_g)
    k = rmsnorm(heads(p[..., D_FOX:2 * D_FOX]), k_g)
    v = heads(p[..., 2 * D_FOX:3 * D_FOX])
    fl = p[..., 3 * D_FOX:]
    log_f = jax.nn.log_sigmoid((fl + b_f).astype(jnp.float32))
    c = jnp.cumsum(log_f, axis=1).transpose(0, 2, 1)
    scale = HEAD_DIM ** -0.5
    nb = S // Q_BLOCK
    q_blk = q.reshape(B, H_FOX, nb, Q_BLOCK, HEAD_DIM).transpose(2, 0, 1, 3, 4)
    c_blk = c.reshape(B, H_FOX, nb, Q_BLOCK).transpose(2, 0, 1, 3)
    pos = jnp.arange(S, dtype=jnp.int32)
    pos_blk = pos.reshape(nb, Q_BLOCK)
    kf = k.astype(jnp.float32)
    vf = v.astype(jnp.float32)

    def attend(args):
        qb, cb, pb = args
        s = jnp.einsum('bhqd,bhkd->bhqk', qb.astype(jnp.float32), kf) * scale
        s = s + cb[..., :, None] - c[:, :, None, :]
        mask = pos[None, :] <= pb[:, None]
        s = jnp.where(mask[None, None], s, -jnp.inf)
        prob = jax.nn.softmax(s, axis=-1)
        return jnp.einsum('bhqk,bhkd->bhqd', prob, vf).astype(dt)

    o = lax.map(attend, (q_blk, c_blk, pos_blk))
    return o.transpose(1, 0, 3, 2, 4).reshape(B, S, D_FOX)

def second_inputs(seed: int = 0) -> dict:
    key = jax.random.key(seed)
    ks = jax.random.split(key, 20)
    f32 = jnp.float32
    n = lambda k, shape, s: (jax.random.normal(k, shape, f32) * s)
    L = DEPTH
    return {
        "x": jax.random.normal(ks[0], (BATCH, SEQ, D_MODEL), f32),
        "norm_g": 1.0 + n(ks[1], (L, D_MODEL), 0.02),
        "w_in": n(ks[2], (L, D_MODEL, D_IN_PROJ), D_MODEL ** -0.5),
        "rw_mu": jax.random.uniform(ks[3], (L, RW_COLS), f32, 0.0, 1.0),
        "rw_w_up": n(ks[4], (L, DECAY_LORA, D_RWKV), 0.5 * DECAY_LORA ** -0.5),
        "rw_w0": jax.random.uniform(ks[5], (L, D_RWKV), f32, -5.0, -0.5),
        "rw_a_up": n(ks[6], (L, AAA_LORA, D_RWKV), 0.5 * AAA_LORA ** -0.5),
        "rw_a0": n(ks[7], (L, D_RWKV), 0.1),
        "rw_k_k": 0.85 + n(ks[8], (L, D_RWKV), 0.05),
        "rw_k_a": 1.0 + n(ks[9], (L, D_RWKV), 0.05),
        "rw_r_k": n(ks[10], (L, H_RWKV, HEAD_DIM), 0.1),
        "rw_gn_g": 1.0 + n(ks[11], (L, D_RWKV), 0.02),
        "rw_gn_b": n(ks[12], (L, D_RWKV), 0.01),
        "fox_q_g": 1.0 + n(ks[13], (L, HEAD_DIM), 0.02),
        "fox_k_g": 1.0 + n(ks[14], (L, HEAD_DIM), 0.02),
        "fox_b_f": 3.0 + n(ks[15], (L, H_FOX), 0.5),
        "w_out": n(ks[16], (L, D_MIX_2, D_MODEL), D_MIX_2 ** -0.5),
        "final_g": 1.0 + n(ks[17], (D_MODEL,), 0.02),
    }

def second_block(x, norm_g, w_in, rw_mu, rw_w_up, rw_w0, rw_a_up, rw_a0, rw_k_k, rw_k_a, rw_r_k,
              rw_gn_g, rw_gn_b, fox_q_g, fox_k_g, fox_b_f, w_out, final_g):
    for l in range(DEPTH):
        h = rmsnorm(x, norm_g[l])
        p = h @ w_in[l]
        p_rw = p[..., :RW_COLS]
        p_fox = p[..., RW_COLS:RW_COLS + FOX_COLS]
        gate = p[..., RW_COLS + FOX_COLS:]
        y_rw = rwkv7_branch(p_rw, rw_mu[l], rw_w_up[l], rw_w0[l], rw_a_up[l], rw_a0[l],
                            rw_k_k[l], rw_k_a[l], rw_r_k[l], rw_gn_g[l], rw_gn_b[l])
        y_fox = fox_branch(p_fox, fox_b_f[l], fox_q_g[l], fox_k_g[l])
        y = jnp.concatenate([y_rw, y_fox], axis=-1) * jax.nn.silu(gate)
        x = x + y @ w_out[l]
    return rmsnorm(x, final_g)


_first_inputs_2 = second_inputs


def second_inputs(seed=0):
    import zlib

    import numpy as np

    out = dict(_first_inputs_2(seed))
    spreads = {}
    factors = {'norm_g': 3.089,
     'rw_w_up': 4.879,
     'rw_a0': 3.382,
     'rw_k_k': 3.781,
     'rw_gn_g': 7.181,
     'rw_gn_b': 8.0,
     'fox_q_g': 8.0,
     'fox_k_g': 8.0,
     'fox_b_f': 3.916,
     'final_g': 2.875}
    for name, (base, spread) in spreads.items():
        noise = np.random.default_rng([zlib.crc32(name.encode()), seed]).standard_normal(out[name].shape)
        drawn = base * np.exp(spread * noise) if base else spread * noise
        out[name] = __import__('jax').numpy.asarray(drawn.astype(out[name].dtype))
    for name, factor in factors.items():
        out[name] = (out[name] * factor).astype(out[name].dtype)
    return out


_narrow_inputs_2 = second_inputs


def second_inputs(seed=0):

    out = dict(_narrow_inputs_2(seed))
    wider = {'rw_k_k': 3.98, 'rw_gn_g': 4.44, 'rw_gn_b': 8.22, 'fox_b_f': 6.97, 'final_g': 3.23}
    for name, times in wider.items():
        mean = out[name].mean()
        out[name] = (mean + times * (out[name] - mean)).astype(out[name].dtype)
    return out


CHUNK = 64
N_BRANCH = 4
BRANCH = D_MODEL // N_BRANCH
D_MIX_3 = N_BRANCH * BRANCH
EPS = 1e-6

CONV_A_WIDTH = 3
CONV_A_GROUPS = 4
GLA_HEADS = 4
GLA_DK = BRANCH // 2
GLA_DV = BRANCH
GLA_GATE_RANK = 16
GLA_TAU = 16.0
POOL_WINDOWS = (2, 4, 8, 16)
POOL_GROUP = BRANCH // len(POOL_WINDOWS)
SSD_HEAD_DIM = 64
SSD_HEADS = BRANCH // SSD_HEAD_DIM
SSD_GROUPS = 2
SSD_STATE = 128
SSD_CONV = 4
SSD_XBC = BRANCH + 2 * SSD_GROUPS * SSD_STATE

PROJ_SPLITS = (BRANCH, BRANCH, BRANCH, BRANCH,
               GLA_DK, GLA_DK, GLA_DV, GLA_GATE_RANK, GLA_DV,
               BRANCH, BRANCH,
               BRANCH, SSD_XBC, SSD_HEADS)
D_PROJ = sum(PROJ_SPLITS)


def _rmsnorm(x, w):
    xf = x.astype(jnp.float32)
    y = xf * lax.rsqrt(jnp.mean(xf * xf, axis=-1, keepdims=True) + EPS)
    return (y * w.astype(jnp.float32)).astype(x.dtype)

def _causal_depthwise_conv(u, w):
    k = w.shape[0]
    return lax.conv_general_dilated(
        u, w[:, None, :].astype(u.dtype), window_strides=(1,), padding=[(k - 1, 0)],
        dimension_numbers=('NWC', 'WIO', 'NWC'), feature_group_count=u.shape[-1])

def _chunk_states(decay, update):
    def step(s, inp):
        a_c, u_c = inp
        s = a_c * s + u_c
        return s, s
    init = jnp.zeros_like(update[:, 0])
    _, states = lax.scan(step, init, (jnp.moveaxis(decay, 1, 0), jnp.moveaxis(update, 1, 0)))
    return jnp.moveaxis(states, 0, 1)

def _conv_mixer(h, bg, cg, z, conv_w):
    y = bg * _causal_depthwise_conv(cg * h, conv_w)
    return y * jax.nn.silu(z)

def _gla_mixer(q, k, v, g_lr, z, gate_w, gate_b, norm_w):
    b, l, _ = q.shape
    nc = l // CHUNK
    dk = GLA_DK // GLA_HEADS
    dv = GLA_DV // GLA_HEADS
    f32 = jnp.float32
    qc = q.astype(f32).reshape(b, nc, CHUNK, GLA_HEADS, dk) * (dk ** -0.5)
    kc = k.astype(f32).reshape(b, nc, CHUNK, GLA_HEADS, dk)
    vc = v.astype(f32).reshape(b, nc, CHUNK, GLA_HEADS, dv)
    log_a = jax.nn.log_sigmoid((g_lr @ gate_w + gate_b).astype(f32)) / GLA_TAU
    log_a = log_a.reshape(b, nc, CHUNK, GLA_HEADS, dk)
    cum = jnp.cumsum(log_a, axis=2)
    total = cum[:, :, -1]
    k_dec = kc * jnp.exp(total[:, :, None] - cum)
    upd = jnp.einsum('bnchk,bnchv->bnhkv', k_dec, vc)
    states = _chunk_states(jnp.exp(total)[..., None], upd)
    o = jnp.einsum('bnchk,bnhkv->bnchv', qc, states)
    o = _rmsnorm(o, norm_w).reshape(b, l, GLA_DV)
    return (o * jax.nn.silu(z.astype(f32))).astype(q.dtype)

def _pool_mixer(u, z, pool_w, pool_scale):
    b, l, _ = u.shape
    f32 = jnp.float32
    uf = u.astype(f32)
    cs = jnp.pad(jnp.cumsum(uf, axis=1), ((0, 0), (1, 0), (0, 0)))
    pos = jnp.arange(l)
    outs = []
    for gi, win in enumerate(POOL_WINDOWS):
        sl = slice(gi * POOL_GROUP, (gi + 1) * POOL_GROUP)
        cg = cs[:, :, sl]
        prev = jnp.pad(cg, ((0, 0), (win - 1, 0), (0, 0)))[:, :l]
        cnt = jnp.minimum(pos + 1, win).astype(f32)[None, :, None]
        outs.append((cg[:, 1:] - prev) / cnt - uf[:, :, sl])
    pooled = jnp.stack(outs, axis=2)
    mixed = jnp.einsum('blgc,gcd->blgd', pooled, pool_w.astype(f32)).reshape(b, l, BRANCH)
    return (pool_scale.astype(f32) * mixed * jax.nn.silu(z.astype(f32))).astype(u.dtype)

def _ssd_mixer(xbc, dt, z, conv_w, conv_b, dt_bias, a_log, d_skip, norm_w):
    b, l, _ = xbc.shape
    nc = l // CHUNK
    hpg = SSD_HEADS // SSD_GROUPS
    f32 = jnp.float32
    xbc = jax.nn.silu(_causal_depthwise_conv(xbc, conv_w) + conv_b).astype(f32)
    xs, bm, cm = jnp.split(xbc, [BRANCH, BRANCH + SSD_GROUPS * SSD_STATE], axis=-1)
    xs = xs.reshape(b, nc, CHUNK, SSD_GROUPS, hpg, SSD_HEAD_DIM)
    bm = bm.reshape(b, nc, CHUNK, SSD_GROUPS, SSD_STATE)
    cm = cm.reshape(b, nc, CHUNK, SSD_GROUPS, SSD_STATE)
    dt = jax.nn.softplus(dt.astype(f32) + dt_bias.astype(f32)).reshape(b, nc, CHUNK, SSD_GROUPS, hpg)
    a = -jnp.exp(a_log.astype(f32)).reshape(SSD_GROUPS, hpg)
    cum = jnp.cumsum(dt * a, axis=2)
    total = cum[:, :, -1]
    w = jnp.exp(total[:, :, None] - cum) * dt
    upd = jnp.einsum('bncgs,bncgh,bncghp->bnghps', bm, w, xs)
    states = _chunk_states(jnp.exp(total)[..., None, None], upd)
    y = jnp.einsum('bncgs,bnghps->bncghp', cm, states)
    y = y + d_skip.astype(f32).reshape(SSD_GROUPS, hpg)[:, :, None] * xs
    y = y.reshape(b, l, BRANCH)
    y = _rmsnorm(y * jax.nn.silu(z.astype(f32)), norm_w)
    return y.astype(z.dtype)

def third_inputs(seed: int = 0) -> dict:
    key = jax.random.key(seed)
    ks = jax.random.split(key, 20)
    f32 = jnp.float32
    nrm = lambda k, shape, s: jax.random.normal(k, shape, f32) * s
    x = jax.random.normal(ks[0], (BATCH, SEQ, D_MODEL), f32)
    norm_w = 1.0 + nrm(ks[1], (DEPTH, D_MODEL), 0.02)
    w_in = nrm(ks[2], (DEPTH, D_MODEL, D_PROJ), D_MODEL ** -0.5)
    conv_a_w = nrm(ks[3], (DEPTH, CONV_A_WIDTH, BRANCH), CONV_A_WIDTH ** -0.5)
    gla_gate_w = nrm(ks[4], (DEPTH, GLA_GATE_RANK, GLA_DK), GLA_GATE_RANK ** -0.5)
    gla_gate_b = nrm(ks[5], (DEPTH, GLA_DK), 0.1)
    gla_norm_w = 1.0 + nrm(ks[6], (DEPTH, GLA_DV // GLA_HEADS), 0.02)
    pool_w = nrm(ks[7], (DEPTH, len(POOL_WINDOWS), POOL_GROUP, POOL_GROUP), POOL_GROUP ** -0.5)
    pool_scale = 1.0 + nrm(ks[8], (DEPTH, BRANCH), 0.1)
    ssd_conv_w = nrm(ks[9], (DEPTH, SSD_CONV, SSD_XBC), SSD_CONV ** -0.5)
    ssd_conv_b = nrm(ks[10], (DEPTH, SSD_XBC), 0.01)
    dt0 = jnp.exp(jax.random.uniform(ks[11], (DEPTH, SSD_HEADS), f32, np.log(1e-3), np.log(1e-1)))
    ssd_dt_bias = dt0 + jnp.log(-jnp.expm1(-dt0))
    ssd_a_log = jnp.log(jax.random.uniform(ks[12], (DEPTH, SSD_HEADS), f32, 1.0, 16.0))
    ssd_d = 1.0 + nrm(ks[13], (DEPTH, SSD_HEADS), 0.1)
    ssd_norm_w = 1.0 + nrm(ks[14], (DEPTH, BRANCH), 0.02)
    w_out = nrm(ks[15], (DEPTH, D_MIX_3, D_MODEL), D_MIX_3 ** -0.5)
    final_norm_w = 1.0 + nrm(ks[16], (D_MODEL,), 0.02)
    return {'x': x, 'norm_w': norm_w, 'w_in': w_in, 'conv_a_w': conv_a_w,
            'gla_gate_w': gla_gate_w, 'gla_gate_b': gla_gate_b, 'gla_norm_w': gla_norm_w,
            'pool_w': pool_w, 'pool_scale': pool_scale,
            'ssd_conv_w': ssd_conv_w, 'ssd_conv_b': ssd_conv_b, 'ssd_dt_bias': ssd_dt_bias,
            'ssd_a_log': ssd_a_log, 'ssd_d': ssd_d, 'ssd_norm_w': ssd_norm_w,
            'w_out': w_out, 'final_norm_w': final_norm_w}

def third_block(x, norm_w, w_in, conv_a_w, gla_gate_w, gla_gate_b, gla_norm_w, pool_w, pool_scale,
              ssd_conv_w, ssd_conv_b, ssd_dt_bias, ssd_a_log, ssd_d, ssd_norm_w, w_out, final_norm_w):
    split_idx = [int(i) for i in np.cumsum(PROJ_SPLITS)[:-1]]
    for layer in range(DEPTH):
        h = _rmsnorm(x, norm_w[layer])
        proj = h @ w_in[layer]
        (a_h, a_b, a_c, a_z, g_q, g_k, g_v, g_lr, g_z, p_u, p_z, s_z, s_xbc, s_dt) = jnp.split(proj, split_idx, axis=-1)
        y_a = _conv_mixer(a_h, a_b, a_c, a_z, conv_a_w[layer])
        y_b = _gla_mixer(g_q, g_k, g_v, g_lr, g_z, gla_gate_w[layer], gla_gate_b[layer], gla_norm_w[layer])
        y_c = _pool_mixer(p_u, p_z, pool_w[layer], pool_scale[layer])
        y_d = _ssd_mixer(s_xbc, s_dt, s_z, ssd_conv_w[layer], ssd_conv_b[layer], ssd_dt_bias[layer],
                         ssd_a_log[layer], ssd_d[layer], ssd_norm_w[layer])
        mix = jnp.concatenate([y_a, y_b, y_c, y_d], axis=-1)
        x = x + mix @ w_out[layer]
    return _rmsnorm(x, final_norm_w)


_first_inputs_3 = third_inputs


def third_inputs(seed=0):
    import zlib

    import numpy as np

    out = dict(_first_inputs_3(seed))
    spreads = {}
    factors = {'norm_w': 2.697,
     'gla_gate_b': 4.209,
     'gla_norm_w': 161.049,
     'pool_scale': 15.28,
     'ssd_conv_b': 63.737,
     'ssd_d': 120.939,
     'ssd_norm_w': 200.0,
     'final_norm_w': 23.41}
    for name, (base, spread) in spreads.items():
        noise = np.random.default_rng([zlib.crc32(name.encode()), seed]).standard_normal(out[name].shape)
        drawn = base * np.exp(spread * noise) if base else spread * noise
        out[name] = __import__('jax').numpy.asarray(drawn.astype(out[name].dtype))
    for name, factor in factors.items():
        out[name] = (out[name] * factor).astype(out[name].dtype)
    return out


_narrow_inputs_3 = third_inputs


def third_inputs(seed=0):

    out = dict(_narrow_inputs_3(seed))
    wider = {'gla_norm_w': 3.58, 'pool_scale': 3.59, 'ssd_norm_w': 6.0, 'final_norm_w': 3.21}
    for name, times in wider.items():
        mean = out[name].mean()
        out[name] = (mean + times * (out[name] - mean)).astype(out[name].dtype)
    return out


def setup_inputs(seed=0):
    out = dict(first_inputs(seed))
    for name, value in second_inputs(seed + 1).items():
        if name != "x":
            out[name + "_2"] = value
    for name, value in third_inputs(seed + 2).items():
        if name != "x":
            out[name + "_3"] = value
    return out


def reference(
    x, w_in, lb_logits, hg_norm_w, sinks, w_out, ln_g, ln_b, norm_g_2, w_in_2, rw_mu_2,
    rw_w_up_2, rw_w0_2, rw_a_up_2, rw_a0_2, rw_k_k_2, rw_k_a_2, rw_r_k_2, rw_gn_g_2, rw_gn_b_2,
    fox_q_g_2, fox_k_g_2, fox_b_f_2, w_out_2, final_g_2, norm_w_3, w_in_3, conv_a_w_3,
    gla_gate_w_3, gla_gate_b_3, gla_norm_w_3, pool_w_3, pool_scale_3, ssd_conv_w_3,
    ssd_conv_b_3, ssd_dt_bias_3, ssd_a_log_3, ssd_d_3, ssd_norm_w_3, w_out_3, final_norm_w_3,
):
    x = first_block(
        x, w_in, lb_logits, hg_norm_w, sinks, w_out, ln_g, ln_b,
    )
    x = second_block(
        x, norm_g_2, w_in_2, rw_mu_2, rw_w_up_2, rw_w0_2, rw_a_up_2, rw_a0_2, rw_k_k_2,
        rw_k_a_2, rw_r_k_2, rw_gn_g_2, rw_gn_b_2, fox_q_g_2, fox_k_g_2, fox_b_f_2, w_out_2,
        final_g_2,
    )
    return third_block(
        x, norm_w_3, w_in_3, conv_a_w_3, gla_gate_w_3, gla_gate_b_3, gla_norm_w_3, pool_w_3,
        pool_scale_3, ssd_conv_w_3, ssd_conv_b_3, ssd_dt_bias_3, ssd_a_log_3, ssd_d_3,
        ssd_norm_w_3, w_out_3, final_norm_w_3,
    )


_drawn_inputs = setup_inputs


def setup_inputs(seed=0):
    import zlib

    import numpy as np

    out = dict(_drawn_inputs(seed))
    spreads = {}
    factors = {}
    for name, (base, spread) in spreads.items():
        noise = np.random.default_rng([zlib.crc32(name.encode()), seed]).standard_normal(out[name].shape)
        drawn = base * np.exp(spread * noise) if base else spread * noise
        out[name] = __import__('jax').numpy.asarray(drawn.astype(out[name].dtype))
    for name, factor in factors.items():
        out[name] = (out[name] * factor).astype(out[name].dtype)
    return out
```

```python
import math
from contextlib import ExitStack

import concourse.bass as bass
import numpy as np
from concourse import mybir

F32 = mybir.dt.float32
BF16 = mybir.dt.bfloat16
ALU = mybir.AluOpType
ACT = mybir.ActivationFunctionType
AX = mybir.AxisListType.X

P = 128
D = 1024
KC = D // P
SEQ = 2048
TILES = SEQ // P
BANK = 512
NEG = -1.0e30


def need(eng, sem, n):
    if isinstance(n, int) and n <= 0:
        return
    eng.wait_ge(sem, n)


def pipeline(eng, step):
    step(0, 0, 0, None, None, None)
    step(1, 0, 1, 0, 0, 0)
    step(2, 1, 0, 1, 0, 1)
    with eng.Fori(1, TILES // 2 - 1) as j:
        step(2 * j + 1, j, 1, 2 * j, j, 0)
        step(2 * j + 2, j + 1, 0, 2 * j + 1, j, 1)
    step(TILES - 1, TILES // 2 - 1, 1, TILES - 2, TILES // 2 - 1, 0)
    step(None, None, None, TILES - 1, TILES // 2 - 1, 1)


class Stage:

    def __init__(self, nc, ctx, name):
        self.nc, self.ctx, self.name, self.sems = nc, ctx, name, []

    def sb(self, name, shape, dt=F32):
        return self.ctx.enter_context(self.nc.sbuf_tensor(f"{self.name}_{name}", shape, dt))

    def bank(self, name):
        return self.ctx.enter_context(self.nc.psum_tensor(f"{self.name}_{name}", [P, BANK], F32))

    def sem(self, name):
        self.sems.append(self.ctx.enter_context(self.nc.semaphore(f"{self.name}_{name}")))
        return self.sems[-1]

    def block(self):
        self.ctx.callback(self.clear)
        return self.ctx.enter_context(self.nc.Block())

    def clear(self):
        with self.nc.Block() as block:
            @block.sync
            def _(sp):
                for one in self.sems:
                    sp.sem_clear(one)


def heads(ap, n):
    return ap.rearrange("p (h d) -> p h d", h=n)


def spread(ap, d):
    return ap.unsqueeze(2).to_broadcast([ap.shape[0], ap.shape[1], d])


def again(ap, n):
    return ap.unsqueeze(1).to_broadcast([ap.shape[0], n, ap.shape[1]])


def row(ap, a, b):
    return ap[0:1, a:b].to_broadcast([P, b - a])


class Normed:

    def __init__(self, s, x, ident, banks, eps=1e-6):
        self.x, self.ident, self.banks, self.eps = x, ident, banks, eps
        self.xt, self.xn, self.hT = s.sb("xt", [P, D]), s.sb("xn", [P, D]), s.sb("hT", [P, KC, P])
        self.total, self.ms, self.rms, self.power = (s.sb(n, [P, 1]) for n in ("x_total", "x_ms", "x_rms", "x_power"))
        self.x_here, self.squared, self.ms_ready, self.rms_ready = (s.sem(n) for n in ("x_here", "x_squared", "x_ms_ready", "x_rms_ready"))
        self.normed, self.turned, self.ready = s.sem("x_normed"), s.sem("x_turned"), s.sem("hT_ready")

    def load(self, sp, n):
        need(sp, self.normed, n)
        sp.dma_start(self.xt[:], self.x[bass.ds(n * P, P), :]).then_inc(self.x_here, 16)

    def square(self, act, n):
        act.wait_ge(self.x_here, 16 * (n + 1))
        need(act, self.turned, 2 * n)
        act.activation(self.xn[:], self.xt[:], ACT.Square, accum_out=self.total[:]).then_inc(self.squared, 1)

    def mean(self, dve, n):
        dve.wait_ge(self.squared, n + 1)
        dve.tensor_scalar(self.ms[:], self.total[:], 1.0 / D, self.eps, ALU.mult, ALU.add).then_inc(self.ms_ready, 1)

    def root(self, pool, n):
        pool.wait_ge(self.ms_ready, n + 1)
        pool.tensor_tensor(self.rms[:], self.ms[:], self.power[:], ALU.pow).then_inc(self.rms_ready, 1)

    def scale(self, dve, n):
        dve.wait_ge(self.rms_ready, n + 1)
        dve.tensor_scalar(self.xn[:], self.xt[:], self.rms[:], None, ALU.mult).then_inc(self.normed, 1)

    def turn(self, pe, i, freed):
        pe.wait_ge(self.normed, i + 1)
        for g in range(2):
            need(pe, freed[g], i)
            for c in range(4):
                last = pe.transpose(self.banks[g][:, c * P:(c + 1) * P], self.xn[:, (4 * g + c) * P:(4 * g + c + 1) * P], self.ident[:])
            last.then_inc(self.turned, 1)

    def take(self, act, i):
        for g in range(2):
            act.wait_ge(self.turned, 2 * i + g + 1)
            act.copy(self.hT[:, 4 * g:4 * g + 4, :], heads(self.banks[g][:], 4)).then_inc(self.ready, 1)


def by_chunk(g):
    return g.rearrange("a (k p) -> (a k) p", p=P)


def rows_of(eng, t):
    return bass.ds(t * P if isinstance(t, int) else eng.snap(t * P), P)


HG = 512
HG_HEADS = 4
CHUNK = 64


def hgrn(nc, x, w_in, lb_logits, hg_norm_w, masks, mixed):
    with ExitStack() as ctx:
        s = Stage(nc, ctx, "hg")
        sb, sem = s.sb, s.sem
        w = sb("w", [P, KC, 4 * HG])
        ident = sb("ident", [P, P])
        upto = sb("upto", [P, P])
        after = sb("after", [P, P])
        halves = sb("halves", [P, 2])
        logits = sb("logits", [P, 2, HG])
        span = sb("span", [P, HG])
        centre = sb("centre", [P, HG])
        half_norm = sb("half_norm", [P, HG])
        power = sb("power", [P, HG_HEADS])
        xt = [sb(f"xt{p}", [P, D]) for p in range(2)]
        hT = sb("hT", [P, KC, P])
        tanh = sb("tanh", [P, HG])
        q2 = [sb(f"q2{p}", [P, HG]) for p in range(2)]
        tanh_f = [sb(f"tanh_f{p}", [P, HG]) for p in range(2)]
        v = [sb(f"v{p}", [P, HG]) for p in range(2)]
        gate2 = [sb(f"gate2{p}", [P, HG]) for p in range(2)]
        part = sb("part", [P, HG])
        f = sb("f", [P, HG])
        k = sb("k", [P, HG])
        logf = sb("logf", [P, HG])
        e_cum = sb("e_cum", [P, HG])
        e_neg = sb("e_neg", [P, HG])
        e_rest = sb("e_rest", [P, HG])
        decay = sb("decay", [P, HG_HEADS, 2])
        qd = sb("qd", [P, HG])
        kd = sb("kd", [P, HG])
        ks = sb("ks", [P, HG])
        qdT = sb("qdT", [P, HG_HEADS, P])
        kdT = sb("kdT", [P, HG_HEADS, P])
        A = sb("A", [P, HG_HEADS, P])
        S = [sb(f"S{c}", [P, HG_HEADS, P]) for c in range(2)]
        o = sb("o", [P, HG])
        sq = sb("sq", [P, HG])
        ms = sb("ms", [P, HG_HEADS])
        rstd = sb("rstd", [P, HG_HEADS])
        mix = [sb(f"mix{p}", [P, HG]) for p in range(2)]
        pj = [s.bank(f"pj{b}") for b in range(2)]
        cum_a = s.bank("cum_a")
        rest_o = s.bank("rest_o")
        tot_i0 = s.bank("tot_i0")
        inc1 = s.bank("inc1")
        tq = s.bank("tq")
        tk = s.bank("tk")

        consts_in, w_in_here = sem("consts_in"), sem("w_here")
        x_here = [sem(f"x_here{p}") for p in range(2)]
        stored = [sem(f"stored{p}") for p in range(2)]
        set_up, set_up_act, set_up_pool = sem("set_up"), sem("set_up_act"), sem("set_up_pool")
        x_turned, hT_ready = sem("x_turned"), sem("hT_ready")
        chunk_ready, tanh_ready = sem("chunk_ready"), sem("tanh_ready")
        taken = [sem(f"taken{c}") for c in range(4)]
        f_ready, logf_ready, cum_ready, exp_ready = sem("f_ready"), sem("logf_ready"), sem("cum_ready"), sem("exp_ready")
        dec_ready, ks_ready, turned_ready = sem("dec_ready"), sem("ks_ready"), sem("turned_ready")
        qdT_ready, kdT_ready, A_done, A_ready = sem("qdT_ready"), sem("kdT_ready"), sem("A_done"), sem("A_ready")
        inc_ready, S_mid, S_end, o_done, o_ready = sem("inc_ready"), sem("S_mid"), sem("S_end"), sem("o_done"), sem("o_ready")
        ms_ready, rstd_ready, mix_ready = sem("ms_ready"), sem("rstd_ready"), sem("mix_ready")

        block = s.block()

        @block.sync
        def _(sp):
            for dst, src in ((ident[:], masks["ident"]), (upto[:], masks["chunk_upto"]), (after[:], masks["chunk_after"]),
                             (halves[:], masks["halves"]), (logits[:, 0, :], row(lb_logits, 0, HG)),
                             (logits[:, 1, :], lb_logits[1:2, :].to_broadcast([P, HG])),
                             (half_norm[:], row(hg_norm_w, 0, HG))):
                sp.dma_start(dst, src).then_inc(consts_in, 16)
            for kc in range(KC):
                sp.dma_start(w[:, kc, :], w_in[kc * P:(kc + 1) * P, 0:4 * HG]).then_inc(w_in_here, 16)

            def step(i, hi, pi, t, ht, pt):
                if i is not None:
                    need(sp, x_turned, 2 * i - 2)
                    sp.dma_start(xt[pi][:], x[bass.ds(i * P, P), :]).then_inc(x_here[pi], 16)
                if t is not None:
                    sp.wait_ge(mix_ready, t + 1)
                    sp.dma_start(mixed[bass.ds(t * P, P), 0:HG], mix[pt][:]).then_inc(stored[pt], 16)

            pipeline(sp, step)
            for p in range(2):
                sp.wait_ge(stored[p], 16 * TILES // 2)

        @block.tensor
        def _(pe):
            pe.wait_ge(consts_in, 16 * 7)
            pe.wait_ge(w_in_here, 16 * KC)
            pe.wait_ge(set_up, 1)

            def turn_x(i, hi, pi):
                pe.wait_ge(x_here[pi], 16 * (hi + 1))
                for g in range(2):
                    need(pe, taken[2 + g], i)
                    for c in range(4):
                        last = pe.transpose(pj[g][:, c * P:(c + 1) * P], xt[pi][:, (4 * g + c) * P:(4 * g + c + 1) * P], ident[:])
                    last.then_inc(x_turned, 1)

            def project(i, c):
                if c == 0:
                    pe.wait_ge(hT_ready, 2 * i + 2)
                if c >= 2:
                    pe.wait_ge(taken[c - 2], i + 1)
                for kc in range(KC):
                    last = pe.matmul(pj[c % 2][:], hT[:, kc, :], w[:, kc, c * HG:(c + 1) * HG], start=kc == 0, stop=kc == KC - 1)
                last.then_inc(chunk_ready, 1)

            def cumulate(t):
                pe.wait_ge(logf_ready, t + 1)
                need(pe, o_ready, t)
                pe.matmul(cum_a[:], upto[:], logf[:], start=True, stop=True)
                pe.matmul(rest_o[:], after[:], logf[:], start=True, stop=True)
                need(pe, S_end, t)
                for h in range(HG_HEADS):
                    last = pe.matmul(tot_i0[:, 2 * h:2 * h + 2], logf[:, h * P:(h + 1) * P], halves[:], start=True, stop=True)
                last.then_inc(cum_ready, 1)

            def turn_qk(t):
                pe.wait_ge(dec_ready, t + 1)
                for h in range(HG_HEADS):
                    pe.transpose(tq[:, h * P:(h + 1) * P], qd[:, h * P:(h + 1) * P], ident[:])
                for h in range(HG_HEADS):
                    last = pe.transpose(tk[:, h * P:(h + 1) * P], kd[:, h * P:(h + 1) * P], ident[:])
                last.then_inc(turned_ready, 1)

            def attend(t):
                pe.wait_ge(qdT_ready, t + 1)
                pe.wait_ge(kdT_ready, t + 1)
                for h in range(HG_HEADS):
                    last = pe.matmul(cum_a[:, h * P:(h + 1) * P], kdT[:, h, :], qdT[:, h, :], start=True, stop=True)
                last.then_inc(A_done, 1)

            def increments(t, pt):
                pe.wait_ge(ks_ready, t + 1)
                for c, bank in ((0, tot_i0), (1, inc1)):
                    lo = c * CHUNK
                    for h in range(HG_HEADS):
                        last = pe.matmul(bank[:, h * P:(h + 1) * P], ks[lo:lo + CHUNK, h * P:(h + 1) * P],
                                         v[pt][lo:lo + CHUNK, h * P:(h + 1) * P], start=True, stop=True)
                    last.then_inc(inc_ready, 1)

            def outputs(t, pt):
                pe.wait_ge(A_ready, t + 1)
                need(pe, S_end, t)
                pe.wait_ge(S_mid, t + 1)
                for h in range(HG_HEADS):
                    cols = slice(h * P, (h + 1) * P)
                    for c in range(2):
                        lo = c * CHUNK
                        pe.matmul(rest_o[lo:lo + CHUNK, cols], qdT[:, h, lo:lo + CHUNK], S[c][:, h, :], start=True, stop=False)
                    last = pe.matmul(rest_o[:, cols], A[:, h, :], v[pt][:, cols], start=False, stop=True)
                last.then_inc(o_done, 1)

            def step(i, hi, pi, t, ht, pt):
                if t is not None:
                    cumulate(t)
                if i is not None:
                    turn_x(i, hi, pi)
                    project(i, 0)
                if t is not None:
                    turn_qk(t)
                if i is not None:
                    project(i, 1)
                if t is not None:
                    attend(t)
                    increments(t, pt)
                if i is not None:
                    project(i, 2)
                if t is not None:
                    outputs(t, pt)
                if i is not None:
                    project(i, 3)

            pipeline(pe, step)

        @block.scalar
        def _(act):
            act.wait_ge(set_up_pool, 1)
            act.activation(span[:], part[:], ACT.Tanh, scale=0.5).then_inc(set_up_act, 1)

            def take_x(i):
                for g in range(2):
                    act.wait_ge(x_turned, 2 * i + g + 1)
                    act.copy(hT[:, 4 * g:4 * g + 4, :], heads(pj[g][:], 4)).then_inc(hT_ready, 1)

            def take(i, pi, c):
                act.wait_ge(chunk_ready, 4 * i + c + 1)
                if c in (0, 3):
                    if c == 0:
                        need(act, taken[3], i)
                    else:
                        act.wait_ge(taken[0], i + 1)
                    act.activation(tanh[:], pj[c % 2][:], ACT.Tanh, scale=0.5).then_inc(tanh_ready, 1)
                elif c == 1:
                    act.activation(tanh_f[pi][:], pj[1][:], ACT.Tanh, scale=0.5).then_inc(taken[1], 1)
                else:
                    act.copy(v[pi][:], pj[0][:]).then_inc(taken[2], 1)

            def step(i, hi, pi, t, ht, pt):
                if t is not None:
                    act.wait_ge(f_ready, t + 1)
                    act.activation(logf[:], f[:], ACT.Ln).then_inc(logf_ready, 1)
                    act.wait_ge(cum_ready, t + 1)
                    act.activation(e_cum[:], cum_a[:], ACT.Exp)
                    act.activation(e_neg[:], cum_a[:], ACT.Exp, scale=-1.0)
                    act.activation(e_rest[:], rest_o[:], ACT.Exp)
                    act.activation(decay[:].rearrange("p h c -> p (h c)"), tot_i0[:, 0:8], ACT.Exp).then_inc(exp_ready, 1)
                if i is not None:
                    take_x(i)
                    take(i, pi, 0)
                if t is not None:
                    act.wait_ge(turned_ready, t + 1)
                    act.copy(qdT[:], heads(tq[:], 4)).then_inc(qdT_ready, 1)
                if i is not None:
                    take(i, pi, 1)
                    take(i, pi, 2)
                if t is not None:
                    act.wait_ge(o_done, t + 1)
                    act.copy(o[:], rest_o[:]).then_inc(o_ready, 1)
                if i is not None:
                    take(i, pi, 3)

            pipeline(act, step)

        @block.gpsimd
        def _(pool):
            pool.memset(power[:], -0.5)
            pool.memset(S[0][:], 0.0)
            pool.wait_ge(consts_in, 16 * 7)
            pool.tensor_tensor(part[:], logits[:, 0, :], logits[:, 1, :], ALU.subtract).then_inc(set_up_pool, 1)
            pool.drain()

            def step(i, hi, pi, t, ht, pt):
                if t is not None:
                    pool.wait_ge(ms_ready, t + 1)
                    pool.tensor_tensor(rstd[:], ms[:], power[:], ALU.pow).then_inc(rstd_ready, 1)

            pipeline(pool, step)

        @block.vector
        def _(dve):
            dve.wait_ge(consts_in, 16 * 7)
            dve.wait_ge(set_up_act, 1)
            dve.tensor_scalar(centre[:], span[:], 0.25, 0.75, ALU.mult, ALU.add)
            dve.tensor_scalar(half_norm[:], half_norm[:], 0.5, None, ALU.mult)
            dve.drain()
            dve.tensor_scalar(span[:], span[:], -0.25, 0.25, ALU.mult, ALU.add).then_inc(set_up, 1)
            dve.drain()

            def gated(i, c, dst):
                dve.wait_ge(tanh_ready, 2 * i + (1 if c == 0 else 2))
                dve.scalar_tensor_tensor(dst[:], tanh[:], 1.0, pj[c % 2][:], ALU.add, ALU.mult).then_inc(taken[c], 1)

            def update(t, c):
                dve.wait_ge(inc_ready, 2 * t + c + 1)
                bank = (tot_i0, inc1)[c]
                for h in range(HG_HEADS):
                    last = dve.scalar_tensor_tensor(S[1 - c][:, h, :], S[c][:, h, :], decay[:, h, c:c + 1], bank[:, h * P:(h + 1) * P],
                                                    ALU.mult, ALU.add)
                last.then_inc((S_mid, S_end)[c], 1)

            def step(i, hi, pi, t, ht, pt):
                if t is not None:
                    dve.wait_ge(taken[1], t + 1)
                    dve.tensor_tensor(part[:], span[:], tanh_f[pt][:], ALU.mult)
                    dve.drain()
                    dve.tensor_tensor(f[:], part[:], centre[:], ALU.add).then_inc(f_ready, 1)
                    dve.tensor_tensor(k[:], span[:], part[:], ALU.subtract)
                if t is not None:
                    dve.drain()
                    dve.wait_ge(exp_ready, t + 1)
                    dve.scalar_tensor_tensor(qd[:], q2[pt][:], 0.5, e_cum[:], ALU.mult, ALU.mult)
                    dve.tensor_tensor(kd[:], k[:], e_neg[:], ALU.mult).then_inc(dec_ready, 1)
                    dve.tensor_tensor(ks[:], k[:], e_rest[:], ALU.mult).then_inc(ks_ready, 1)
                if i is not None:
                    gated(i, 0, q2[pi])
                if t is not None:
                    dve.wait_ge(turned_ready, t + 1)
                    dve.tensor_copy(kdT[:], heads(tk[:], 4)).then_inc(kdT_ready, 1)
                    dve.wait_ge(A_done, t + 1)
                    dve.tensor_tensor(A[:], heads(cum_a[:], 4), again(upto[:], 4), ALU.mult).then_inc(A_ready, 1)
                    update(t, 0)
                    dve.wait_ge(o_done, t + 1)
                    update(t, 1)
                    dve.wait_ge(o_ready, t + 1)
                    dve.tensor_tensor(sq[:], o[:], o[:], ALU.mult)
                    dve.drain()
                    dve.tensor_reduce(ms[:], heads(sq[:], HG_HEADS), AX, ALU.add)
                    dve.drain()
                    dve.tensor_scalar(ms[:], ms[:], 1.0 / P, 1e-6, ALU.mult, ALU.add).then_inc(ms_ready, 1)
                    need(dve, stored[pt], 16 * ht)
                    dve.tensor_tensor(mix[pt][:], half_norm[:], gate2[pt][:], ALU.mult)
                    dve.wait_ge(rstd_ready, t + 1)
                    dve.tensor_tensor(heads(o[:], 4), heads(o[:], 4), spread(rstd[:], P), ALU.mult)
                    dve.drain()
                    dve.tensor_tensor(mix[pt][:], mix[pt][:], o[:], ALU.mult).then_inc(mix_ready, 1)
                if i is not None:
                    gated(i, 3, gate2[pi])

            pipeline(dve, step)


SW = 512
SW_HEADS = 8
SW_DIM = 64
SW_KV = 128
QKV = SW + 2 * SW_KV
ROPE = 8
FIRST_COL = 4 * HG
ALPHA = 2.0 ** 0.25


def window_attention(nc, x, w_in, w_out, sinks, ln_g, ln_b, rope, masks, mixed, x_out):
    with ExitStack() as ctx:
        s = Stage(nc, ctx, "sw")
        sb, sem = s.sb, s.sem
        w = sb("w", [P, KC, QKV + SW])
        wo = sb("wo", [P, KC, D])
        ident = sb("ident", [P, P])
        band = [sb(f"band{p}", [P, 2 * P]) for p in range(2)]
        before = sb("before", [P, P])
        sink = sb("sink", [P, SW_HEADS])
        gain, shift = sb("gain", [P, D]), sb("shift", [P, D])
        power = sb("power", [P, 1])
        xt = [sb(f"xt{p}", [P, D]) for p in range(2)]
        xres = [sb(f"xres{p}", [P, D]) for p in range(2)]
        hgm = [sb(f"hgm{p}", [P, HG]) for p in range(2)]
        cs = [sb(f"cs{p}", [P, 2 * ROPE]) for p in range(2)]
        hT = sb("hT", [P, KC, P])
        qkv = [sb(f"qkv{p}", [P, QKV]) for p in range(2)]
        gate2 = [sb(f"gate2{p}", [P, SW]) for p in range(2)]
        tanh = sb("tanh", [P, SW])
        rot = [sb(f"rot{n}", [P, 10, ROPE]) for n in range(4)]
        vr = sb("vr", [P, 2, SW_KV])
        qT = sb("qT", [P, 4, P])
        kT = sb("kT", [P, 2, P])
        sm = sb("sm", [P, SW_HEADS, 2 * P])
        top, negtop, sinkd, expsink, total, rden = (sb(n, [P, SW_HEADS]) for n in ("top", "negtop", "sinkd", "expsink", "total", "rden"))
        pT = sb("pT", [P, 2 * SW_HEADS, P])
        oa = sb("oa", [P, SW])
        mixa = sb("mixa", [P, SW])
        mixT = sb("mixT", [P, KC, P])
        z = sb("z", [P, D])
        stats = sb("stats", [P, 2, 6])
        moments = sb("moments", [P, 2])
        rstd = sb("rstd", [P, 1])
        y = [sb(f"y{p}", [P, D]) for p in range(2)]
        pj = [s.bank(f"pj{b}") for b in range(2)]
        sc = [s.bank(f"sc{b}") for b in range(2)]
        tp = [s.bank(f"tp{b}") for b in range(2)]
        ov = s.bank("ov")
        th = s.bank("th")

        consts_in, w_here, set_up, set_up_pool = sem("consts_in"), sem("w_here"), sem("set_up"), sem("set_up_pool")
        x_here, t_here, stored = ([sem(f"{n}{p}") for p in range(2)] for n in ("x_here", "t_here", "stored"))
        x_turned, hT_ready, chunk_ready, tanh_ready = sem("x_turned"), sem("hT_ready"), sem("chunk_ready"), sem("tanh_ready")
        taken = [sem(f"taken{c}") for c in range(3)]
        roped, v_kept, qk_turned, qT_ready, kT_ready = sem("roped"), sem("v_kept"), sem("qk_turned"), sem("qT_ready"), sem("kT_ready")
        scored, masked, top_ready, p_ready, den_ready = sem("scored"), sem("masked"), sem("top_ready"), sem("p_ready"), sem("den_ready")
        p_turned, pT_act, pT_dve, weighed, mixa_ready = sem("p_turned"), sem("pT_act"), sem("pT_dve"), sem("weighed"), sem("mixa_ready")
        hg_turned, hgT_ready, a_turned, aT_ready = sem("hg_turned"), sem("hgT_ready"), sem("a_turned"), sem("aT_ready")
        out_done, z_ready, var_ready, rstd_ready, y_ready = sem("out_done"), sem("z_ready"), sem("var_ready"), sem("rstd_ready"), sem("y_ready")

        block = s.block()
        CONSTS = 7
        by_pair = lambda ap: ap.rearrange("p (j g) -> p j g", g=2)
        sink_by_pair = sink[:].rearrange("p (g j) -> p j g", g=2)

        @block.sync
        def _(sp):
            for dst, src in ((ident[:], masks["ident"]), (band[0][:], masks["band_first"]), (band[1][:], masks["band_odd"]),
                             (before[:], masks["band_odd"][:, 0:P]), (gain[:], row(ln_g, 0, D)), (shift[:], row(ln_b, 0, D)),
                             (sink[:], row(sinks, 0, SW_HEADS))):
                sp.dma_start(dst, src).then_inc(consts_in, 16)
            for kc in range(KC):
                sp.dma_start(w[:, kc, :], w_in[kc * P:(kc + 1) * P, FIRST_COL:FIRST_COL + QKV + SW]).then_inc(w_here, 16)
            for kc in range(KC):
                sp.dma_start(wo[:, kc, :], w_out[kc * P:(kc + 1) * P, :]).then_inc(w_here, 16)

            sp.dma_start(xt[0][:], x[0:P, :]).then_inc(x_here[0], 16)

            def step(i, hi, pi, t, ht, pt):
                if i is not None:
                    need(sp, z_ready, 2 * i - 2)
                    sp.dma_start(xres[pi][:], x[bass.ds(i * P, P), :]).then_inc(t_here[pi], 16)
                    sp.dma_start(hgm[pi][:], mixed[bass.ds(i * P, P), 0:HG]).then_inc(t_here[pi], 16)
                    sp.dma_start(cs[pi][:], rope[bass.ds(i * P, P), :]).then_inc(t_here[pi], 16)
                    if not (isinstance(i, int) and i == TILES - 1):
                        need(sp, x_turned, 2 * i)
                        sp.dma_start(xt[1 - pi][:], x[bass.ds((i + 1) * P, P), :]).then_inc(x_here[1 - pi], 16)
                if t is not None:
                    sp.wait_ge(y_ready, t + 1)
                    sp.dma_start(x_out[bass.ds(t * P, P), :], y[pt][:]).then_inc(stored[pt], 16)

            pipeline(sp, step)
            for p in range(2):
                sp.wait_ge(stored[p], 16 * TILES // 2)

        @block.tensor
        def _(pe):
            pe.wait_ge(consts_in, 16 * CONSTS)
            pe.wait_ge(w_here, 16 * 2 * KC)
            pe.wait_ge(set_up_pool, 1)

            def turn_x(i, hi, pi):
                pe.wait_ge(x_here[pi], 16 * (hi + 1))
                for g in range(2):
                    need(pe, taken[(2, 1)[g]], i)
                    for c in range(4):
                        last = pe.transpose(pj[g][:, c * P:(c + 1) * P], xt[pi][:, (4 * g + c) * P:(4 * g + c + 1) * P], ident[:])
                    last.then_inc(x_turned, 1)

            def project(i, c, lo, hi):
                if c == 0:
                    pe.wait_ge(hT_ready, 2 * i + 2)
                if c == 2 and lo == 0:
                    pe.wait_ge(taken[0], i + 1)
                a = c * SW if c < 2 else QKV
                for kc in range(KC):
                    last = pe.matmul(pj[c % 2][:, lo:hi], hT[:, kc, :], w[:, kc, a + lo:a + hi], start=kc == 0, stop=kc == KC - 1)
                return last

            def turn_qk(t, pt):
                pe.wait_ge(roped, t + 1)
                need(pe, aT_ready, t)
                for j in range(4):
                    pe.transpose(tp[0][:, j * P:(j + 1) * P], qkv[pt][:, j * P:(j + 1) * P], ident[:])
                pe.transpose(tp[1][:, 0:P], qkv[pt][:, SW:SW + SW_KV], ident[:]).then_inc(qk_turned, 1)

            def turn_hg(t, ht, pt):
                pe.wait_ge(t_here[pt], 16 * 3 * (ht + 1))
                for c in range(4):
                    last = pe.transpose(th[:, c * P:(c + 1) * P], hgm[pt][:, c * P:(c + 1) * P], ident[:])
                last.then_inc(hg_turned, 1)

            def score(t, r):
                if r == 0:
                    pe.wait_ge(qT_ready, t + 1)
                    pe.wait_ge(kT_ready, t + 1)
                    need(pe, z_ready, 2 * t)
                else:
                    pe.wait_ge(masked, 4 * t + 2)
                for j in range(2):
                    for g in range(2):
                        part = slice(g * SW_DIM, (g + 1) * SW_DIM)
                        last = pe.matmul(sc[g][:, j * 2 * P:(j + 1) * 2 * P], qT[part, 2 * r + j, :], kT[part, :, :], start=True, stop=True)
                last.then_inc(scored, 1)

            def project_out(t, half):
                if half == 0:
                    pe.wait_ge(hgT_ready, t + 1)
                    pe.wait_ge(masked, 4 * t + 4)
                else:
                    pe.wait_ge(aT_ready, t + 1)
                for c in range(2):
                    for kc in range(4 * half, 4 * half + 4):
                        last = pe.matmul(sc[c][:], mixT[:, kc, :], wo[:, kc, c * BANK:(c + 1) * BANK], start=kc == 0, stop=kc == KC - 1)
                    if half == 1:
                        last.then_inc(out_done, 1)

            def turn_p(t, rounds):
                if 0 in rounds:
                    pe.wait_ge(p_ready, t + 1)
                for n in rounds:
                    if n >= 2:
                        pe.wait_ge((pT_act, pT_dve)[n % 2], 2 * t + 1)
                    for m in range(4):
                        k = 4 * n + m
                        last = pe.transpose(tp[n % 2][:, m * P:(m + 1) * P], sm[:, k // 2, (k % 2) * P:(k % 2 + 1) * P], ident[:])
                    last.then_inc(p_turned, 1)

            def weigh(t):
                pe.wait_ge(pT_act, 2 * t + 2)
                pe.wait_ge(pT_dve, 2 * t + 2)
                pe.wait_ge(v_kept, t + 1)
                need(pe, mixa_ready, t)
                for j in range(4):
                    for g in range(2):
                        h = 4 * g + j
                        for slot in range(2):
                            last = pe.matmul(ov[:, h * SW_DIM:(h + 1) * SW_DIM], pT[:, 2 * (2 * j + g) + slot, :],
                                             vr[:, slot, g * SW_DIM:(g + 1) * SW_DIM], start=slot == 0, stop=slot == 1)
                last.then_inc(weighed, 1)

            def turn_a(t):
                pe.wait_ge(mixa_ready, t + 1)
                for c in range(4):
                    last = pe.transpose(tp[1][:, c * P:(c + 1) * P], mixa[:, c * P:(c + 1) * P], ident[:])
                last.then_inc(a_turned, 1)

            def step(i, hi, pi, t, ht, pt):
                p, m = i is not None, t is not None
                if m:
                    turn_qk(t, pt)
                if p:
                    turn_x(i, hi, pi)
                    project(i, 0, 0, SW).then_inc(chunk_ready, 1)
                if m:
                    score(t, 0)
                    turn_hg(t, ht, pt)
                if p:
                    project(i, 1, 0, 2 * SW_KV).then_inc(chunk_ready, 1)
                if m:
                    score(t, 1)
                    project_out(t, 0)
                if p:
                    project(i, 2, 0, P)
                if m:
                    turn_p(t, (0, 1))
                if p:
                    project(i, 2, P, 2 * P)
                if m:
                    turn_p(t, (2, 3))
                if p:
                    project(i, 2, 2 * P, 3 * P)
                if m:
                    weigh(t)
                if p:
                    project(i, 2, 3 * P, 4 * P).then_inc(chunk_ready, 1)
                if m:
                    turn_a(t)
                    project_out(t, 1)

            pipeline(pe, step)

        @block.scalar
        def _(act):
            def step(i, hi, pi, t, ht, pt):
                p, m = i is not None, t is not None
                if m:
                    act.wait_ge(qk_turned, t + 1)
                    act.copy(qT[:], heads(tp[0][:], 4)).then_inc(qT_ready, 1)
                if p:
                    for g in range(2):
                        act.wait_ge(x_turned, 2 * i + g + 1)
                        act.copy(hT[:, 4 * g:4 * g + 4, :], heads(pj[g][:], 4)).then_inc(hT_ready, 1)
                    act.wait_ge(chunk_ready, 3 * i + 1)
                    act.copy(qkv[pi][:, 0:SW].rearrange("p (j g d) -> p g j d", g=2, j=4),
                             pj[0][:].rearrange("p (g j d) -> p g j d", g=2, j=4)).then_inc(taken[0], 1)
                if m:
                    act.wait_ge(hg_turned, t + 1)
                    need(act, out_done, 2 * t)
                    act.copy(mixT[:, 0:4, :], heads(th[:], 4)).then_inc(hgT_ready, 1)
                    act.wait_ge(top_ready, t + 1)
                    for h in range(SW_HEADS):
                        act.activation(sm[:, h, :], sm[:, h, :], ACT.Exp, bias=negtop[:, h:h + 1], accum_out=total[:, h:h + 1])
                    act.activation(expsink[:], sinkd[:], ACT.Exp).then_inc(p_ready, 1)
                    for n in (0, 2):
                        act.wait_ge(p_turned, 4 * t + n + 1)
                        act.copy(pT[:, 4 * n:4 * n + 4, :], heads(tp[0][:], 4)).then_inc(pT_act, 1)
                if p:
                    act.wait_ge(chunk_ready, 3 * i + 3)
                    need(act, taken[2], i)
                    act.activation(tanh[:], pj[0][:], ACT.Tanh, scale=0.5).then_inc(tanh_ready, 1)
                if m:
                    act.wait_ge(a_turned, t + 1)
                    act.copy(mixT[:, 4:8, :], heads(tp[1][:], 4)).then_inc(aT_ready, 1)

            pipeline(act, step)

        @block.gpsimd
        def _(pool):
            pool.memset(power[:], -0.5)
            pool.memset(kT[:, 1, :], 0.0)
            pool.memset(vr[:, 1, :], 0.0)
            pool.drain()
            pool.memset(rstd[:], 0.0).then_inc(set_up_pool, 1)

            def rotate(t, ht, pt):
                pool.wait_ge(t_here[pt], 16 * 3 * (ht + 1))
                pool.wait_ge(taken[0], t + 1)
                pool.wait_ge(taken[1], t + 1)
                qk = qkv[pt][:, 0:SW + SW_KV].rearrange("p (h d) -> p h d", h=10)
                x1, x2 = qk[:, :, 0:ROPE], qk[:, :, ROPE:2 * ROPE]
                cos, sin = again(cs[pt][:, 0:ROPE], 10), again(cs[pt][:, ROPE:], 10)
                pool.tensor_tensor(rot[0][:], x1, cos, ALU.mult)
                pool.tensor_tensor(rot[1][:], x2, sin, ALU.mult)
                pool.tensor_tensor(rot[2][:], x2, cos, ALU.mult)
                pool.tensor_tensor(rot[3][:], x1, sin, ALU.mult)
                pool.drain()
                pool.tensor_tensor(x1, rot[0][:], rot[1][:], ALU.subtract)
                pool.tensor_tensor(x2, rot[2][:], rot[3][:], ALU.add).then_inc(roped, 1)

            def step(i, hi, pi, t, ht, pt):
                if i is not None:
                    rotate(i, hi, pi)
                if t is not None:
                    pool.wait_ge(var_ready, t + 1)
                    pool.tensor_tensor(rstd[:], moments[:, 1:2], power[:], ALU.pow).then_inc(rstd_ready, 1)

            pipeline(pool, step)

        @block.vector
        def _(dve):
            dve.wait_ge(consts_in, 16 * CONSTS)
            dve.wait_ge(set_up_pool, 1)

            def softmax(t, pt):
                by_group = sm[:].rearrange("p (j g) k -> p j g k", g=2)
                for r in range(2):
                    dve.wait_ge(scored, 2 * t + r + 1)
                    for g in range(2):
                        dve.scalar_tensor_tensor(by_group[:, 2 * r:2 * r + 2, g, :], sc[g][:].rearrange("p (j k) -> p j k", j=2), SW_DIM ** -0.5,
                                                 again(band[pt][:], 2), ALU.mult, ALU.add).then_inc(masked, 1)
                dve.drain()
                if pt == 0:
                    dve.tensor_copy(band[0][:, P:2 * P], before[:])
                dve.tensor_reduce(top[:], sm[:], AX, ALU.max)
                dve.drain()
                dve.tensor_tensor(by_pair(top[:]), by_pair(top[:]), sink_by_pair, ALU.max)
                dve.drain()
                dve.tensor_tensor(by_pair(sinkd[:]), sink_by_pair, by_pair(top[:]), ALU.subtract)
                dve.tensor_scalar(negtop[:], top[:], -1.0, None, ALU.mult).then_inc(top_ready, 1)
                dve.wait_ge(p_ready, t + 1)
                dve.tensor_tensor(total[:], total[:], expsink[:], ALU.add)
                dve.drain()
                dve.reciprocal(rden[:], total[:])
                for n in (1, 3):
                    dve.wait_ge(p_turned, 4 * t + n + 1)
                    dve.tensor_copy(pT[:, 4 * n:4 * n + 4, :], heads(tp[1][:], 4)).then_inc(pT_dve, 1)

            def step(i, hi, pi, t, ht, pt):
                p, m = i is not None, t is not None
                if m:
                    dve.wait_ge(qk_turned, t + 1)
                    dve.tensor_copy(kT[:, pt, :], tp[1][:, 0:P]).then_inc(kT_ready, 1)
                    dve.tensor_copy(vr[:, pt, :], qkv[pt][:, SW + SW_KV:QKV]).then_inc(v_kept, 1)
                if p:
                    dve.wait_ge(chunk_ready, 3 * i + 2)
                    dve.tensor_copy(qkv[pi][:, SW:QKV], pj[1][:, 0:2 * SW_KV]).then_inc(taken[1], 1)
                if m:
                    softmax(t, pt)
                    dve.drain()
                    dve.wait_ge(weighed, t + 1)
                    by_group = rden[:].rearrange("p (j g) -> p g j", g=2).unsqueeze(3).to_broadcast([P, 2, 4, SW_DIM])
                    dve.tensor_tensor(oa[:].rearrange("p (g j d) -> p g j d", g=2, j=4), ov[:].rearrange("p (g j d) -> p g j d", g=2, j=4),
                                      by_group, ALU.mult)
                    dve.drain()
                    dve.scalar_tensor_tensor(mixa[:], oa[:], 0.5, gate2[pt][:], ALU.mult, ALU.mult).then_inc(mixa_ready, 1)
                if p:
                    dve.wait_ge(tanh_ready, i + 1)
                    dve.scalar_tensor_tensor(gate2[pi][:], tanh[:], 1.0, pj[0][:], ALU.add, ALU.mult).then_inc(taken[2], 1)
                if m:
                    dve.wait_ge(t_here[pt], 16 * 3 * (ht + 1))
                    for c in range(2):
                        dve.wait_ge(out_done, 2 * t + c + 1)
                        cols = slice(c * BANK, (c + 1) * BANK)
                        dve.scalar_tensor_tensor(z[:, cols], xres[pt][:, cols], ALPHA, sc[c][:], ALU.mult, ALU.add).then_inc(z_ready, 1)
                    dve.drain()
                    for c in range(2):
                        dve.bn_stats(stats[:, c, :], z[:, c * BANK:(c + 1) * BANK])
                    dve.drain()
                    dve.bn_aggr(moments[:], stats[:])
                    dve.drain()
                    dve.tensor_scalar(moments[:, 1:2], moments[:, 1:2], 1e-5, None, ALU.add).then_inc(var_ready, 1)
                    need(dve, stored[pt], 16 * ht)
                    dve.wait_ge(rstd_ready, t + 1)
                    dve.tensor_scalar(y[pt][:], z[:], moments[:, 0:1], rstd[:], ALU.subtract, ALU.mult)
                    dve.drain()
                    dve.tensor_tensor(y[pt][:], y[pt][:], gain[:], ALU.mult)
                    dve.drain()
                    dve.tensor_tensor(y[pt][:], y[pt][:], shift[:], ALU.add).then_inc(y_ready, 1)

            pipeline(dve, step)


RW = 512
RW_HEADS = 8
RW_DIM = 64
PAIRS = RW_HEADS // 2
LORA = 64
RW_COLS = 3 * RW + 2 * LORA
LEVELS = 7


HALF = P // 2


def halves_of(ap, l, n):
    return ap.rearrange("p (b two w) -> p b two w", two=2, w=1 << l)[:, :, n, :]


def rwkv(nc, x, norm_g, w_in, gate_col, par, masks, mixed):
    with ExitStack() as ctx:
        s = Stage(nc, ctx, "rw")
        sb, sem = s.sb, s.sem
        w = sb("w", [P, KC, RW_COLS + RW])
        ident = sb("ident", [P, P])
        from_mid = sb("from_mid", [P, 2, P])
        halves = sb("halves", [P, 2])
        causal2 = sb("causal2", [P, 2, P])
        blocks = sb("blocks", [P, LEVELS, P])
        own_head = sb("own_head", [P, P])
        mu = sb("mu", [P, RW_COLS])
        w0, a0, k_k, k_a, r_k, gn_g, gn_b = rows = [sb(n, [P, RW]) for n in ("w0", "a0", "k_k", "k_a", "r_k", "gn_g", "gn_b")]
        up = sb("up", [P, RW])
        gains = sb("gains", [KC, P])
        gainT = sb("gainT", [P, KC])
        power = sb("power", [P, RW_HEADS])
        U = [sb(f"U{p}", [P, RW_COLS]) for p in range(2)]
        M = [sb(f"M{p}", [P, RW_COLS]) for p in range(2)]
        gate2 = [sb(f"gate2{p}", [P, RW]) for p in range(2)]
        tanh = sb("tanh", [P, RW])
        lowT = sb("lowT", [P, P])
        lw, a, kk, b = (sb(n, [P, RW]) for n in ("lw", "a", "kk", "b"))
        tmp, tmp2 = sb("tmp", [P, RW]), sb("tmp2", [P, RW])
        e_in, e_ex, e_neg = (sb(n, [P, RW]) for n in ("e_in", "e_ex", "e_neg"))
        e_tot = sb("e_tot", [P, PAIRS, 2])
        ss, rss, bonus, mean, var, rstd = (sb(n, [P, RW_HEADS]) for n in ("ss", "rss", "bonus", "mean", "var", "rstd"))
        krT = sb("krT", [P, PAIRS, 2, P])
        bT = sb("bT", [P, PAIRS, P])
        kT = sb("kT", [P, PAIRS, P])
        BA = sb("BA", [P, RW_HEADS, 2, P])
        KA = sb("KA", [P, RW_HEADS, 2, P])
        X = sb("X", [P, RW_HEADS, P])
        XT = sb("XT", [P, RW_HEADS, P])
        CT = sb("CT", [P, RW_HEADS, P])
        T1 = sb("T1", [P, RW_HEADS, P])
        Z, SA, y = e_neg, e_ex, e_in
        S = sb("S", [P, PAIRS, P])
        out = [sb(f"out{p}", [P, RW]) for p in range(2)]
        pj = [s.bank(f"pj{n}") for n in range(2)]
        B = [s.bank(f"b{n}") for n in range(6)]
        front = Normed(s, x, ident, [pj[1], pj[0]])

        CONSTS = 18
        consts_in, w_here, set_up, scaled_w, gain_turned = (sem(n) for n in ("consts_in", "w_here", "set_up", "scaled_w", "gain_turned"))
        shifted, stored = ([sem(f"{n}{p}") for p in range(2)] for n in ("shifted", "stored"))
        chunk_ready, tanh_ready = sem("chunk_ready"), sem("tanh_ready")
        taken = [sem(f"taken{c}") for c in range(5)]
        (mixed_in, low_ready, low_turned, lowT_ready, up_done, wa_ready, wa_tanh, lw_ready, cum_done, exp_ready) = (sem(n) for n in (
            "mixed_in", "low_ready", "low_turned", "lowT_ready", "up_done", "wa_ready", "wa_tanh", "lw_ready", "cum_done", "exp_ready"))
        ss_ready, rss_ready, dec_ready, turned4, krT_ready, bkT_ready = (sem(n) for n in (
            "ss_ready", "rss_ready", "dec_ready", "turned4", "krT_ready", "bkT_ready"))
        products, masked, first_turned, X_ready, XT_ready = (sem(n) for n in (
            "products", "masked", "first_turned", "X_ready", "XT_ready"))
        CT_ready, T1_done, T1_ready, corr_done = (sem(n) for n in ("CT_ready", "T1_done", "T1_ready", "corr_done"))
        S_in, Z_done, Z_ready, SA_done, SA_ready, y_done, y_ready, inc_done, S_out = (sem(n) for n in (
            "S_in", "Z_done", "Z_ready", "SA_done", "SA_ready", "y_done", "y_ready", "inc_done", "S_out"))
        var_ready, rstd_ready, out_ready = sem("var_ready"), sem("rstd_ready"), sem("out_ready")
        ORDER = [0, 1, 3, 2, 4]
        COLS = [(0, RW), (RW, 2 * RW), (2 * RW, 3 * RW), (3 * RW, RW_COLS), (RW_COLS, RW_COLS + RW)]

        block = s.block()

        @block.sync
        def _(sp):
            small = [(ident[:], masks["ident"]), (from_mid[:], masks["from_mid"]), (halves[:], masks["halves"]),
                     (causal2[:], masks["causal2"]), (blocks[:], masks["blocks"]), (own_head[:], masks["own_head"]),
                     (mu[:], row(par["mu"], 0, RW_COLS)), (up[0:LORA, :], par["w_up"]), (up[LORA:P, :], par["a_up"]),
                     (gains[:], by_chunk(norm_g))]
            small += [(r[:], row(par[n], 0, RW)) for r, n in zip(rows, ("w0", "a0", "k_k", "k_a", "r_k", "gn_g", "gn_b"))]
            small += [(M[0][0:1, :], masks["zeros"][:, 0:RW_COLS])]
            assert len(small) == CONSTS
            for dst, src in small:
                sp.dma_start(dst, src).then_inc(consts_in, 16)
            for kc in range(KC):
                sp.dma_start(w[:, kc, 0:RW_COLS], w_in[kc * P:(kc + 1) * P, 0:RW_COLS]).then_inc(w_here, 16)
                sp.dma_start(w[:, kc, RW_COLS:], w_in[kc * P:(kc + 1) * P, gate_col:gate_col + RW]).then_inc(w_here, 16)
            front.load(sp, 0)

            def shift(i, pi, first):
                for c in range(4):
                    sp.wait_ge(taken[c], i + 1)
                if not first:
                    need(sp, out_ready, i - 1)
                    sp.dma_start(M[pi][0:1, :], U[1 - pi][P - 1:P, :]).then_inc(shifted[pi], 16)
                sp.dma_start(M[pi][1:P, :], U[pi][0:P - 1, :]).then_inc(shifted[pi], 16)

            def step(i, hi, pi, t, ht, pt):
                if i is not None:
                    if not (isinstance(i, int) and i == TILES - 1):
                        front.load(sp, i + 1)
                    shift(i, pi, t is None)
                if t is not None:
                    sp.wait_ge(out_ready, t + 1)
                    sp.dma_start(mixed[bass.ds(t * P, P), 0:RW], out[pt][:]).then_inc(stored[pt], 16)

            pipeline(sp, step)
            for p in range(2):
                sp.wait_ge(stored[p], 16 * TILES // 2)

        def shift_count(ht, pt):
            return 32 * ht + (16 if pt == 0 else 32)

        @block.tensor
        def _(pe):
            pe.wait_ge(consts_in, 16 * CONSTS)
            pe.transpose(B[0][:, 0:KC], gains[:], ident[0:KC, 0:KC]).then_inc(gain_turned, 1)
            pe.wait_ge(scaled_w, KC)

            def project(i, c, lo=0, hi=None):
                a0_, b0_ = COLS[c]
                hi = hi or b0_ - a0_
                pos = ORDER.index(c)
                if lo == 0:
                    if pos == 0:
                        pe.wait_ge(front.ready, 2 * i + 2)
                    if pos >= 2:
                        pe.wait_ge(taken[ORDER[pos - 2]], i + 1)
                for kc in range(KC):
                    last = pe.matmul(pj[pos % 2][:, lo:hi], front.hT[:, kc, :], w[:, kc, a0_ + lo:a0_ + hi], start=kc == 0, stop=kc == KC - 1)
                return last

            def turn_low(t, pt):
                pe.wait_ge(low_ready, t + 1)
                pe.transpose(B[0][:, 0:P], M[pt][:, 3 * RW:RW_COLS], ident[:]).then_inc(low_turned, 1)

            def raise_low(t):
                pe.wait_ge(lowT_ready, t + 1)
                pe.matmul(B[1][:], lowT[0:LORA, :], up[0:LORA, :], start=True, stop=True)
                pe.matmul(B[2][:], lowT[LORA:P, :], up[LORA:P, :], start=True, stop=True).then_inc(up_done, 1)

            def cumulate(t):
                pe.wait_ge(lw_ready, t + 1)
                need(pe, S_out, t)
                for n in range(2):
                    pe.matmul(B[3 + n][:], from_mid[:, n, :], lw[:], start=True, stop=True)
                for p in range(PAIRS):
                    last = pe.matmul(B[5][:, 2 * p:2 * p + 2], lw[:, p * P:(p + 1) * P], halves[:], start=True, stop=True)
                last.then_inc(cum_done, 1)

            def turn_all(t, pt):
                pe.wait_ge(dec_ready, t + 1)
                for bank, src in ((0, kk[:]), (1, M[pt][:, 0:RW]), (2, b[:]), (3, M[pt][:, RW:2 * RW])):
                    for p in range(PAIRS):
                        last = pe.transpose(B[bank][:, p * P:(p + 1) * P], src[:, p * P:(p + 1) * P], ident[:])
                    last.then_inc(turned4, 1)

            def multiply(t, r):
                if r == 0:
                    pe.wait_ge(krT_ready, 2 * t + 2)
                    pe.wait_ge(bkT_ready, 2 * t + 2)
                else:
                    pe.wait_ge(masked, 8 * t + 2)
                for n, (lhs, banks) in enumerate(((bT, ((4, 5), (2, 3))[r]), (kT, ((0, 1), (4, 5))[r]))):
                    for p in (2 * r, 2 * r + 1):
                        for o in range(2):
                            part = slice(o * RW_DIM, (o + 1) * RW_DIM)
                            cols = slice((p - 2 * r) * 2 * P, (p - 2 * r + 1) * 2 * P)
                            last = pe.matmul(B[banks[o]][:, cols], lhs[part, p, :], krT[part, p, :, :].rearrange("k n t -> k (n t)"), start=True, stop=True)
                    last.then_inc(products, 1)

            def turn_first(t, g):
                pe.wait_ge(XT_ready, 2 * LEVELS * t + g + 1)
                if g == 0:
                    pe.wait_ge(masked, 8 * t + 8)
                for h in range(4):
                    last = pe.transpose(B[3 * g][:, h * P:(h + 1) * P], XT[:, 4 * g + h, :], ident[:])
                last.then_inc(first_turned, 1)

            def level(t, l, g, stage):
                hs = range(4 * g, 4 * g + 4)
                done = 12 * t + 2 * (l - 1)
                top = l == LEVELS - 1
                if stage == 0:
                    pe.wait_ge(CT_ready, done + g + 1)
                    pe.wait_ge(X_ready, (2 * LEVELS - 2) * t + 2 * (l - 1) + g + 1)
                    width = P // 2 if top else P
                    for h in hs:
                        last = pe.matmul(B[3 * g][:, (h % 4) * P:(h % 4) * P + width], CT[:, h, :], X[:, h, 0:width], start=True, stop=True)
                    last.then_inc(T1_done, 1)
                else:
                    pe.wait_ge(T1_ready, done + g + 1)
                    pe.wait_ge(XT_ready, 2 * LEVELS * t + 2 * (l - 1) + g + 1)
                    if not top:
                        for h in hs:
                            pe.matmul(B[3 * g + 1][:, (h % 4) * HALF:(h % 4 + 1) * HALF], XT[:, h, :], halves_of(T1[:, h, :], l, 0), start=True, stop=True)
                    for h in hs:
                        lhs, rows = (T1[:, h, 0:HALF], HALF) if top else (T1[:, h, :], P)
                        last = pe.matmul(B[3 * g + 2][0:rows, (h % 4) * HALF:(h % 4 + 1) * HALF], lhs, halves_of(XT[:, h, :], l, 1), start=True, stop=True)
                    last.then_inc(corr_done, 1)

            def solve(t, pt):
                V = M[pt][:, 2 * RW:3 * RW]
                pe.wait_ge(S_in, t + 1)
                for p in range(PAIRS):
                    pe.matmul(B[0][:, p * P:(p + 1) * P], krT[:, p, 0, :], S[:, p, :], start=True, stop=False)
                    for o in range(2):
                        h = 2 * p + o
                        last = pe.matmul(B[0][:, h * RW_DIM:(h + 1) * RW_DIM], KA[:, h, 0, :], V[:, h * RW_DIM:(h + 1) * RW_DIM], start=False, stop=o == 1)
                last.then_inc(Z_done, 1)

            def read_out(t, pt):
                V = M[pt][:, 2 * RW:3 * RW]
                pe.wait_ge(XT_ready, 2 * LEVELS * t + 2 * LEVELS)
                pe.wait_ge(Z_ready, t + 1)
                for h in range(RW_HEADS):
                    cols = slice(h * RW_DIM, (h + 1) * RW_DIM)
                    last = pe.matmul(B[1][:, cols], XT[:, h, :], Z[:, cols], start=True, stop=True)
                last.then_inc(SA_done, 1)
                for p in range(PAIRS):
                    pe.matmul(B[2][:, p * P:(p + 1) * P], krT[:, p, 1, :], S[:, p, :], start=True, stop=False)
                    for o in range(2):
                        h = 2 * p + o
                        cols = slice(h * RW_DIM, (h + 1) * RW_DIM)
                        pe.matmul(B[2][:, cols], KA[:, h, 1, :], V[:, cols], start=False, stop=False)
                        if p == 0 and o == 0:
                            pe.wait_ge(SA_ready, t + 1)
                        last = pe.matmul(B[2][:, cols], BA[:, h, 1, :], SA[:, cols], start=False, stop=o == 1)
                last.then_inc(y_done, 1)
                for p in range(PAIRS):
                    cols = slice(p * P, (p + 1) * P)
                    pe.matmul(B[3][:, cols], b[:, cols], SA[:, cols], start=True, stop=False)
                    last = pe.matmul(B[3][:, cols], M[pt][:, RW + p * P:RW + (p + 1) * P], V[:, cols], start=False, stop=True)
                last.then_inc(inc_done, 1)

            def step(i, hi, pi, t, ht, pt):
                pr, m = i is not None, t is not None
                if pr:
                    front.turn(pe, i, (taken[4], taken[2]))
                    project(i, 0).then_inc(chunk_ready, 1)
                if m:
                    turn_low(t, pt)
                if pr:
                    project(i, 1, 0, 256)
                if m:
                    raise_low(t)
                if pr:
                    project(i, 1, 256, 512).then_inc(chunk_ready, 1)
                    project(i, 3).then_inc(chunk_ready, 1)
                if m:
                    cumulate(t)
                if pr:
                    project(i, 2).then_inc(chunk_ready, 1)
                if m:
                    turn_all(t, pt)
                if pr:
                    project(i, 4, 0, 256)
                if m:
                    multiply(t, 0)
                    multiply(t, 1)
                if pr:
                    project(i, 4, 256, 512).then_inc(chunk_ready, 1)
                if m:
                    for g in range(2):
                        turn_first(t, g)
                    for l in range(1, LEVELS):
                        for g in range(2):
                            level(t, l, g, 0)
                        for g in range(2):
                            level(t, l, g, 1)
                    solve(t, pt)
                    read_out(t, pt)

            pipeline(pe, step)

        @block.scalar
        def _(act):
            act.wait_ge(set_up, 1)
            front.square(act, 0)

            def take(i, pi, c, t=None, ht=None, pt=None):
                pos = ORDER.index(c)
                act.wait_ge(chunk_ready, 5 * i + pos + 1)
                lo, hi = COLS[c]
                if c == 4:
                    need(act, taken[4], i)
                    act.activation(tanh[:], pj[0][:], ACT.Tanh, scale=0.5).then_inc(tanh_ready, 1)
                    return
                if c == 0:
                    if t is not None:
                        act.wait_ge(shifted[pt], shift_count(ht, pt))
                act.copy(U[pi][:, lo:hi], pj[pos % 2][:, 0:hi - lo]).then_inc(taken[c], 1)

            def step(i, hi, pi, t, ht, pt):
                pr, m = i is not None, t is not None
                if pr:
                    front.take(act, i)
                    take(i, pi, 0, t, ht, pt)
                if m:
                    act.wait_ge(mixed_in, t + 1)
                    act.activation(M[pt][:, 3 * RW:3 * RW + LORA], M[pt][:, 3 * RW:3 * RW + LORA], ACT.Tanh).then_inc(low_ready, 1)
                    act.wait_ge(low_turned, t + 1)
                    act.copy(lowT[:], B[0][:, 0:P]).then_inc(lowT_ready, 1)
                if pr:
                    take(i, pi, 1)
                if m:
                    act.wait_ge(wa_ready, t + 1)
                    act.activation(e_in[:], tmp[:], ACT.Tanh, scale=0.5)
                    act.activation(e_ex[:], tmp2[:], ACT.Tanh, scale=0.5).then_inc(wa_tanh, 1)
                if pr:
                    take(i, pi, 3)
                if m:
                    act.wait_ge(cum_done, t + 1)
                    act.wait_ge(lw_ready, t + 1)
                    act.activation(e_in[:], B[3][:], ACT.Exp)
                    act.activation(e_neg[:], B[3][:], ACT.Exp, scale=-1.0)
                    act.activation(e_ex[:], B[4][:], ACT.Exp)
                    act.activation(e_tot[:].rearrange("p h c -> p (h c)"), B[5][:, 0:2 * PAIRS], ACT.Exp).then_inc(exp_ready, 1)
                if pr:
                    take(i, pi, 2)
                if m:
                    for n in range(2):
                        act.wait_ge(turned4, 4 * t + n + 1)
                        act.copy(krT[:, :, n, :], heads(B[n][:], PAIRS)).then_inc(krT_ready, 1)
                if pr:
                    if not (isinstance(i, int) and i == TILES - 1):
                        front.square(act, i + 1)
                    take(i, pi, 4)
                if m:
                    for l in range(1, LEVELS):
                        for g in range(2):
                            act.wait_ge(T1_done, 12 * t + 2 * (l - 1) + g + 1)
                            width = HALF if l == LEVELS - 1 else P
                            act.copy(T1[:, 4 * g:4 * g + 4, 0:width], heads(B[3 * g][:], 4)[:, :, 0:width]).then_inc(T1_ready, 1)
                    act.wait_ge(Z_done, t + 1)
                    act.activation(Z[:], B[0][:], ACT.Copy, scale=-1.0).then_inc(Z_ready, 1)
                    act.wait_ge(SA_done, t + 1)
                    act.copy(SA[:], B[1][:]).then_inc(SA_ready, 1)
                    act.wait_ge(y_done, t + 1)
                    act.copy(y[:], B[2][:]).then_inc(y_ready, 1)

            pipeline(act, step)

        @block.gpsimd
        def _(pool):
            pool.memset(power[:], -0.5)
            pool.memset(front.power[:], -0.5)
            pool.memset(S[:], 0.0)
            pool.drain()
            pool.memset(rss[:], 0.0).then_inc(set_up, 1)
            front.root(pool, 0)

            def step(i, hi, pi, t, ht, pt):
                pr, m = i is not None, t is not None
                if m:
                    pool.wait_ge(ss_ready, t + 1)
                    pool.tensor_tensor(rss[:], ss[:], power[:], ALU.pow).then_inc(rss_ready, 1)
                if pr and not (isinstance(i, int) and i == TILES - 1):
                    front.root(pool, i + 1)
                if m:
                    pool.wait_ge(masked, 8 * t + 8)
                    for l in range(1, LEVELS):
                        for g in range(2):
                            if l > 1:
                                pool.wait_ge(T1_done, 12 * t + 2 * (l - 1) + g - 1)
                            pool.tensor_tensor(CT[:, 4 * g:4 * g + 4, :], BA[:, 4 * g:4 * g + 4, 0, :], again(blocks[:, l, :], 4), ALU.mult).then_inc(CT_ready, 1)
                    pool.wait_ge(var_ready, t + 1)
                    pool.tensor_tensor(rstd[:], var[:], power[:], ALU.pow).then_inc(rstd_ready, 1)

            pipeline(pool, step)

        @block.vector
        def _(dve):
            dve.wait_ge(consts_in, 16 * CONSTS)
            dve.wait_ge(set_up, 1)
            dve.wait_ge(gain_turned, 1)
            dve.tensor_copy(gainT[:], B[0][:, 0:KC])
            dve.wait_ge(w_here, 16 * 2 * KC)
            dve.drain()
            for kc in range(KC):
                dve.tensor_scalar(w[:, kc, :], w[:, kc, :], gainT[:, kc:kc + 1], None, ALU.mult).then_inc(scaled_w, 1)
            front.mean(dve, 0)
            front.scale(dve, 0)
            C2 = math.exp(-0.5) / 2

            def tt(out_, a_, b_, op):
                return dve.tensor_tensor(out_, a_, b_, op)

            def gates(t, ht, pt):
                dve.wait_ge(up_done, t + 1)
                tt(tmp[:], B[1][:], w0[:], ALU.add)
                tt(tmp2[:], B[2][:], a0[:], ALU.add).then_inc(wa_ready, 1)
                dve.wait_ge(wa_tanh, t + 1)
                dve.tensor_scalar(lw[:], e_in[:], -C2, -C2, ALU.mult, ALU.add)
                dve.tensor_scalar(a[:], e_ex[:], 0.5, 0.5, ALU.mult, ALU.add).then_inc(lw_ready, 1)

            def keys(t, pt):
                r, k = M[pt][:, 0:RW], M[pt][:, RW:2 * RW]
                tt(kk[:], k, k_k[:], ALU.mult)
                dve.drain()
                tt(tmp[:], kk[:], kk[:], ALU.mult)
                dve.scalar_tensor_tensor(tmp2[:], a[:], 1.0, k_a[:], ALU.subtract, ALU.mult)
                dve.drain()
                dve.tensor_reduce(ss[:], heads(tmp[:], RW_HEADS), AX, ALU.add)
                dve.scalar_tensor_tensor(k, tmp2[:], 1.0, k, ALU.add, ALU.mult)
                dve.drain()
                dve.tensor_scalar(ss[:], ss[:], 1e-24, None, ALU.max).then_inc(ss_ready, 1)
                tt(tmp2[:], r, k, ALU.mult)
                dve.drain()
                tt(tmp2[:], tmp2[:], r_k[:], ALU.mult)
                dve.drain()
                dve.tensor_reduce(bonus[:], heads(tmp2[:], RW_HEADS), AX, ALU.add)
                dve.wait_ge(rss_ready, t + 1)
                tt(heads(kk[:], RW_HEADS), heads(kk[:], RW_HEADS), spread(rss[:], RW_DIM), ALU.mult)
                dve.drain()
                tt(b[:], kk[:], a[:], ALU.mult)
                dve.drain()
                dve.wait_ge(exp_ready, t + 1)
                tt(kk[:], kk[:], e_ex[:], ALU.mult)
                tt(r, r, e_in[:], ALU.mult)
                tt(b[:], b[:], e_neg[:], ALU.mult)
                tt(k, k, e_neg[:], ALU.mult).then_inc(dec_ready, 1)
                for p in range(PAIRS):
                    last = dve.tensor_scalar(S[:, p, :], S[:, p, :], e_tot[:, p, 0:1], None, ALU.mult)
                last.then_inc(S_in, 1)

            def mask_products(t, r, n):
                dve.wait_ge(products, 4 * t + 2 * r + n + 1)
                banks = (((4, 5), (2, 3))[r], ((0, 1), (4, 5))[r])[n]
                dst = (BA, KA)[n]
                for o in range(2):
                    tt(dst[:, 4 * r + o:4 * r + 4:2].rearrange("p h n t -> p h (n t)"), heads(B[banks[o]][:], 2),
                       again(causal2[:].rearrange("p n t -> p (n t)"), 2), ALU.mult).then_inc(masked, 1)

            def first_level(t, g):
                hs = slice(4 * g, 4 * g + 4)
                tt(X[:, hs, :], BA[:, hs, 0, :], again(blocks[:, 0, :], 4), ALU.mult)
                dve.drain()
                tt(XT[:, hs, :], again(ident[:], 4), X[:, hs, :], ALU.subtract).then_inc(XT_ready, 1)

            def mix_shifted(i, hi, pi, part):
                if part == 0:
                    dve.wait_ge(shifted[pi], shift_count(hi, pi))
                    tt(M[pi][:], M[pi][:], U[pi][:], ALU.subtract)
                elif part == 1:
                    tt(M[pi][:], M[pi][:], mu[:], ALU.mult)
                else:
                    tt(M[pi][:], M[pi][:], U[pi][:], ALU.add).then_inc(mixed_in, 1)

            def step(i, hi, pi, t, ht, pt):
                pr, m = i is not None, t is not None
                if m:
                    gates(t, ht, pt)
                    dve.drain()
                    keys(t, pt)
                    for n in range(2):
                        dve.wait_ge(turned4, 4 * t + 3 + n)
                        dve.tensor_copy((bT, kT)[n][:], heads(B[2 + n][:], PAIRS)).then_inc(bkT_ready, 1)
                if pr and not (isinstance(i, int) and i == TILES - 1):
                    front.mean(dve, i + 1)
                    front.scale(dve, i + 1)
                if m:
                    mask_products(t, 0, 0)
                    mask_products(t, 0, 1)
                    dve.drain()
                    first_level(t, 0)
                    mask_products(t, 1, 0)
                    dve.drain()
                    first_level(t, 1)
                    mask_products(t, 1, 1)
                if pr:
                    dve.wait_ge(tanh_ready, i + 1)
                    dve.scalar_tensor_tensor(gate2[pi][:], tanh[:], 1.0, pj[0][:], ALU.add, ALU.mult).then_inc(taken[4], 1)
                    if not m:
                        for part in range(3):
                            mix_shifted(i, hi, pi, part)
                            dve.drain()
                if m:
                    for g in range(2):
                        if g == 0:
                            dve.drain()
                        dve.wait_ge(first_turned, 2 * t + g + 1)
                        dve.tensor_copy(X[:, 4 * g:4 * g + 4, :], heads(B[3 * g][:], 4)).then_inc(X_ready, 1)
                    for l in range(1, LEVELS):
                        for g in range(2):
                            hs = slice(4 * g, 4 * g + 4)
                            if g == 0:
                                dve.drain()
                            dve.wait_ge(corr_done, 12 * t + 2 * (l - 1) + g + 1)
                            compact = lambda bank, rows: bank[0:rows, 0:4 * HALF].rearrange("p (b w) -> p b w", w=1 << l)
                            view = lambda ap, rows, n: halves_of(ap[0:rows, hs, :].rearrange("p h t -> p (h t)"), l, n)
                            rows = HALF if l == LEVELS - 1 else P
                            if l < LEVELS - 1:
                                tt(view(X, P, 0), view(X, P, 0), compact(B[3 * g + 1], P), ALU.subtract).then_inc(X_ready, 1)
                            tt(view(XT, rows, 1), view(XT, rows, 1), compact(B[3 * g + 2], rows), ALU.subtract).then_inc(XT_ready, 1)
                        if pr and 1 <= l <= 3:
                            mix_shifted(i, hi, pi, l - 1)
                    dve.wait_ge(inc_done, t + 1)
                    tt(heads(tmp[:], PAIRS), heads(B[3][:], PAIRS), again(own_head[:], PAIRS), ALU.mult)
                    dve.drain()
                    tt(S[:], S[:], heads(tmp[:], PAIRS), ALU.add)
                    dve.drain()
                    for p in range(PAIRS):
                        last = dve.tensor_scalar(S[:, p, :], S[:, p, :], e_tot[:, p, 1:2], None, ALU.mult)
                    last.then_inc(S_out, 1)
                    H = lambda ap: heads(ap, RW_HEADS)
                    dve.wait_ge(y_ready, t + 1)
                    dve.tensor_reduce(mean[:], H(y[:]), AX, ALU.add)
                    dve.drain()
                    dve.tensor_scalar(mean[:], mean[:], 1.0 / RW_DIM, None, ALU.mult)
                    dve.drain()
                    tt(H(y[:]), H(y[:]), spread(mean[:], RW_DIM), ALU.subtract)
                    dve.drain()
                    tt(tmp[:], y[:], y[:], ALU.mult)
                    dve.drain()
                    dve.tensor_reduce(var[:], H(tmp[:]), AX, ALU.add)
                    dve.drain()
                    dve.tensor_scalar(var[:], var[:], 1.0 / RW_DIM, 64e-5, ALU.mult, ALU.add).then_inc(var_ready, 1)
                    need(dve, stored[pt], 16 * ht)
                    tt(H(tmp[:]), H(M[pt][:, 2 * RW:3 * RW]), spread(bonus[:], RW_DIM), ALU.mult)
                    dve.wait_ge(rstd_ready, t + 1)
                    tt(H(y[:]), H(y[:]), spread(rstd[:], RW_DIM), ALU.mult)
                    dve.drain()
                    tt(y[:], y[:], gn_g[:], ALU.mult)
                    tt(tmp[:], tmp[:], gn_b[:], ALU.add)
                    dve.drain()
                    tt(y[:], y[:], tmp[:], ALU.add)
                    dve.drain()
                    dve.scalar_tensor_tensor(out[pt][:], y[:], 0.5, gate2[pt][:], ALU.mult, ALU.mult).then_inc(out_ready, 1)

            pipeline(dve, step)


FX = 512
FX_HEADS = 8
FX_DIM = 64


def fox_project(nc, x, norm_g, w_in, q_g, k_g, b_f, masks, keysT, values, cum3, queries, gates):
    with ExitStack() as ctx:
        s = Stage(nc, ctx, "fp")
        sb, sem = s.sb, s.sem
        WIDTH = 4 * FX + FX_HEADS
        w = sb("w", [P, KC, WIDTH])
        COLS = [(0, FX), (FX, 2 * FX), (2 * FX, 3 * FX), (3 * FX, 4 * FX), (4 * FX, WIDTH)]
        ident = sb("ident", [P, P])
        gains, gainT = sb("gains", [KC, P]), sb("gainT", [P, KC])
        qk_gain = sb("qk_gain", [P, 2, FX_DIM])
        bias = sb("bias", [P, FX_HEADS])
        power = sb("power", [P, 2 * FX_HEADS])
        qk = [sb(f"qk{p}", [P, 2 * FX]) for p in range(2)]
        tanh = sb("tanh", [P, FX])
        gate2 = [sb(f"gate2{p}", [P, FX]) for p in range(2)]
        sq = sb("sq", [P, 2 * FX])
        ms, rms = sb("ms", [P, 2 * FX_HEADS]), sb("rms", [P, 2 * FX_HEADS])
        qT = [sb(f"qT{p}", [P, 4 * P]) for p in range(2)]
        forget = sb("forget", [P, TILES, FX_HEADS])
        fa, fe = sb("fa", [P, TILES, FX_HEADS]), sb("fe", [P, TILES, FX_HEADS])
        lf = sb("lf", [FX_HEADS, SEQ])
        cum = sb("cum", [FX_HEADS, SEQ])
        ones = sb("ones", [FX_HEADS, SEQ])
        part = [sb(f"part{n}", [FX_HEADS, SEQ], BF16) for n in range(3)]
        pj = [s.bank(f"pj{n}") for n in range(2)]
        tq, tk = s.bank("tq"), s.bank("tk")
        tf = [s.bank(f"tf{n}") for n in range(4)]
        front = Normed(s, x, ident, [pj[1], pj[0]])

        consts_in, w_here, set_up, scaled_w, gain_turned = (sem(n) for n in ("consts_in", "w_here", "set_up", "scaled_w", "gain_turned"))
        chunk_ready, tanh_ready = sem("chunk_ready"), sem("tanh_ready")
        taken = [sem(f"taken{c}") for c in range(5)]
        ms_ready, rms_ready, qk_ready, turned, qT_ready, kT_ready = (sem(n) for n in ("ms_ready", "rms_ready", "qk_ready", "turned", "qT_ready", "kT_ready"))
        stored, gate_stored = ([sem(f"{n}{p}") for p in range(2)] for n in ("stored", "gate_stored"))
        forget_ready, exp_ready, ln_ready, soft_ready, forget_turned, parts_ready, parts_moved = (sem(n) for n in (
            "forget_ready", "exp_ready", "ln_ready", "soft_ready", "forget_turned", "parts_ready", "parts_moved"))
        block = s.block()
        CONSTS = 5

        @block.sync
        def _(sp):
            for dst, src in ((ident[:], masks["ident"]), (gains[:], by_chunk(norm_g)), (qk_gain[:, 0, :], row(q_g, 0, FX_DIM)),
                             (qk_gain[:, 1, :], row(k_g, 0, FX_DIM)), (bias[:], row(b_f, 0, FX_HEADS))):
                sp.dma_start(dst, src).then_inc(consts_in, 16)
            gate = RW_COLS + 3 * FX + FX_HEADS + 512
            for kc in range(KC):
                rows = slice(kc * P, (kc + 1) * P)
                sp.dma_start(w[:, kc, 0:3 * FX], w_in[rows, RW_COLS:RW_COLS + 3 * FX]).then_inc(w_here, 16)
                sp.dma_start(w[:, kc, 3 * FX:4 * FX], w_in[rows, gate:gate + FX]).then_inc(w_here, 16)
                sp.dma_start(w[:, kc, 4 * FX:], w_in[rows, RW_COLS + 3 * FX:RW_COLS + 3 * FX + FX_HEADS]).then_inc(w_here, 16)
            front.load(sp, 0)

            def step(i, hi, pi, t, ht, pt):
                if i is not None:
                    if not (isinstance(i, int) and i == TILES - 1):
                        front.load(sp, i + 1)
                    sp.wait_ge(taken[3], i + 1)
                    sp.dma_start(gates[bass.ds(i * P, P), :], gate2[pi][:]).then_inc(gate_stored[pi], 16)
                if t is not None:
                    sp.wait_ge(qT_ready, t + 1)
                    sp.dma_start(queries[bass.ds(t * P, P), :], qT[pt][:]).then_inc(stored[pt], 16)

            pipeline(sp, step)
            sp.wait_ge(parts_ready, 1)
            for n in range(3):
                sp.dma_start(cum3[n * FX_HEADS:(n + 1) * FX_HEADS, :], part[n][:]).then_inc(parts_moved, 16)
            sp.wait_ge(parts_moved, 48)
            for p in range(2):
                sp.wait_ge(stored[p], 16 * TILES // 2)
                sp.wait_ge(gate_stored[p], 16 * TILES // 2)

        @block.tensor
        def _(pe):
            pe.wait_ge(consts_in, 16 * CONSTS)
            pe.transpose(tq[:, 0:KC], gains[:], ident[0:KC, 0:KC]).then_inc(gain_turned, 1)
            pe.wait_ge(scaled_w, KC)

            def project(i, c):
                lo, hi = COLS[c]
                if c == 0:
                    pe.wait_ge(front.ready, 2 * i + 2)
                if c >= 2:
                    pe.wait_ge(taken[c - 2], i + 1)
                for kc in range(KC):
                    last = pe.matmul(pj[c % 2][:, 0:hi - lo], front.hT[:, kc, :], w[:, kc, lo:hi], start=kc == 0, stop=kc == KC - 1)
                last.then_inc(chunk_ready, 1)

            def step(i, hi, pi, t, ht, pt):
                if i is not None:
                    front.turn(pe, i, (taken[3], taken[4]))
                    for c in range(2):
                        project(i, c)
                if t is not None:
                    pe.wait_ge(qk_ready, t + 1)
                    for c in range(8):
                        last = pe.transpose((tq, tk)[c // 4][:, (c % 4) * P:(c % 4 + 1) * P], qk[pt][:, c * P:(c + 1) * P], ident[:])
                    last.then_inc(turned, 1)
                if i is not None:
                    for c in range(2, 5):
                        project(i, c)

            pipeline(pe, step)
            pe.wait_ge(soft_ready, 1)
            for t in range(TILES):
                last = pe.transpose(tf[t // 4][0:FX_HEADS, (t % 4) * P:(t % 4 + 1) * P], forget[:, t, :], ident[:])
            last.then_inc(forget_turned, 1)

        @block.scalar
        def _(act):
            act.wait_ge(set_up, 1)
            front.square(act, 0)

            def step(i, hi, pi, t, ht, pt):
                if i is not None:
                    front.take(act, i)
                    act.wait_ge(chunk_ready, 5 * i + 1)
                    act.copy(qk[pi][:, 0:FX], pj[0][:]).then_inc(taken[0], 1)
                if t is not None:
                    act.wait_ge(turned, t + 1)
                    need(act, stored[pt], 16 * ht)
                    act.copy(qT[pt][:], tq[:]).then_inc(qT_ready, 1)
                if i is not None:
                    act.wait_ge(chunk_ready, 5 * i + 3)
                    act.copy(values[:, bass.ds(i, 1), :], pj[0][:].unsqueeze(1)).then_inc(taken[2], 1)
                    if not (isinstance(i, int) and i == TILES - 1):
                        front.square(act, i + 1)
                    act.wait_ge(chunk_ready, 5 * i + 4)
                    need(act, taken[3], i)
                    act.activation(tanh[:], pj[1][:], ACT.Tanh, scale=0.5).then_inc(tanh_ready, 1)

            pipeline(act, step)
            act.wait_ge(forget_ready, 1)
            act.activation(fe[:], fe[:], ACT.Exp, scale=-1.0).then_inc(exp_ready, 1)
            act.drain()
            act.activation(fe[:], fe[:], ACT.Ln, bias=1.0).then_inc(ln_ready, 1)

        @block.gpsimd
        def _(pool):
            pool.memset(power[:], -0.5)
            pool.memset(ones[:], 1.0)
            pool.memset(cum3[:], 0.0)
            pool.memset(front.power[:], -0.5)
            pool.drain()
            pool.memset(rms[:], 0.0).then_inc(set_up, 1)
            front.root(pool, 0)

            def step(i, hi, pi, t, ht, pt):
                if t is not None:
                    pool.wait_ge(ms_ready, t + 1)
                    pool.tensor_tensor(rms[:], ms[:], power[:], ALU.pow).then_inc(rms_ready, 1)
                if i is not None and not (isinstance(i, int) and i == TILES - 1):
                    front.root(pool, i + 1)

            pipeline(pool, step)

        @block.vector
        def _(dve):
            dve.wait_ge(consts_in, 16 * CONSTS)
            dve.wait_ge(set_up, 1)
            dve.wait_ge(gain_turned, 1)
            dve.tensor_copy(gainT[:], tq[:, 0:KC])
            dve.tensor_scalar(qk_gain[:, 0, :], qk_gain[:, 0, :], FX_DIM ** -0.5, None, ALU.mult)
            dve.wait_ge(w_here, 16 * 3 * KC)
            dve.drain()
            for kc in range(KC):
                dve.tensor_scalar(w[:, kc, :], w[:, kc, :], gainT[:, kc:kc + 1], None, ALU.mult).then_inc(scaled_w, 1)
            front.mean(dve, 0)
            front.scale(dve, 0)
            H = 2 * FX_HEADS

            def step(i, hi, pi, t, ht, pt):
                if t is not None:
                    dve.wait_ge(taken[0], t + 1)
                    dve.tensor_tensor(sq[:], qk[pt][:], qk[pt][:], ALU.mult)
                    dve.drain()
                    dve.tensor_reduce(ms[:], heads(sq[:], H), AX, ALU.add)
                    dve.drain()
                    dve.tensor_scalar(ms[:], ms[:], 1.0 / FX_DIM, 1e-6, ALU.mult, ALU.add).then_inc(ms_ready, 1)
                    dve.wait_ge(rms_ready, t + 1)
                    dve.tensor_tensor(heads(qk[pt][:], H), heads(qk[pt][:], H), spread(rms[:], FX_DIM), ALU.mult)
                    dve.drain()
                    four = qk[pt][:].rearrange("p (n h d) -> p n h d", n=2, h=FX_HEADS)
                    dve.tensor_tensor(four, four, qk_gain[:].unsqueeze(2).to_broadcast([P, 2, FX_HEADS, FX_DIM]), ALU.mult).then_inc(qk_ready, 1)
                if i is not None:
                    dve.wait_ge(chunk_ready, 5 * i + 2)
                    dve.tensor_copy(qk[pi][:, FX:], pj[1][:]).then_inc(taken[1], 1)
                    dve.drain()
                if t is not None:
                    dve.wait_ge(turned, t + 1)
                    dve.tensor_copy(keysT[:, :, bass.ds(t * P, P)], heads(tk[:], 4)).then_inc(kT_ready, 1)
                if i is not None:
                    if not (isinstance(i, int) and i == TILES - 1):
                        front.mean(dve, i + 1)
                        front.scale(dve, i + 1)
                    need(dve, gate_stored[pi], 16 * hi)
                    dve.wait_ge(tanh_ready, i + 1)
                    dve.scalar_tensor_tensor(gate2[pi][:], tanh[:], 1.0, pj[1][:], ALU.add, ALU.mult).then_inc(taken[3], 1)
                    dve.wait_ge(chunk_ready, 5 * i + 5)
                    dve.tensor_copy(forget[:, bass.ds(i, 1), :], pj[0][:, 0:FX_HEADS].unsqueeze(1)).then_inc(taken[4], 1)

            pipeline(dve, step)
            dve.drain()
            dve.tensor_tensor(forget[:], forget[:], again(bias[:], TILES), ALU.add)
            dve.drain()
            dve.tensor_scalar(fa[:], forget[:], -1.0, None, ALU.mult)
            dve.drain()
            dve.tensor_tensor(fe[:], forget[:], fa[:], ALU.max).then_inc(forget_ready, 1)
            dve.tensor_scalar(fa[:], fa[:], 0.0, None, ALU.max)
            dve.drain()
            dve.wait_ge(ln_ready, 1)
            dve.tensor_tensor(forget[:], fa[:], fe[:], ALU.add).then_inc(soft_ready, 1)
            dve.wait_ge(forget_turned, 1)
            for n in range(4):
                dve.tensor_copy(lf[:, n * BANK:(n + 1) * BANK], tf[n][0:FX_HEADS, :])
            dve.drain()
            dve.tensor_tensor_scan(cum[:], ones[:], lf[:], 0.0, ALU.mult, ALU.add)
            dve.drain()
            for n in range(3):
                last = dve.tensor_copy(part[n][:], cum[:])
                dve.drain()
                if n < 2:
                    dve.tensor_tensor(cum[:], cum[:], part[n][:], ALU.subtract)
                    dve.drain()
            last.then_inc(parts_ready, 1)


GROUPS = 4
LAG = 3
UNITS = 2 * FX_HEADS


def forgetting_attention(nc, x, w_out, final_g, masks, keysT, values, cum3, queries, gates, mixed, x_out):
    with ExitStack() as ctx:
        s = Stage(nc, ctx, "fa")
        sb, sem = s.sb, s.sem
        wo = sb("wo", [P, KC, D])
        ident = sb("ident", [P, P])
        ident16 = sb("ident16", [P, P], BF16)
        causal = sb("causal", [P, GROUPS, BANK], BF16)
        pick = sb("pick", [P, FX_HEADS, P], BF16)
        gain = sb("gain", [P, D])
        power = sb("power", [P, 1])
        qT = [sb(f"qT{p}", [P, FX_HEADS, P]) for p in range(2)]
        gate2 = [sb(f"gate2{p}", [P, FX]) for p in range(2)]
        rw = [sb(f"rw{p}", [P, FX]) for p in range(2)]
        xres = [sb(f"xres{p}", [P, D]) for p in range(2)]
        sm = [sb(f"sm{n}", [P, GROUPS * BANK]) for n in range(4)]
        tops, spare = ([sb(f"{name}{n}", [P, GROUPS]) for n in range(4)] for name in ("tops", "spare"))
        negtop = [sb(f"negtop{n}", [P, 1]) for n in range(4)]
        total = [sb(f"total{p}", [P, FX_HEADS]) for p in range(2)]
        rden = sb("rden", [P, FX_HEADS])
        pT = [sb(f"pT{n}", [P, 4, P]) for n in range(2)]
        o = sb("o", [P, FX])
        mixb = sb("mixb", [P, FX])
        mixT = sb("mixT", [P, KC, P])
        z = sb("z", [P, D])
        sq_sum, ms, rms = sb("sq_sum", [P, 1]), sb("ms", [P, 1]), sb("rms", [P, 1])
        y = [sb(f"y{p}", [P, D]) for p in range(2)]
        sc = [s.bank(f"sc{n}") for n in range(2)]
        tp = [s.bank(f"tp{n}") for n in range(2)]
        ov = [s.bank(f"ov{n}") for n in range(2)]
        out = [s.bank(f"out{n}") for n in range(2)]

        consts_in, w_here, set_up, set_up_pool = sem("consts_in"), sem("w_here"), sem("set_up"), sem("set_up_pool")
        q_here, here, stored = ([sem(f"{n}{p}") for p in range(2)] for n in ("q_here", "here", "stored"))
        (scored, topped, neg_ready, p_ready, p_turned, weighed, o_ready) = (sem(n) for n in (
            "scored", "topped", "neg_ready", "p_ready", "p_turned", "weighed", "o_ready"))
        pT_ready = [sem(f"pT_ready{n}") for n in range(2)]
        mix_turned, mixT_ready, out_done, z_ready, squared, ms_ready, rms_ready, y_ready = (sem(n) for n in (
            "mix_turned", "mixT_ready", "out_done", "z_ready", "squared", "ms_ready", "rms_ready", "y_ready"))
        block = s.block()
        CONSTS = 4

        class At:

            def __init__(self, g, j):
                self.g, self.j, self.n = g, j, g + 1
                self.pair = 2 * g + j

            def unit(self, u):
                return UNITS * self.pair + u

            def chunk(self, u, c):
                return UNITS * self.g * (self.g + 1) + UNITS * self.n * self.j + self.n * u + c

            def tile(self, p):
                return 2 * self.pair + p

            def blocks(self, u, c):
                return 3 if u < FX_HEADS and c == self.n - 1 else 4

            def keys(self, u):
                return (self.n - 1) * BANK + self.blocks(u, self.n - 1) * P

        def pairs(eng, body):
            for j in range(2):
                body(At(0, j))
            for g in range(1, GROUPS):
                with eng.Fori(0, 2) as j:
                    body(At(g, j))

        def stores_before(t, p):
            return 8 * (t - p)

        def idle(at, u, c):
            pass

        def slots(at, ahead, late, finish):
            for u in range(UNITS + LAG):
                if u >= UNITS:
                    finish(at.tile(0), 0, u - UNITS + 1)
                for c in range(at.n):
                    if u < UNITS:
                        ahead(at, u, c)
                    if u >= LAG:
                        late(at, u - LAG, c)
                if LAG - 2 <= u < LAG + 2 and not (isinstance(at.pair, int) and at.pair == 0):
                    finish(at.tile(0) - 1, 1, u - LAG + 2)
                if u == UNITS - 1:
                    finish(at.tile(0), 0, 0)

        def turned_before(at, u, c):
            whole = UNITS // 2 * at.g * (at.g + 1) + UNITS // 2 * at.n * at.j
            return whole + (at.n * u + c) // 2

        @block.sync
        def _(sp):
            def load_q(t, p):
                rows = bass.ds(t * P, P)
                for half in range(2):
                    part = slice(half * FX_DIM, (half + 1) * FX_DIM)
                    dst = qT[p][part].rearrange("p (a b) t -> p a b t", b=2)[:, :, half, :]
                    sp.dma_start(dst, queries[rows, :].rearrange("p (a t) -> p a t", a=4)[part]).then_inc(q_here[p], 16)

            def load(t, p):
                rows = bass.ds(t * P, P)
                for dst, src in ((gate2[p][:], gates[rows, :]), (rw[p][:], mixed[rows, 0:FX]), (xres[p][:], x[rows, :])):
                    sp.dma_start(dst, src).then_inc(here[p], 16)

            sp.dma_start(ident[:], masks["ident"]).then_inc(consts_in, 16)
            for n, src in enumerate((masks["causal4"], masks["pick"])):
                sp.dma_start(sm[n][:, 0:src.shape[1] * src.shape[2]], src.rearrange("p a b -> p (a b)")).then_inc(consts_in, 16)
            sp.dma_start(gain[:], row(final_g, 0, D)).then_inc(consts_in, 16)
            sp.wait_ge(set_up_pool, 1)
            for p in range(2):
                load_q(p, p)
            for p in range(2):
                load(p, p)
            for kc in range(KC):
                sp.dma_start(wo[:, kc, :], w_out[kc * P:(kc + 1) * P, :]).then_inc(w_here, 16)

            def finished(t, p):
                sp.wait_ge(y_ready, t + 1)
                sp.dma_start(x_out[bass.ds(t * P, P), :], y[p][:]).then_inc(stored[p], 16)
                if t + 2 < TILES:
                    load(t + 2, p)

            for at in (At(g, j) for g in range(GROUPS) for j in range(2)):
                if at.pair > 0:
                    finished(at.tile(0) - 1, 1)
                if at.tile(2) < TILES:
                    for p in range(2):
                        sp.wait_ge(scored, at.chunk(FX_HEADS * (p + 1), 0))
                        load_q(at.tile(2 + p), p)
                finished(at.tile(0), 0)
            finished(TILES - 1, 1)
            for p in range(2):
                sp.wait_ge(stored[p], 16 * TILES // 2)

        @block.tensor
        def _(pe):
            pe.wait_ge(consts_in, 16 * CONSTS)
            pe.wait_ge(set_up, 1)

            def score(at, u, c):
                p, h = divmod(u, FX_HEADS)
                if h == 0 and c == 0:
                    pe.wait_ge(q_here[p], 32 * (at.pair + 1))
                if at.n * u + c >= 2:
                    pe.wait_ge(topped, at.chunk(u, c) - 1)
                width = at.blocks(u, c) * P
                bank = sc[(at.n * u + c) % 2][:, 0:width]
                keys = slice(c * BANK, c * BANK + width)
                pe.matmul(bank, pick[:, h, :], cum3[:, keys], start=True, stop=False)
                if c == at.n - 1:
                    pe.matmul(bank, ident16[:], causal[:, bass.ds(2 * at.j + p, 1), 0:width].rearrange("q a k -> q (a k)"), start=False, stop=False)
                pe.matmul(bank, qT[p][:, h, :], keysT[:, h // 2, keys], start=False, stop=True).then_inc(scored, 1)

            def weigh(at, u, c):
                if c == 0:
                    pe.wait_ge(p_ready, at.unit(u) + 1)
                k = (at.n * u + c) % 2
                need(pe, pT_ready[k], turned_before(at, u, c))
                for m in range(at.blocks(u, c)):
                    last = pe.transpose(tp[k][:, m * P:(m + 1) * P], sm[u % 4][:, (4 * c + m) * P:(4 * c + m + 1) * P], ident[:])
                last.then_inc(p_turned, 1)
                if at.n * u + c > 0:
                    apply(at, *divmod(at.n * u + c - 1, at.n))
                if u == UNITS - 1 and c == at.n - 1:
                    apply(at, u, c)

            def apply(at, u, c):
                p, h = divmod(u, FX_HEADS)
                k = (at.n * u + c) % 2
                pe.wait_ge(pT_ready[k], turned_before(at, u, c) + 1)
                blocks = at.blocks(u, c)
                for m in range(blocks):
                    last = pe.matmul(ov[p][:, h * FX_DIM:(h + 1) * FX_DIM], pT[k][:, m, :],
                                     values[:, 4 * c + m, h * FX_DIM:(h + 1) * FX_DIM], start=c == 0 and m == 0, stop=c == at.n - 1 and m == blocks - 1)
                if c == at.n - 1:
                    last.then_inc(weighed, 1)

            def finish(t, p, part):
                if part == 0:
                    pe.wait_ge(o_ready, t + 1)
                    need(pe, z_ready, 2 * t)
                    for g, src in ((0, rw[p]), (1, mixb)):
                        for m in range(4):
                            last = pe.transpose(out[g][:, m * P:(m + 1) * P], src[:, m * P:(m + 1) * P], ident[:])
                        last.then_inc(mix_turned, 1)
                if part == 1:
                    pe.wait_ge(w_here, 16 * KC)
                    pe.wait_ge(mixT_ready, 2 * t + 2)
                    for c in range(2):
                        for kc in range(KC):
                            last = pe.matmul(out[c][:], mixT[:, kc, :], wo[:, kc, c * BANK:(c + 1) * BANK], start=kc == 0, stop=kc == KC - 1)
                        last.then_inc(out_done, 1)

            pairs(pe, lambda at: slots(at, score, weigh, finish))
            for part in range(4):
                finish(TILES - 1, 1, part)

        @block.scalar
        def _(act):
            def soft(at, u, c):
                if c == at.n - 1:
                    act.wait_ge(neg_ready, at.unit(u) + 1)
                    p, h = divmod(u, FX_HEADS)
                    view = sm[u % 4][:, 0:at.keys(u)]
                    act.activation(view, view, ACT.Exp, bias=negtop[u % 4][:], accum_out=total[p][:, h:h + 1]).then_inc(p_ready, 1)

            def finish(t, p, part):
                if part == 0:
                    for g in range(2):
                        act.wait_ge(mix_turned, 2 * t + g + 1)
                        act.copy(mixT[:, 4 * g:4 * g + 4, :], heads(out[g][:], 4)).then_inc(mixT_ready, 1)
                if part == 2:
                    act.wait_ge(z_ready, 2 * t + 2)
                    need(act, stored[p], stores_before(t, p))
                    act.activation(y[p][:], z[:], ACT.Square, accum_out=sq_sum[:]).then_inc(squared, 1)

            pairs(act, lambda at: slots(at, soft, idle, finish))
            for part in range(4):
                finish(TILES - 1, 1, part)

        @block.gpsimd
        def _(pool):
            pool.memset(power[:], -0.5)
            for p in range(2):
                pool.memset(qT[p][:], 0.0)
            pool.drain()
            pool.memset(rms[:], 0.0).then_inc(set_up_pool, 1)

            def finish(t, p, part):
                if part == 2:
                    pool.wait_ge(ms_ready, t + 1)
                    pool.tensor_tensor(rms[:], ms[:], power[:], ALU.pow).then_inc(rms_ready, 1)

            pairs(pool, lambda at: slots(at, idle, idle, finish))
            finish(TILES - 1, 1, 2)

        @block.vector
        def _(dve):
            dve.wait_ge(consts_in, 16 * CONSTS)
            dve.tensor_copy(ident16[:], ident[:])
            dve.tensor_copy(causal[:].rearrange("p a b -> p (a b)"), sm[0][:])
            dve.tensor_copy(pick[:].rearrange("p a b -> p (a b)"), sm[1][:, 0:FX_HEADS * P]).then_inc(set_up, 1)
            dve.wait_ge(set_up_pool, 1)
            dve.drain()

            def top(at, u, c):
                if u >= 4 and c == 0:
                    dve.wait_ge(p_turned, at.chunk(u - 3, 0))
                dve.wait_ge(scored, at.chunk(u, c) + 1)
                width = at.blocks(u, c) * P
                dst, bank = sm[u % 4][:, c * BANK:c * BANK + width], sc[(at.n * u + c) % 2][:, 0:width]
                dve.tensor_scalar(dst, bank, 0.0, NEG, ALU.add, ALU.max, accum_out=tops[u % 4][:, c:c + 1]).then_inc(topped, 1)
                if c == at.n - 1:
                    dve.drain()
                    dve.tensor_scalar(spare[u % 4][:, 0:at.n], tops[u % 4][:, 0:at.n], -1.0, -NEG, ALU.mult, ALU.min, accum_out=negtop[u % 4][:]).then_inc(neg_ready, 1)

            def take_p(at, u, c):
                k = (at.n * u + c) % 2
                dve.wait_ge(p_turned, at.chunk(u, c) + 1)
                width = at.blocks(u, c)
                dve.tensor_copy(pT[k][:, 0:width, :], heads(tp[k][:], 4)[:, 0:width, :]).then_inc(pT_ready[k], 1)
                if u == FX_HEADS and c == 0:
                    mix(at, 0)
                if u == UNITS - 1 and c == at.n - 1:
                    mix(at, 1)

            def mix(at, p):
                if p == 0:
                    dve.wait_ge(here[0], 48 * (at.pair + 1))
                else:
                    dve.wait_ge(here[1], 48 * (at.pair + 1))
                dve.wait_ge(p_ready, at.unit(FX_HEADS * (p + 1)))
                dve.reciprocal(rden[:], total[p][:])
                dve.drain()
                dve.wait_ge(weighed, at.unit(FX_HEADS * (p + 1)))
                dve.tensor_tensor(heads(o[:], FX_HEADS), heads(ov[p][:], FX_HEADS), spread(rden[:], FX_DIM), ALU.mult)
                dve.drain()
                dve.scalar_tensor_tensor(mixb[:], o[:], 0.5, gate2[p][:], ALU.mult, ALU.mult).then_inc(o_ready, 1)

            def finish(t, p, part):
                if part == 1:
                    for c in range(2):
                        dve.wait_ge(out_done, 2 * t + c + 1)
                        cols = slice(c * BANK, (c + 1) * BANK)
                        dve.tensor_tensor(z[:, cols], xres[p][:, cols], out[c][:], ALU.add).then_inc(z_ready, 1)
                if part == 2:
                    dve.wait_ge(squared, t + 1)
                    dve.tensor_scalar(ms[:], sq_sum[:], 1.0 / D, 1e-6, ALU.mult, ALU.add).then_inc(ms_ready, 1)
                if part == 3:
                    dve.wait_ge(rms_ready, t + 1)
                    dve.scalar_tensor_tensor(y[p][:], z[:], rms[:], gain[:], ALU.mult, ALU.mult).then_inc(y_ready, 1)

            pairs(dve, lambda at: slots(at, top, take_p, finish))
            for part in range(4):
                finish(TILES - 1, 1, part)


BR = 256
A_COL, P_COL = 0, 1808
POOLS = 4
POOL_DIM = 64
A_TAPS = 3


def short_mixers(nc, x, norm_w, w_in, conv_w, pool_w, pool_scale, masks, mixed):
    with ExitStack() as ctx:
        s = Stage(nc, ctx, "sh")
        sb, sem = s.sb, s.sem
        w = sb("w", [P, KC, 6 * BR])
        ident = sb("ident", [P, P])
        gains, gainT = sb("gains", [KC, P]), sb("gainT", [P, KC])
        taps = sb("taps", [P, A_TAPS, BR])
        scale = sb("scale", [P, BR])
        pw = sb("pw", [P, 2, POOL_DIM])
        window = sb("window", [P, POOLS, P])
        window_later = sb("window_later", [P, POOLS, P])
        window_prev = sb("window_prev", [P, POOLS, P])
        tmp_c = sb("tmp_c", [P, BR])
        tanh = sb("tanh", [P, 2, BR])
        U = [sb(f"U{p}", [P, BR]) for p in range(2)]
        back = [sb(f"back{n}", [P, BR]) for n in range(1, A_TAPS)]
        GB = [sb(f"GB{p}", [P, BR]) for p in range(2)]
        PU = [sb(f"PU{p}", [P, BR]) for p in range(2)]
        PG = [sb(f"PG{p}", [P, BR]) for p in range(2)]
        pu_prev = sb("pu_prev", [P, BR])
        zeros4 = sb("zeros4", [P, POOLS, P])
        part = [sb(f"part{n}", [P, BR]) for n in range(A_TAPS)]
        pooledT = sb("pooledT", [P, 2, P])
        out = [sb(f"out{p}", [P, 2 * BR]) for p in range(2)]
        pj = [s.bank(f"pj{n}") for n in range(2)]
        pooled = s.bank("pooled")
        mx = [s.bank(f"mx{n}") for n in range(2)]
        tg = s.bank("tg")
        front = Normed(s, x, ident, [pj[1], pj[0]])

        CONSTS = 12
        consts_in, w_here, set_up, scaled_w, gain_turned = (sem(n) for n in ("consts_in", "w_here", "set_up", "scaled_w", "gain_turned"))
        chunk_ready, c_ready, tanh_b, b_free = (sem(n) for n in ("chunk_ready", "c_ready", "tanh_b", "b_free"))
        tanh_p, u_taken = sem("tanh_p"), sem("u_taken")
        taken = [sem(f"taken{c}") for c in range(3)]
        shifted, stored = ([sem(f"{n}{p}") for p in range(2)] for n in ("shifted", "stored"))
        conved, pool_done, pooledT_ready, mx_done, prev_kept, out_ready = (sem(n) for n in (
            "conved", "pool_done", "pooledT_ready", "mx_done", "prev_kept", "out_ready"))
        block = s.block()

        def shift_count(ht, pt):
            return 64 * ht + (32 if pt == 0 else 64)

        @block.sync
        def _(sp):
            small = [(ident[:], masks["ident"]), (gains[:], by_chunk(norm_w)), (scale[:], row(pool_scale, 0, BR)),
                     (window[:], masks["window_first"]), (window_later[:], masks["window"]), (window_prev[:], masks["window_prev"]),
                     (back[0][0:1, :], masks["zeros"][:, 0:BR]), (back[1][0:2, :], masks["zeros"][:, 0:2 * BR].rearrange("a (b c) -> (a b) c", b=2)),
                     (pw[:], pool_w.rearrange("(q o) c d -> (o c) q d", q=2))]
            small += [(taps[:, n, :], conv_w[n:n + 1, :].to_broadcast([P, BR])) for n in range(A_TAPS)]
            assert len(small) == CONSTS
            for dst, src in small:
                sp.dma_start(dst, src).then_inc(consts_in, 16)
            for kc in range(KC):
                r = slice(kc * P, (kc + 1) * P)
                for n, col in enumerate((A_COL, A_COL + 2 * BR, A_COL + BR, A_COL + 3 * BR, P_COL, P_COL + BR)):
                    sp.dma_start(w[:, kc, n * BR:(n + 1) * BR], w_in[r, col:col + BR]).then_inc(w_here, 16)
            front.load(sp, 0)
            sp.wait_ge(consts_in, 16 * CONSTS)

            def shift(i, pi, first):
                if not first:
                    sp.wait_ge(conved, i)
                sp.wait_ge(taken[0], i + 1)
                for n in range(1, A_TAPS):
                    if not first:
                        sp.dma_start(back[n - 1][0:n, :], U[1 - pi][P - n:P, :]).then_inc(shifted[pi], 16)
                    sp.dma_start(back[n - 1][n:P, :], U[pi][0:P - n, :]).then_inc(shifted[pi], 16)

            def step(i, hi, pi, t, ht, pt):
                if i is not None:
                    if not (isinstance(i, int) and i == TILES - 1):
                        front.load(sp, i + 1)
                    shift(i, pi, t is None)
                if t is not None:
                    rows = rows_of(sp, t)
                    sp.wait_ge(out_ready, t + 1)
                    sp.dma_start(mixed[rows, 0:2 * BR], out[pt][:]).then_inc(stored[pt], 16)

            pipeline(sp, step)
            for p in range(2):
                sp.wait_ge(stored[p], 16 * TILES // 2)

        @block.tensor
        def _(pe):
            pe.wait_ge(consts_in, 16 * CONSTS)
            pe.transpose(tg[:, 0:KC], gains[:], ident[0:KC, 0:KC]).then_inc(gain_turned, 1)
            pe.wait_ge(scaled_w, KC)

            def project(i, c):
                if c == 0:
                    pe.wait_ge(front.ready, 2 * i + 2)
                if c == 2:
                    pe.wait_ge(taken[0], i + 1)
                for kc in range(KC):
                    last = pe.matmul(pj[c % 2][:], front.hT[:, kc, :], w[:, kc, c * BANK:(c + 1) * BANK], start=kc == 0, stop=kc == KC - 1)
                last.then_inc(chunk_ready, 1)

            def pool_windows(t, pt):
                pe.wait_ge(u_taken, t + 1)
                pe.wait_ge(prev_kept, t + 1)
                for g in range(POOLS):
                    o, q = g % 2, g // 2
                    dst = pooled[o * POOL_DIM:(o + 1) * POOL_DIM, q * P:(q + 1) * P]
                    cols = slice(g * POOL_DIM, (g + 1) * POOL_DIM)
                    pe.matmul(dst, PU[pt][:, cols], window[:, g, :], start=True, stop=False)
                    last = pe.matmul(dst, pu_prev[:, cols], window_prev[:, g, :], start=False, stop=True)
                last.then_inc(pool_done, 1)

            def mix_pools(t):
                pe.wait_ge(pooledT_ready, t + 1)
                need(pe, out_ready, t)
                for q in range(2):
                    for o in range(2):
                        half = slice(o * POOL_DIM, (o + 1) * POOL_DIM)
                        last = pe.matmul(mx[o][:, q * POOL_DIM:(q + 1) * POOL_DIM], pooledT[half, q, :], pw[half, q, :], start=True, stop=True)
                last.then_inc(mx_done, 1)

            def step(i, hi, pi, t, ht, pt):
                pr, m = i is not None, t is not None
                if m:
                    pool_windows(t, pt)
                if pr:
                    front.turn(pe, i, (taken[1], taken[2]))
                    project(i, 0)
                if m:
                    mix_pools(t)
                if pr:
                    project(i, 1)
                    project(i, 2)

            pipeline(pe, step)

        @block.scalar
        def _(act):
            act.wait_ge(set_up, 1)
            front.square(act, 0)

            def step(i, hi, pi, t, ht, pt):
                pr, m = i is not None, t is not None
                if m:
                    act.wait_ge(pool_done, t + 1)
                    act.copy(pooledT[:], pooled[:, 0:2 * P].rearrange("p (q t) -> p q t", q=2)).then_inc(pooledT_ready, 1)
                if pr:
                    front.take(act, i)
                    act.wait_ge(chunk_ready, 3 * i + 1)
                    need(act, taken[0], i)
                    act.copy(tmp_c[:], pj[0][:, BR:]).then_inc(c_ready, 1)
                    if not (isinstance(i, int) and i == TILES - 1):
                        front.square(act, i + 1)
                    act.wait_ge(chunk_ready, 3 * i + 2)
                    need(act, taken[1], i)
                    act.activation(tanh[:, 0, :], pj[1][:, BR:], ACT.Tanh, scale=0.5).then_inc(tanh_b, 1)
                    act.wait_ge(chunk_ready, 3 * i + 3)
                    act.copy(PU[pi][:], pj[0][:, 0:BR]).then_inc(u_taken, 1)
                    need(act, taken[2], i)
                    act.activation(tanh[:, 1, :], pj[0][:, BR:], ACT.Tanh, scale=0.5).then_inc(tanh_p, 1)

            pipeline(act, step)

        @block.gpsimd
        def _(pool):
            pool.memset(front.power[:], -0.5)
            pool.drain()
            pool.memset(pu_prev[:], 0.0).then_inc(set_up, 1)
            pool.wait_ge(consts_in, 16 * CONSTS)
            front.root(pool, 0)

            def step(i, hi, pi, t, ht, pt):
                if i is not None and not (isinstance(i, int) and i == TILES - 1):
                    front.root(pool, i + 1)
                if t is not None:
                    pool.wait_ge(pool_done, t + 1)
                    if pt == 0:
                        pool.tensor_tensor(window[:], window_later[:], zeros4[:], ALU.add)
                    pool.tensor_tensor(pu_prev[:], PU[pt][:], zeros4[:, 0:2, :].rearrange("p a b -> p (a b)"), ALU.add).then_inc(prev_kept, 1)

            pool.memset(zeros4[:], 0.0)
            pool.drain()
            pool.memset(pu_prev[:], 0.0).then_inc(prev_kept, 1)
            pipeline(pool, step)

        @block.vector
        def _(dve):
            dve.wait_ge(consts_in, 16 * CONSTS)
            dve.wait_ge(set_up, 1)
            dve.wait_ge(gain_turned, 1)
            dve.tensor_copy(gainT[:], tg[:, 0:KC])
            dve.tensor_scalar(scale[:], scale[:], 0.5, None, ALU.mult)
            dve.tensor_scalar(taps[:], taps[:], 0.5, None, ALU.mult)
            dve.wait_ge(w_here, 16 * 6 * KC)
            dve.drain()
            for kc in range(KC):
                dve.tensor_scalar(w[:, kc, :], w[:, kc, :], gainT[:, kc:kc + 1], None, ALU.mult).then_inc(scaled_w, 1)
            front.mean(dve, 0)
            front.scale(dve, 0)

            def step(i, hi, pi, t, ht, pt):
                pr, m = i is not None, t is not None
                if m:
                    dve.wait_ge(shifted[pt], shift_count(ht, pt))
                    for n in range(A_TAPS):
                        src = U[pt] if n == 0 else back[n - 1]
                        last = dve.tensor_tensor(part[n][:], src[:], taps[:, A_TAPS - 1 - n, :], ALU.mult)
                    last.then_inc(conved, 1)
                    dve.drain()
                    dve.tensor_tensor(part[0][:], part[0][:], part[1][:], ALU.add)
                    dve.drain()
                    dve.tensor_tensor(part[0][:], part[0][:], part[2][:], ALU.add)
                    dve.drain()
                    need(dve, stored[pt], 16 * ht)
                    dve.tensor_tensor(out[pt][:, 0:BR], part[0][:], GB[pt][:], ALU.mult)
                if pr:
                    dve.wait_ge(c_ready, i + 1)
                    dve.tensor_tensor(U[pi][:], pj[0][:, 0:BR], tmp_c[:], ALU.mult).then_inc(taken[0], 1)
                if m:
                    dve.wait_ge(mx_done, t + 1)
                    four = lambda ap: ap.rearrange("p (q o d) -> p q o d", q=2, o=2)
                    for o in range(2):
                        last = dve.tensor_tensor(four(out[pt][:, BR:])[:, :, o, :], mx[o][:, 0:2 * POOL_DIM].rearrange("p (q d) -> p q d", q=2),
                                                 four(PG[pt][:])[:, :, o, :], ALU.mult)
                    last.then_inc(out_ready, 1)
                if pr:
                    if not (isinstance(i, int) and i == TILES - 1):
                        front.mean(dve, i + 1)
                        front.scale(dve, i + 1)
                    dve.wait_ge(tanh_b, i + 1)
                    dve.scalar_tensor_tensor(GB[pi][:], tanh[:, 0, :], 1.0, pj[1][:, BR:], ALU.add, ALU.mult)
                    dve.drain()
                    dve.tensor_tensor(GB[pi][:], GB[pi][:], pj[1][:, 0:BR], ALU.mult).then_inc(taken[1], 1)
                    dve.wait_ge(tanh_p, i + 1)
                    dve.scalar_tensor_tensor(PG[pi][:], tanh[:, 1, :], 1.0, pj[0][:, BR:], ALU.add, ALU.mult).then_inc(taken[2], 1)
                    dve.drain()
                    dve.tensor_tensor(PG[pi][:], PG[pi][:], scale[:], ALU.mult)

            pipeline(dve, step)


GLA_K = 128
GLA_HEADS, GLA_V = 4, 64
RANK = 16
SSD_HEADS, SSD_DIM = 4, 64
XBC = 3 * BR
TAPS = 4
LOGS = GLA_K + SSD_HEADS
WIDE = XBC + RANK + SSD_HEADS
QKV_COL, LR_COL, GZ_COL, SZ_COL, XBC_COL, DT_COL = 1024, 1536, 1552, 2320, 2576, 3344


def recurrences(nc, x, norm_w, w_in, par, w_out, masks, mixed, x_out):
    with ExitStack() as ctx:
        s = Stage(nc, ctx, "rc")
        sb, sem = s.sb, s.sem
        w = sb("w", [P, KC, 2 * BANK + WIDE])
        COLS = [(0, BANK), (BANK, 2 * BANK), (2 * BANK, 3 * BANK), (3 * BANK, 2 * BANK + WIDE)]
        wo = sb("wo", [P, KC, D])
        ident = sb("ident", [P, P])
        gains, gainT = sb("gains", [KC, P]), sb("gainT", [P, KC])
        after, halves = sb("after", [P, P]), sb("halves", [P, 2])
        chunk_ones = sb("chunk_ones", [P, 2, P])
        state_mask = sb("state_mask", [P, BANK])
        taps, conv_b = sb("taps", [P, TAPS, XBC]), sb("conv_b", [P, XBC])
        gate_w, gate_b = sb("gate_w", [RANK, GLA_K]), sb("gate_b", [P, GLA_K])
        dt_bias, rate, skip = sb("dt_bias", [P, SSD_HEADS]), sb("rate", [P, LOGS]), sb("skip", [P, SSD_HEADS])
        gla_norm, ssd_norm, gain = sb("gla_norm", [P, GLA_V]), sb("ssd_norm", [P, BR]), sb("gain", [P, D])
        power = sb("power", [P, GLA_HEADS + 1])
        QKV = [sb(f"QKV{p}", [P, BANK]) for p in range(2)]
        tanh = sb("tanh", [P, BANK])
        G2 = [sb(f"G2{p}", [P, BANK]) for p in range(2)]
        XB = [sb(f"XB{p}", [P, WIDE]) for p in range(2)]
        back = [sb(f"back{n}", [P, XBC]) for n in range(1, TAPS)]
        conv = sb("conv", [P, XBC])
        prod = sb("prod", [P, XBC])
        th = sb("th", [P, XBC])
        qT = sb("qT", [P, P])
        lrT = sb("lrT", [RANK, P])
        CT = sb("CT", [P, 2, P])
        la, neg, mag, soft = (sb(n, [P, LOGS]) for n in ("la", "neg", "mag", "soft"))
        e_rest = sb("e_rest", [P, LOGS])
        e_tot = sb("e_tot", [P, 2 + 2 * SSD_HEADS])
        kd, wx, wgt = sb("kd", [P, GLA_K]), sb("wx", [P, BR]), sb("wgt", [P, SSD_HEADS])
        upd = sb("upd", [P, BANK])
        S = [sb(f"S{c}", [P, BANK]) for c in range(2)]
        o, sq = sb("o", [P, BANK]), sb("sq", [P, BANK])
        ms, rms = sb("ms", [P, GLA_HEADS + 1]), sb("rms", [P, GLA_HEADS + 1])
        mix = sb("mix", [P, BANK])
        ac = [sb(f"ac{p}", [P, BANK]) for p in range(2)]
        xres = [sb(f"xres{p}", [P, D]) for p in range(2)]
        mixT = sb("mixT", [P, KC, P])
        z = sb("z", [P, D])
        zs, zm, zr = sb("zs", [P, 1]), sb("zm", [P, 1]), sb("zr", [P, 1])
        y = sb("y", [P, D])
        pj = [s.bank(f"pj{n}") for n in range(2)]
        B = [s.bank(f"b{n}") for n in range(6)]
        front = Normed(s, x, ident, [pj[0], pj[1]])

        consts_in, w_here, wo_here, set_up, scaled_w, gain_turned = (sem(n) for n in ("consts_in", "w_here", "wo_here", "set_up", "scaled_w", "gain_turned"))
        chunk_ready, tanh_ready, rate_ready = sem("chunk_ready"), sem("tanh_ready"), sem("rate_ready")
        taken = [sem(f"taken{c}") for c in range(4)]
        shifted, here = ([sem(f"{n}{p}") for p in range(2)] for n in ("shifted", "here"))
        stored = sem("stored")
        (small_turned, small_ready, q_ready, logit_done, neg_ready, soft_in, exp_ready, ln_ready, la_ready, rest_done, rest_ready) = (sem(n) for n in (
            "small_turned", "small_ready", "q_ready", "logit_done", "neg_ready", "soft_in", "exp_ready", "ln_ready", "la_ready", "rest_done", "rest_ready"))
        conv_used, conv_ready, th_ready, xbc_ready, C_turned, CT_ready, wx_ready, upd_done, S_ready = (sem(n) for n in (
            "conv_used", "conv_ready", "th_ready", "xbc_ready", "C_turned", "CT_ready", "wx_ready", "upd_done", "S_ready"))
        o_done, o_ready, ms_ready, rms_ready, mix_ready, mix_turned, mixT_ready, out_done, z_ready = (sem(n) for n in (
            "o_done", "o_ready", "ms_ready", "rms_ready", "mix_ready", "mix_turned", "mixT_ready", "out_done", "z_ready"))
        squared, zm_ready, zr_ready, y_ready = (sem(n) for n in ("squared", "zm_ready", "zr_ready", "y_ready"))
        block = s.block()

        def shift_count(ht, pt):
            return 96 * ht + (48 if pt == 0 else 96)

        small = [(ident[:], masks["ident"]), (gains[:], by_chunk(norm_w)), (after[:], masks["chunk_after"]), (halves[:], masks["halves"]),
                 (chunk_ones[:], masks["chunk_ones"]), (state_mask[:], masks["state_mask"]), (conv_b[:], row(par["conv_b"], 0, XBC)),
                 (gate_w[:], par["gate_w"]), (gate_b[:], row(par["gate_b"], 0, GLA_K)), (dt_bias[:], row(par["dt_bias"], 0, SSD_HEADS)),
                 (rate[:, GLA_K:], row(par["a_log"], 0, SSD_HEADS)), (skip[:], row(par["d"], 0, SSD_HEADS)),
                 (gla_norm[:], row(par["gla_norm"], 0, GLA_V)), (ssd_norm[:], row(par["ssd_norm"], 0, BR)), (gain[:], row(par["final"], 0, D))]
        small += [(taps[:, n, :], par["conv_w"][n:n + 1, :].to_broadcast([P, XBC])) for n in range(TAPS)]
        small += [(back[n - 1][0:n, :], masks["zeros"][:, 0:n * XBC].rearrange("a (b c) -> (a b) c", b=n)) for n in range(1, TAPS)]
        CONSTS = len(small)

        @block.sync
        def _(sp):
            for dst, src in small:
                sp.dma_start(dst, src).then_inc(consts_in, 16)
            for kc in range(KC):
                r = slice(kc * P, (kc + 1) * P)
                for at, col, n in ((0, QKV_COL, BANK), (BANK, GZ_COL, BR), (BANK + BR, SZ_COL, BR), (2 * BANK, XBC_COL, XBC),
                                   (2 * BANK + XBC, LR_COL, RANK), (2 * BANK + XBC + RANK, DT_COL, SSD_HEADS)):
                    sp.dma_start(w[:, kc, at:at + n], w_in[r, col:col + n]).then_inc(w_here, 16)
            front.load(sp, 0)
            for kc, src in enumerate((0, 1, 4, 5, 2, 3, 6, 7)):
                sp.dma_start(wo[:, kc, :], w_out[src * P:(src + 1) * P, :]).then_inc(wo_here, 16)
            sp.wait_ge(consts_in, 16 * CONSTS)

            def shift(i, pi, first):
                sp.wait_ge(taken[2], i + 1)
                sp.wait_ge(taken[3], i + 1)
                if not first:
                    sp.wait_ge(conv_used, i)
                for n in range(1, TAPS):
                    if not first:
                        sp.dma_start(back[n - 1][0:n, :], XB[1 - pi][P - n:P, 0:XBC]).then_inc(shifted[pi], 16)
                    sp.dma_start(back[n - 1][n:P, :], XB[pi][0:P - n, 0:XBC]).then_inc(shifted[pi], 16)

            def step(i, hi, pi, t, ht, pt):
                if i is not None:
                    if not (isinstance(i, int) and i == TILES - 1):
                        front.load(sp, i + 1)
                    rows = rows_of(sp, i)
                    need(sp, z_ready, 2 * i - 2)
                    sp.dma_start(ac[pi][:], mixed[rows, 0:BANK]).then_inc(here[pi], 16)
                    sp.dma_start(xres[pi][:], x[rows, :]).then_inc(here[pi], 16)
                    shift(i, pi, t is None)
                if t is not None:
                    rows = rows_of(sp, t)
                    sp.wait_ge(y_ready, t + 1)
                    sp.dma_start(x_out[rows, :], y[:]).then_inc(stored, 16)

            pipeline(sp, step)
            sp.wait_ge(stored, 16 * TILES)

        @block.tensor
        def _(pe):
            pe.wait_ge(consts_in, 16 * CONSTS)
            pe.transpose(B[0][:, 0:KC], gains[:], ident[0:KC, 0:KC]).then_inc(gain_turned, 1)
            pe.wait_ge(scaled_w, KC)
            pe.wait_ge(wo_here, 16 * KC)

            def project(i, c):
                lo, hi = COLS[c]
                if c == 0:
                    pe.wait_ge(front.ready, 2 * i + 2)
                if c >= 2:
                    pe.wait_ge(taken[c - 2], i + 1)
                for kc in range(KC):
                    last = pe.matmul(pj[c % 2][:, 0:hi - lo], front.hT[:, kc, :], w[:, kc, lo:hi], start=kc == 0, stop=kc == KC - 1)
                last.then_inc(chunk_ready, 1)

            def turn_small(t, pt):
                pe.wait_ge(taken[0], t + 1)
                pe.wait_ge(taken[3], t + 1)
                need(pe, o_ready, t)
                pe.transpose(B[0][:, 0:P], QKV[pt][:, 0:GLA_K], ident[:])
                pe.transpose(B[0][0:RANK, P:2 * P], XB[pt][:, XBC:XBC + RANK], ident[:]).then_inc(small_turned, 1)

            def logits(t):
                pe.wait_ge(small_ready, t + 1)
                need(pe, mixT_ready, 2 * t)
                pe.matmul(B[1][:, 0:GLA_K], lrT[:], gate_w[:], start=True, stop=True).then_inc(logit_done, 1)

            def rest(t):
                pe.wait_ge(la_ready, t + 1)
                pe.matmul(B[2][:, 0:LOGS], after[:], la[:], start=True, stop=True)
                pe.matmul(B[2][:, LOGS:LOGS + 2], la[:, 0:GLA_K], halves[:], start=True, stop=True)
                for c in range(2):
                    at = LOGS + 2 + c * SSD_HEADS
                    last = pe.matmul(B[2][:, at:at + SSD_HEADS], chunk_ones[:, c, :], la[:, GLA_K:], start=True, stop=True)
                last.then_inc(rest_done, 1)

            def turn_C(t):
                pe.wait_ge(xbc_ready, t + 1)
                need(pe, z_ready, 2 * t)
                for g in range(2):
                    last = pe.transpose(B[3][:, g * P:(g + 1) * P], conv[:, 2 * BR + g * P:2 * BR + (g + 1) * P], ident[:])
                last.then_inc(C_turned, 1)

            def update(t, pt):
                pe.wait_ge(wx_ready, t + 1)
                need(pe, S_ready, 2 * t)
                need(pe, z_ready, 2 * t)
                for c in range(2):
                    r = slice(c * CHUNK, (c + 1) * CHUNK)
                    bank = B[4 + c]
                    pe.matmul(bank[:, 0:BR], kd[r, :], QKV[pt][r, 2 * GLA_K:], start=True, stop=True)
                    for g in range(2):
                        last = pe.matmul(bank[:, BR + g * P:BR + (g + 1) * P], conv[r, BR + g * P:BR + (g + 1) * P], wx[r, g * P:(g + 1) * P], start=True, stop=True)
                    last.then_inc(upd_done, 1)

            def read_out(t):
                pe.wait_ge(CT_ready, t + 1)
                pe.wait_ge(q_ready, t + 1)
                for c in range(2):
                    pe.wait_ge(S_ready, 2 * t + c + 1)
                    r = slice(c * CHUNK, (c + 1) * CHUNK)
                    pe.matmul(B[0][r, 0:BR], qT[:, r], S[c][:, 0:BR], start=True, stop=True)
                    for g in range(2):
                        last = pe.matmul(B[0][r, BR + g * P:BR + (g + 1) * P], CT[:, g, r], S[c][:, BR + g * P:BR + (g + 1) * P], start=True, stop=True)
                last.then_inc(o_done, 1)

            def turn_ac(t, ht, pt):
                pe.wait_ge(here[pt], 32 * (ht + 1))
                pe.wait_ge(neg_ready, t + 1)
                for m in range(4):
                    last = pe.transpose(B[1][:, m * P:(m + 1) * P], ac[pt][:, m * P:(m + 1) * P], ident[:])
                last.then_inc(mix_turned, 1)

            def turn_bd(t):
                pe.wait_ge(mix_ready, 2 * t + 2)
                for m in range(4):
                    last = pe.transpose(B[2][:, m * P:(m + 1) * P], mix[:, m * P:(m + 1) * P], ident[:])
                last.then_inc(mix_turned, 1)

            def project_out(t, half):
                pe.wait_ge(mixT_ready, 2 * t + half + 1)
                for c in range(2):
                    if half == 0:
                        pe.wait_ge((CT_ready, S_ready)[c], (t, 2 * t)[c] + 1)
                    for kc in range(4 * half, 4 * half + 4):
                        last = pe.matmul(B[3 + c][:], mixT[:, kc, :], wo[:, kc, c * BANK:(c + 1) * BANK], start=kc == 0, stop=kc == KC - 1)
                    if half:
                        last.then_inc(out_done, 1)

            def step(i, hi, pi, t, ht, pt):
                pr, m = i is not None, t is not None
                if m:
                    turn_small(t, pt)
                if pr:
                    front.turn(pe, i, (taken[2], taken[3]))
                if m:
                    logits(t)
                if pr:
                    project(i, 0)
                if m:
                    rest(t)
                    turn_ac(t, ht, pt)
                if pr:
                    project(i, 1)
                if m:
                    turn_C(t)
                    update(t, pt)
                if pr:
                    project(i, 2)
                if m:
                    read_out(t)
                    project_out(t, 0)
                if pr:
                    project(i, 3)
                if m:
                    turn_bd(t)
                    project_out(t, 1)

            pipeline(pe, step)

        @block.scalar
        def _(act):
            act.wait_ge(set_up, 1)
            front.square(act, 0)
            act.wait_ge(consts_in, 16 * CONSTS)
            act.activation(rate[:, GLA_K:], rate[:, GLA_K:], ACT.Exp).then_inc(rate_ready, 1)

            def step(i, hi, pi, t, ht, pt):
                pr, m = i is not None, t is not None
                if m:
                    act.wait_ge(small_turned, t + 1)
                    act.copy(lrT[:], B[0][0:RANK, P:2 * P]).then_inc(small_ready, 1)
                    act.copy(qT[:], B[0][:, 0:P]).then_inc(q_ready, 1)
                if pr:
                    front.take(act, i)
                if m:
                    act.wait_ge(soft_in, t + 1)
                    act.activation(mag[:], mag[:], ACT.Exp, scale=-1.0)
                    act.drain()
                    act.activation(mag[:], mag[:], ACT.Ln, bias=1.0).then_inc(ln_ready, 1)
                if pr:
                    act.wait_ge(chunk_ready, 4 * i + 1)
                    act.activation(QKV[pi][:, 0:GLA_K], pj[0][:, 0:GLA_K], ACT.Copy, scale=(GLA_K // GLA_HEADS) ** -0.5)
                    act.copy(QKV[pi][:, GLA_K:], pj[0][:, GLA_K:]).then_inc(taken[0], 1)
                if m:
                    act.wait_ge(rest_done, t + 1)
                    act.activation(e_rest[:], B[2][:, 0:LOGS], ACT.Exp)
                    act.activation(e_tot[:], B[2][:, LOGS:LOGS + 10], ACT.Exp).then_inc(rest_ready, 1)
                    act.wait_ge(mix_turned, 2 * t + 1)
                    need(act, out_done, 2 * t)
                    act.copy(mixT[:, 0:4, :], heads(B[1][:], 4)).then_inc(mixT_ready, 1)
                    act.wait_ge(conv_ready, t + 1)
                    act.activation(th[:], conv[:], ACT.Tanh).then_inc(th_ready, 1)
                if pr:
                    act.wait_ge(chunk_ready, 4 * i + 2)
                    need(act, taken[1], i)
                    act.activation(tanh[:], pj[1][:], ACT.Tanh, scale=0.5).then_inc(tanh_ready, 1)
                if m:
                    act.wait_ge(C_turned, t + 1)
                    act.copy(CT[:], B[3][:, 0:BR].rearrange("p (g t) -> p g t", g=2)).then_inc(CT_ready, 1)
                if pr:
                    act.wait_ge(chunk_ready, 4 * i + 3)
                    if t is not None:
                        act.wait_ge(shifted[pt], shift_count(ht, pt))
                    act.copy(XB[pi][:, 0:BANK], pj[0][:]).then_inc(taken[2], 1)
                    if not (isinstance(i, int) and i == TILES - 1):
                        front.square(act, i + 1)
                if m:
                    act.wait_ge(o_done, t + 1)
                    act.copy(o[:], B[0][:]).then_inc(o_ready, 1)
                if pr:
                    act.wait_ge(chunk_ready, 4 * i + 4)
                    act.copy(XB[pi][:, BANK:WIDE], pj[1][:, 0:WIDE - BANK]).then_inc(taken[3], 1)
                if m:
                    act.wait_ge(mix_turned, 2 * t + 2)
                    act.copy(mixT[:, 4:8, :], heads(B[2][:], 4)).then_inc(mixT_ready, 1)
                    act.wait_ge(z_ready, 2 * t + 2)
                    need(act, stored, 16 * t)
                    act.activation(y[:], z[:], ACT.Square, accum_out=zs[:]).then_inc(squared, 1)

            pipeline(act, step)

        @block.gpsimd
        def _(pool):
            pool.memset(power[:], -0.5)
            pool.memset(rate[:, 0:GLA_K], 1.0 / 16.0)
            pool.memset(S[1][:], 0.0)
            pool.memset(front.power[:], -0.5)
            pool.drain()
            pool.memset(rms[:], 0.0).then_inc(set_up, 1)
            front.root(pool, 0)

            def step(i, hi, pi, t, ht, pt):
                pr, m = i is not None, t is not None
                if pr and not (isinstance(i, int) and i == TILES - 1):
                    front.root(pool, i + 1)
                if m:
                    pool.wait_ge(ms_ready, t + 1)
                    pool.tensor_tensor(rms[:], ms[:], power[:], ALU.pow).then_inc(rms_ready, 1)
                    pool.wait_ge(zm_ready, t + 1)
                    pool.tensor_tensor(zr[:], zm[:], power[:, 0:1], ALU.pow).then_inc(zr_ready, 1)

            pipeline(pool, step)

        @block.vector
        def _(dve):
            dve.wait_ge(consts_in, 16 * CONSTS)
            dve.wait_ge(set_up, 1)
            dve.wait_ge(gain_turned, 1)
            dve.tensor_copy(gainT[:], B[0][:, 0:KC])
            dve.tensor_scalar(taps[:], taps[:], 0.5, None, ALU.mult)
            dve.tensor_scalar(conv_b[:], conv_b[:], 0.5, None, ALU.mult)
            dve.wait_ge(rate_ready, 1)
            dve.tensor_scalar(rate[:], rate[:], -1.0, None, ALU.mult)
            dve.wait_ge(w_here, 16 * 6 * KC)
            dve.drain()
            for kc in range(KC):
                dve.tensor_scalar(w[:, kc, :], w[:, kc, :], gainT[:, kc:kc + 1], None, ALU.mult).then_inc(scaled_w, 1)
            front.mean(dve, 0)
            front.scale(dve, 0)

            def softplus(t, pt):
                dve.wait_ge(logit_done, t + 1)
                dve.tensor_tensor(neg[:, 0:GLA_K], B[1][:, 0:GLA_K], gate_b[:], ALU.add).then_inc(neg_ready, 1)
                dve.tensor_tensor(neg[:, GLA_K:], XB[pt][:, XBC + RANK:WIDE], dt_bias[:], ALU.add)
                dve.drain()
                dve.tensor_scalar(neg[:, 0:GLA_K], neg[:, 0:GLA_K], -1.0, None, ALU.mult)
                dve.drain()
                dve.scalar_tensor_tensor(mag[:], neg[:], -1.0, neg[:], ALU.mult, ALU.max).then_inc(soft_in, 1)
                dve.wait_ge(ln_ready, t + 1)
                dve.scalar_tensor_tensor(soft[:], neg[:], 0.0, mag[:], ALU.max, ALU.add)
                dve.drain()
                dve.tensor_tensor(la[:], soft[:], rate[:], ALU.mult).then_inc(la_ready, 1)

            def convolve(t, ht, pt):
                dve.wait_ge(shifted[pt], shift_count(ht, pt))
                dve.tensor_tensor(conv[:], XB[pt][:, 0:XBC], taps[:, TAPS - 1, :], ALU.mult)
                dve.drain()
                dve.tensor_tensor(conv[:], conv[:], conv_b[:], ALU.add)
                for n in range(1, TAPS):
                    last = dve.tensor_tensor(prod[:], back[n - 1][:], taps[:, TAPS - 1 - n, :], ALU.mult)
                    if n == TAPS - 1:
                        last.then_inc(conv_used, 1)
                    dve.drain()
                    last = dve.tensor_tensor(conv[:], conv[:], prod[:], ALU.add)
                    if n < TAPS - 1:
                        dve.drain()
                last.then_inc(conv_ready, 1)

            def step(i, hi, pi, t, ht, pt):
                pr, m = i is not None, t is not None
                if m:
                    softplus(t, pt)
                    convolve(t, ht, pt)
                    dve.wait_ge(th_ready, t + 1)
                    dve.scalar_tensor_tensor(conv[:], th[:], 1.0, conv[:], ALU.add, ALU.mult).then_inc(xbc_ready, 1)
                    dve.drain()
                    dve.wait_ge(rest_ready, t + 1)
                    dve.tensor_tensor(wgt[:], e_rest[:, GLA_K:], soft[:, GLA_K:], ALU.mult)
                    dve.tensor_tensor(kd[:], QKV[pt][:, GLA_K:2 * GLA_K], e_rest[:, 0:GLA_K], ALU.mult)
                    dve.drain()
                    dve.tensor_tensor(heads(wx[:], 4), heads(conv[:, 0:BR], 4), spread(wgt[:], SSD_DIM), ALU.mult).then_inc(wx_ready, 1)
                if pr:
                    dve.wait_ge(tanh_ready, i + 1)
                    dve.scalar_tensor_tensor(G2[pi][:], tanh[:], 1.0, pj[1][:], ALU.add, ALU.mult).then_inc(taken[1], 1)
                if m:
                    for c in range(2):
                        dve.wait_ge(upd_done, 2 * t + c + 1)
                        dve.tensor_tensor(upd[:], B[4 + c][:], state_mask[:], ALU.mult)
                        src, dst = S[1 - c], S[c]
                        if c == 1:
                            need(dve, o_done, t)
                        dve.tensor_scalar(dst[:, 0:BR], src[:, 0:BR], e_tot[:, c:c + 1], None, ALU.mult)
                        dve.tensor_tensor(heads(dst[:, BR:], 4), heads(src[:, BR:], 4),
                                          spread(e_tot[:, 2 + 4 * c:6 + 4 * c], SSD_DIM), ALU.mult)
                        dve.drain()
                        dve.tensor_tensor(dst[:], dst[:], upd[:], ALU.add).then_inc(S_ready, 1)
                        dve.drain()
                if pr and not (isinstance(i, int) and i == TILES - 1):
                    front.mean(dve, i + 1)
                    front.scale(dve, i + 1)
                if m:
                    dve.tensor_tensor(heads(sq[:, BR:], 4), heads(conv[:, 0:BR], 4), spread(skip[:], SSD_DIM), ALU.mult)
                    dve.drain()
                    dve.wait_ge(o_ready, t + 1)
                    dve.tensor_tensor(o[:, BR:], o[:, BR:], sq[:, BR:], ALU.add)
                    dve.drain()
                    dve.scalar_tensor_tensor(o[:, BR:], o[:, BR:], 0.5, G2[pt][:, BR:], ALU.mult, ALU.mult)
                    dve.drain()
                    dve.tensor_tensor(sq[:], o[:], o[:], ALU.mult)
                    dve.drain()
                    dve.tensor_reduce(ms[:, 0:4], heads(sq[:, 0:BR], 4), AX, ALU.add)
                    dve.tensor_reduce(ms[:, 4:5], sq[:, BR:], AX, ALU.add)
                    dve.drain()
                    dve.tensor_scalar(ms[:, 0:4], ms[:, 0:4], 1.0 / GLA_V, 1e-6, ALU.mult, ALU.add)
                    dve.tensor_scalar(ms[:, 4:5], ms[:, 4:5], 1.0 / BR, 1e-6, ALU.mult, ALU.add)
                    dve.drain()
                    dve.tensor_copy(ms[:, 0:1], ms[:, 0:1]).then_inc(ms_ready, 1)
                    dve.wait_ge(rms_ready, t + 1)
                    dve.tensor_tensor(heads(o[:, 0:BR], 4), heads(o[:, 0:BR], 4), spread(rms[:, 0:4], GLA_V), ALU.mult)
                    dve.scalar_tensor_tensor(mix[:, BR:], o[:, BR:], rms[:, 4:5], ssd_norm[:], ALU.mult, ALU.mult).then_inc(mix_ready, 1)
                    dve.drain()
                    dve.tensor_tensor(heads(o[:, 0:BR], 4), heads(o[:, 0:BR], 4), again(gla_norm[:], 4), ALU.mult)
                    dve.drain()
                    dve.scalar_tensor_tensor(mix[:, 0:BR], o[:, 0:BR], 0.5, G2[pt][:, 0:BR], ALU.mult, ALU.mult).then_inc(mix_ready, 1)
                    dve.wait_ge(here[pt], 32 * (ht + 1))
                    for c in range(2):
                        dve.wait_ge(out_done, 2 * t + c + 1)
                        cols = slice(c * BANK, (c + 1) * BANK)
                        dve.tensor_tensor(z[:, cols], xres[pt][:, cols], B[3 + c][:], ALU.add).then_inc(z_ready, 1)
                    dve.wait_ge(squared, t + 1)
                    dve.tensor_scalar(zm[:], zs[:], 1.0 / D, 1e-6, ALU.mult, ALU.add).then_inc(zm_ready, 1)
                    dve.wait_ge(zr_ready, t + 1)
                    dve.scalar_tensor_tensor(y[:], z[:], zr[:], gain[:], ALU.mult, ALU.mult).then_inc(y_ready, 1)

            pipeline(dve, step)


def constants():
    f32 = np.float32
    a = np.arange(P)
    s, t = a[:, None], a[None, :]
    same = (s // CHUNK) == (t // CHUNK)
    m = {"ident": np.eye(P), "chunk_upto": (s <= t) & same, "chunk_after": (s > t) & same,
         "halves": np.stack([a < P // 2, a >= P // 2], 1)}
    own = np.where(t <= s, 0.0, NEG)
    earlier = np.where(t > s, 0.0, NEG)
    m["band_first"] = np.concatenate([own, np.full((P, P), NEG)], 1)
    m["band_odd"] = np.concatenate([earlier, own], 1)
    freq = f32(500000.0) ** (-np.arange(0, 2 * ROPE, 2, dtype=f32) / f32(2 * ROPE))
    angle = np.arange(SEQ, dtype=f32)[:, None] * freq[None].astype(f32)
    m["rope"] = np.concatenate([np.cos(angle), np.sin(angle)], 1)
    first = (s < P // 2).astype(f32)
    m["from_mid"] = np.stack([(s <= t) - first, (s < t) - first], 1)
    m["causal2"] = np.stack([s < t, s <= t], 1)
    m["blocks"] = np.stack([((s >> (n + 1)) == (t >> (n + 1))) & ((s >> n) % 2 == 0) & ((t >> n) % 2 == 1) for n in range(LEVELS)], 1)
    m["own_head"] = (s // RW_DIM) == (t // RW_DIM)
    k = np.arange(BANK)[None]
    m["causal4"] = np.stack([np.where(k <= P * r + s, 0.0, NEG) for r in range(GROUPS)], 1)
    pick = np.zeros((3, FX_HEADS, FX_HEADS, P))
    for h in range(FX_HEADS):
        pick[:, h, h] = 1
    m["pick"] = np.concatenate([pick.reshape(3 * FX_HEADS, FX_HEADS, P), np.zeros((P - 3 * FX_HEADS, FX_HEADS, P))])
    sizes = (2, 4, 8, 16)
    def windows(count):
        return np.stack([((s <= t) & (s > t - n)) / count(n) - (s == t) for n in sizes], 1)
    m["window_first"] = windows(lambda n: np.minimum(t + 1, n))
    m["window"] = windows(lambda n: n)
    m["window_prev"] = np.stack([(s - P > t - n) / n for n in sizes], 1)
    m["chunk_ones"] = np.stack([np.broadcast_to(s < CHUNK, (P, P)), np.broadcast_to(s >= CHUNK, (P, P))], 1)
    v = np.arange(BR)[None]
    m["state_mask"] = np.concatenate([s // (GLA_K // GLA_HEADS) == v // GLA_V, np.ones((P, BR), bool)], 1)
    m["zeros"] = np.zeros((1, 4 * D))
    return {n: np.ascontiguousarray(c.astype(f32)) for n, c in m.items()}


def build_program(nc, a, c, out):
    x = a["x"][0]

    def scratch(name, shape):
        return nc.dram_tensor(name, shape, F32, kind="Internal").ap()

    x1, x2 = scratch("x1_dram", [SEQ, D]), scratch("x2_dram", [SEQ, D])
    mixed, queries, gates = (scratch(f"{n}_dram", [SEQ, BANK]) for n in ("mixed", "queries", "gates"))
    hgrn(nc, x, a["w_in"][0], a["lb_logits"], a["hg_norm_w"], c, mixed)
    window_attention(nc, x, a["w_in"][0], a["w_out"][0], a["sinks"], a["ln_g"], a["ln_b"], c["rope"], c, mixed, x1)
    par = {n: a[f"rw_{n}_2"] for n in ("mu", "w0", "a0", "k_k", "k_a", "gn_g", "gn_b")}
    par |= {"w_up": a["rw_w_up_2"][0], "a_up": a["rw_a_up_2"][0], "r_k": a["rw_r_k_2"].rearrange("a h d -> a (h d)")}
    rwkv(nc, x1, a["norm_g_2"], a["w_in_2"][0], RW_COLS + 3 * FX + FX_HEADS, par, c, mixed)
    with ExitStack() as ctx:
        keysT = ctx.enter_context(nc.sbuf_tensor("keysT", [P, FX_HEADS // 2, SEQ], F32))
        values = ctx.enter_context(nc.sbuf_tensor("values", [P, TILES, FX], F32))
        cum3 = ctx.enter_context(nc.sbuf_tensor("cum3", [P, SEQ], BF16))
        fox_project(nc, x1, a["norm_g_2"], a["w_in_2"][0], a["fox_q_g_2"], a["fox_k_g_2"], a["fox_b_f_2"], c, keysT, values, cum3, queries, gates)
        forgetting_attention(nc, x1, a["w_out_2"][0], a["final_g_2"].rearrange("(a d) -> a d", a=1), c, keysT, values, cum3, queries, gates, mixed, x2)
    short_mixers(nc, x2, a["norm_w_3"], a["w_in_3"][0], a["conv_a_w_3"][0], a["pool_w_3"][0], a["pool_scale_3"], c, mixed)
    par = {"conv_w": a["ssd_conv_w_3"][0], "conv_b": a["ssd_conv_b_3"], "gate_w": a["gla_gate_w_3"][0], "gate_b": a["gla_gate_b_3"],
           "dt_bias": a["ssd_dt_bias_3"], "a_log": a["ssd_a_log_3"], "d": a["ssd_d_3"], "gla_norm": a["gla_norm_w_3"],
           "ssd_norm": a["ssd_norm_w_3"], "final": a["final_norm_w_3"].rearrange("(a d) -> a d", a=1)}
    recurrences(nc, x2, a["norm_w_3"], a["w_in_3"][0], par, a["w_out_3"][0], c, mixed, out[0])


INPUTS = ["x", "w_in", "lb_logits", "hg_norm_w", "sinks", "w_out", "ln_g", "ln_b", "norm_g_2", "w_in_2", "rw_mu_2", "rw_w_up_2",
          "rw_w0_2", "rw_a_up_2", "rw_a0_2", "rw_k_k_2", "rw_k_a_2", "rw_r_k_2", "rw_gn_g_2", "rw_gn_b_2", "fox_q_g_2", "fox_k_g_2",
          "fox_b_f_2", "w_out_2", "final_g_2", "norm_w_3", "w_in_3", "conv_a_w_3", "gla_gate_w_3", "gla_gate_b_3", "gla_norm_w_3",
          "pool_w_3", "pool_scale_3", "ssd_conv_w_3", "ssd_conv_b_3", "ssd_dt_bias_3", "ssd_a_log_3", "ssd_d_3", "ssd_norm_w_3",
          "w_out_3", "final_norm_w_3"]


def kernel(**inputs):
    import concourse.bacc as bacc
    from concourse.bass_utils import run_bass_kernel_spmd

    nc = bacc.Bacc("TRN2", target_bir_lowering=False, num_devices=1)
    arrays, a, c = {}, {}, {}
    for name in INPUTS:
        v = np.ascontiguousarray(inputs[name])
        arrays[f"in_{name}"] = v
        a[name] = nc.dram_tensor(f"in_{name}", v.shape, mybir.dt.from_np(v.dtype), kind="ExternalInput").ap()
    for name, v in constants().items():
        arrays[f"const_{name}"] = v
        c[name] = nc.dram_tensor(f"const_{name}", v.shape, F32, kind="ExternalInput").ap()
    out = nc.dram_tensor("out_dram", [1, SEQ, D], F32, kind="ExternalOutput").ap()
    build_program(nc, a, c, out)
    r = run_bass_kernel_spmd(nc, [arrays], core_ids=[0])
    return r.results[0]["out_dram"]
```

```python
import math
from contextlib import ExitStack

import concourse.bass as bass
import numpy as np
from concourse import mybir

F32 = mybir.dt.float32
BF16 = mybir.dt.bfloat16
F32R = mybir.dt.float32r
ALU = mybir.AluOpType
ACT = mybir.ActivationFunctionType
AX = mybir.AxisListType.X

P = 128
D = 1024
KC = D // P
SEQ = 2048
TILES = SEQ // P
BANK = 512
NEG = -1.0e30


def need(eng, sem, n):
    if isinstance(n, int) and n <= 0:
        return
    eng.wait_ge(sem, n)


def pipeline(eng, step):
    step(0, 0, 0, None, None, None)
    step(1, 0, 1, 0, 0, 0)
    step(2, 1, 0, 1, 0, 1)
    with eng.Fori(1, TILES // 2 - 1) as j:
        step(2 * j + 1, j, 1, 2 * j, j, 0)
        step(2 * j + 2, j + 1, 0, 2 * j + 1, j, 1)
    step(TILES - 1, TILES // 2 - 1, 1, TILES - 2, TILES // 2 - 1, 0)
    step(None, None, None, TILES - 1, TILES // 2 - 1, 1)


class Stage:

    def __init__(self, nc, ctx, name):
        self.nc, self.ctx, self.name, self.sems = nc, ctx, name, []

    def sb(self, name, shape, dt=F32):
        return self.ctx.enter_context(self.nc.sbuf_tensor(f"{self.name}_{name}", shape, dt))

    def bank(self, name):
        return self.ctx.enter_context(self.nc.psum_tensor(f"{self.name}_{name}", [P, BANK], F32))

    def sem(self, name):
        self.sems.append(self.ctx.enter_context(self.nc.semaphore(f"{self.name}_{name}")))
        return self.sems[-1]

    def block(self):
        self.ctx.callback(self.clear)
        return self.ctx.enter_context(self.nc.Block())

    def clear(self):
        with self.nc.Block() as block:
            @block.sync
            def _(sp):
                for one in self.sems:
                    sp.sem_clear(one)


def heads(ap, n):
    return ap.rearrange("p (h d) -> p h d", h=n)


def spread(ap, d):
    return ap.unsqueeze(2).to_broadcast([ap.shape[0], ap.shape[1], d])


def again(ap, n):
    return ap.unsqueeze(1).to_broadcast([ap.shape[0], n, ap.shape[1]])


def row(ap, a, b):
    return ap[0:1, a:b].to_broadcast([P, b - a])


class Normed:

    def __init__(self, s, x, gain, ident, banks, eps=1e-6, split=False):
        self.split = split
        if split:
            self.parts, self.low_ready = Parts(s, "hT", [P, KC, P]), s.sem("hT_low_ready")
        self.gain_row, self.gain, self.gain_here = gain, s.sb("x_gain", [P, D]), s.sem("x_gain_here")
        self.x, self.ident, self.banks, self.eps = x, ident, banks, eps
        self.xt, self.xn, self.hT = s.sb("xt", [P, D]), s.sb("xn", [P, D]), self.parts.high if split else s.sb("hT", [P, KC, P])
        self.total, self.ms, self.rms, self.power = (s.sb(n, [P, 1]) for n in ("x_total", "x_ms", "x_rms", "x_power"))
        self.x_here, self.squared, self.ms_ready, self.rms_ready = (s.sem(n) for n in ("x_here", "x_squared", "x_ms_ready", "x_rms_ready"))
        self.normed, self.turned, self.ready = s.sem("x_normed"), s.sem("x_turned"), s.sem("hT_ready")

    def load_gain(self, sp):
        sp.dma_start(self.gain[:], row(self.gain_row, 0, D)).then_inc(self.gain_here, 16)

    def load(self, sp, n):
        need(sp, self.normed, n)
        sp.dma_start(self.xt[:], self.x[bass.ds(n * P, P), :]).then_inc(self.x_here, 16)

    def square(self, act, n):
        act.wait_ge(self.x_here, 16 * (n + 1))
        need(act, self.turned, 2 * n)
        act.activation(self.xn[:], self.xt[:], ACT.Square, accum_out=self.total[:]).then_inc(self.squared, 1)

    def mean(self, dve, n):
        dve.wait_ge(self.squared, n + 1)
        dve.tensor_scalar(self.ms[:], self.total[:], 1.0 / D, self.eps, ALU.mult, ALU.add).then_inc(self.ms_ready, 1)

    def root(self, pool, n):
        pool.wait_ge(self.ms_ready, n + 1)
        pool.tensor_tensor(self.rms[:], self.ms[:], self.power[:], ALU.pow).then_inc(self.rms_ready, 1)

    def scale(self, dve, n):
        if isinstance(n, int) and n == 0:
            dve.wait_ge(self.gain_here, 16)
        dve.wait_ge(self.rms_ready, n + 1)
        dve.scalar_tensor_tensor(self.xn[:], self.xt[:], self.rms[:], self.gain[:], ALU.mult, ALU.mult).then_inc(self.normed, 1)

    def turn(self, pe, i, freed=None):
        pe.wait_ge(self.normed, i + 1)
        if self.split:
            need(pe, self.low_ready, 2 * i)
        for g in range(2):
            if not self.split:
                need(pe, freed[g], i)
            for c in range(4):
                last = pe.transpose(self.banks[g][:, c * P:(c + 1) * P], self.xn[:, (4 * g + c) * P:(4 * g + c + 1) * P], self.ident[:])
            last.then_inc(self.turned, 1)

    def take(self, act, i):
        for g in range(2):
            act.wait_ge(self.turned, 2 * i + g + 1)
            act.copy(self.hT[:, 4 * g:4 * g + 4, :], heads(self.banks[g][:], 4)).then_inc(self.ready, 1)


    def take_low(self, dve, i):
        for g in range(2):
            dve.wait_ge(self.ready, 2 * i + g + 1)
            self.parts.take_low(dve, lambda ap: ap[:, 4 * g:4 * g + 4, :], heads(self.banks[g][:], 4)).then_inc(self.low_ready, 1)


def load_columns(sp, w, w_in, pieces, here):
    for at, col, n in pieces:
        sp.dma_start(w[:, :, at:at + n], w_in[:, col:col + n].rearrange("(k p) n -> p k n", p=P)).then_inc(here, 16)


class Parts:

    def __init__(self, s, name, shape):
        self.high, self.low = s.sb(f"{name}_high", shape, F32R), s.sb(f"{name}_low", shape, F32R)

    def take_low(self, dve, part, whole):
        return dve.tensor_tensor(part(self.low), whole, part(self.high).bitcast(F32), ALU.subtract)


class SplitWeights(Parts):

    def __init__(self, s, cols):
        shape = [P, KC, cols[-1][1]]
        self.high = s.sb("w_high", shape, F32R)
        with s.nc.sbuf_tensor(f"{s.name}_w_loaded", shape, F32) as loaded:
            self.loaded = loaded
        self.low = s.sb("w_low", shape, F32R)
        self.cols = cols
        self.here, self.high_ready, self.low_ready = ([s.sem(f"{n}{c}") for c in range(len(cols))] for n in ("w_here", "w_high", "w_low"))

    def load(self, sp, w_in, c, pieces):
        load_columns(sp, self.loaded, w_in, pieces, self.here[c])

    def take_high_of(self, act, c, transfers):
        lo, hi = self.cols[c]
        act.wait_ge(self.here[c], 16 * transfers)
        act.copy(self.high[:, :, lo:hi], self.loaded[:, :, lo:hi]).then_inc(self.high_ready[c], 1)

    def take_low_of(self, dve, c):
        lo, hi = self.cols[c]
        dve.wait_ge(self.high_ready[c], 1)
        self.take_low(dve, lambda ap: ap[:, :, lo:hi], self.loaded[:, :, lo:hi]).then_inc(self.low_ready[c], 1)

    def project(self, pe, out, hT, c, low_here, lo=None, hi=None):
        if lo is None:
            lo, hi = self.cols[c]
        for kc in range(KC):
            pe.matmul(out, hT.high[:, kc, :], self.high[:, kc, lo:hi], start=kc == 0, stop=False)
            pe.matmul(out, hT.high[:, kc, :], self.low[:, kc, lo:hi], start=False, stop=False)
        low_here()
        for kc in range(KC):
            last = pe.matmul(out, hT.low[:, kc, :], self.high[:, kc, lo:hi], start=False, stop=kc == KC - 1)
        return last


def rows_of(eng, t):
    return bass.ds(t * P if isinstance(t, int) else eng.snap(t * P), P)


HG = 512
HG_HEADS = 4
CHUNK = 64


def hgrn(nc, x, w_in, lb_logits, hg_norm_w, masks, mixed):
    with ExitStack() as ctx:
        s = Stage(nc, ctx, "hg")
        sb, sem = s.sb, s.sem
        w = SplitWeights(s, [(c * HG, (c + 1) * HG) for c in range(4)])
        ident = sb("ident", [P, P])
        upto = sb("upto", [P, P])
        after = sb("after", [P, P])
        halves = sb("halves", [P, 2])
        span = sb("span", [P, HG])
        centre = sb("centre", [P, HG])
        half_norm = sb("half_norm", [P, HG])
        power = sb("power", [P, HG_HEADS])
        xt = [sb(f"xt{p}", [P, D]) for p in range(2)]
        hT = Parts(s, "hT", [P, KC, P])
        tanh = sb("tanh", [P, HG])
        q2 = [sb(f"q2{p}", [P, HG]) for p in range(2)]
        tanh_f = [sb(f"tanh_f{p}", [P, HG]) for p in range(2)]
        v = [sb(f"v{p}", [P, HG]) for p in range(2)]
        gate2 = [sb(f"gate2{p}", [P, HG]) for p in range(2)]
        part = sb("part", [P, HG])
        f = sb("f", [P, HG])
        k = sb("k", [P, HG])
        logf = sb("logf", [P, HG])
        e_cum = sb("e_cum", [P, HG])
        e_neg = sb("e_neg", [P, HG])
        e_rest = sb("e_rest", [P, HG])
        decay = sb("decay", [P, HG_HEADS, 2])
        qd = sb("qd", [P, HG])
        kd = sb("kd", [P, HG])
        ks = sb("ks", [P, HG])
        qdT = sb("qdT", [P, HG_HEADS, P])
        kdT = sb("kdT", [P, HG_HEADS, P])
        A = sb("A", [P, HG_HEADS, P])
        S = [sb(f"S{c}", [P, HG_HEADS, P]) for c in range(2)]
        o = sb("o", [P, HG])
        logits = [n[:].rearrange("p h t -> p (h t)") for n in (A, kdT)]
        sq = e_neg
        ms = sb("ms", [P, HG_HEADS])
        rstd = sb("rstd", [P, HG_HEADS])
        mix = [sb(f"mix{p}", [P, HG]) for p in range(2)]
        pj = [s.bank(f"pj{b}") for b in range(2)]
        cum_a = s.bank("cum_a")
        rest_o = s.bank("rest_o")
        tot_i0 = s.bank("tot_i0")
        inc1 = s.bank("inc1")
        tq = s.bank("tq")
        tk = s.bank("tk")

        consts_in, low_ready = sem("consts_in"), sem("low_ready")
        x_here = [sem(f"x_here{p}") for p in range(2)]
        stored = [sem(f"stored{p}") for p in range(2)]
        set_up, set_up_act, set_up_pool = sem("set_up"), sem("set_up_act"), sem("set_up_pool")
        x_turned, hT_ready = sem("x_turned"), sem("hT_ready")
        chunk_ready, tanh_ready = sem("chunk_ready"), sem("tanh_ready")
        taken = [sem(f"taken{c}") for c in range(4)]
        f_ready, logf_ready, cum_ready, exp_ready = sem("f_ready"), sem("logf_ready"), sem("cum_ready"), sem("exp_ready")
        dec_ready, ks_ready, turned_ready = sem("dec_ready"), sem("ks_ready"), sem("turned_ready")
        qdT_ready, kdT_ready, A_done, A_ready = sem("qdT_ready"), sem("kdT_ready"), sem("A_done"), sem("A_ready")
        inc_ready, S_mid, S_end, o_done, o_ready = sem("inc_ready"), sem("S_mid"), sem("S_end"), sem("o_done"), sem("o_ready")
        ms_ready, rstd_ready, mix_ready = sem("ms_ready"), sem("rstd_ready"), sem("mix_ready")

        block = s.block()

        @block.sync
        def _(sp):
            for dst, src in ((ident[:], masks["ident"]), (upto[:], masks["chunk_upto"]), (after[:], masks["chunk_after"]),
                             (halves[:], masks["halves"]), (logits[0], row(lb_logits, 0, HG)),
                             (logits[1], lb_logits[1:2, :].to_broadcast([P, HG])),
                             (half_norm[:], row(hg_norm_w, 0, HG))):
                sp.dma_start(dst, src).then_inc(consts_in, 16)
            sp.dma_start(xt[0][:], x[0:P, :]).then_inc(x_here[0], 16)
            for c in range(4):
                w.load(sp, w_in, c, [(c * HG, c * HG, HG)])

            def step(i, hi, pi, t, ht, pt):
                if i is not None and not (isinstance(i, int) and i == TILES - 1):
                    need(sp, x_turned, 2 * i)
                    sp.dma_start(xt[1 - pi][:], x[bass.ds((i + 1) * P, P), :]).then_inc(x_here[1 - pi], 16)
                if t is not None:
                    sp.wait_ge(mix_ready, t + 1)
                    sp.dma_start(mixed[bass.ds(t * P, P), 0:HG], mix[pt][:]).then_inc(stored[pt], 16)

            pipeline(sp, step)
            for p in range(2):
                sp.wait_ge(stored[p], 16 * TILES // 2)

        @block.tensor
        def _(pe):
            pe.wait_ge(consts_in, 16 * 7)

            def turn_x(i, hi, pi):
                pe.wait_ge(x_here[pi], 16 * (hi + 1))
                need(pe, low_ready, 2 * i)
                for g in range(2):
                    for c in range(4):
                        last = pe.transpose((tq, tk)[g][:, c * P:(c + 1) * P], xt[pi][:, (4 * g + c) * P:(4 * g + c + 1) * P], ident[:])
                    last.then_inc(x_turned, 1)

            def project(i, c):
                if c == 0:
                    pe.wait_ge(hT_ready, 2 * i + 2)
                if c < 2:
                    need(pe, taken[c + 2], i)
                else:
                    pe.wait_ge(taken[c - 2], i + 1)
                if isinstance(i, int) and i == 0:
                    pe.wait_ge(w.low_ready[c], 1)
                last = w.project(pe, pj[c % 2][:], hT, c, lambda: c == 0 and pe.wait_ge(low_ready, 2 * i + 2))
                last.then_inc(chunk_ready, 1)

            def cumulate(t):
                pe.wait_ge(logf_ready, t + 1)
                need(pe, o_ready, t)
                pe.matmul(cum_a[:], upto[:], logf[:], start=True, stop=True)
                pe.matmul(rest_o[:], after[:], logf[:], start=True, stop=True)
                need(pe, S_end, t)
                for h in range(HG_HEADS):
                    last = pe.matmul(tot_i0[:, 2 * h:2 * h + 2], logf[:, h * P:(h + 1) * P], halves[:], start=True, stop=True)
                last.then_inc(cum_ready, 1)

            def turn_qk(t):
                pe.wait_ge(dec_ready, t + 1)
                for h in range(HG_HEADS):
                    pe.transpose(tq[:, h * P:(h + 1) * P], qd[:, h * P:(h + 1) * P], ident[:])
                for h in range(HG_HEADS):
                    last = pe.transpose(tk[:, h * P:(h + 1) * P], kd[:, h * P:(h + 1) * P], ident[:])
                last.then_inc(turned_ready, 1)

            def attend(t):
                pe.wait_ge(qdT_ready, t + 1)
                pe.wait_ge(kdT_ready, t + 1)
                for h in range(HG_HEADS):
                    last = pe.matmul(cum_a[:, h * P:(h + 1) * P], kdT[:, h, :], qdT[:, h, :], start=True, stop=True)
                last.then_inc(A_done, 1)

            def increments(t, pt):
                pe.wait_ge(ks_ready, t + 1)
                for c, bank in ((0, tot_i0), (1, inc1)):
                    lo = c * CHUNK
                    for h in range(HG_HEADS):
                        last = pe.matmul(bank[:, h * P:(h + 1) * P], ks[lo:lo + CHUNK, h * P:(h + 1) * P],
                                         v[pt][lo:lo + CHUNK, h * P:(h + 1) * P], start=True, stop=True)
                    last.then_inc(inc_ready, 1)

            def outputs(t, pt):
                pe.wait_ge(A_ready, t + 1)
                need(pe, S_end, t)
                pe.wait_ge(S_mid, t + 1)
                for h in range(HG_HEADS):
                    cols = slice(h * P, (h + 1) * P)
                    for c in range(2):
                        lo = c * CHUNK
                        pe.matmul(rest_o[lo:lo + CHUNK, cols], qdT[:, h, lo:lo + CHUNK], S[c][:, h, :], start=True, stop=False)
                    last = pe.matmul(rest_o[:, cols], A[:, h, :], v[pt][:, cols], start=False, stop=True)
                last.then_inc(o_done, 1)

            def step(i, hi, pi, t, ht, pt):
                if i is not None:
                    turn_x(i, hi, pi)
                if t is not None:
                    cumulate(t)
                if i is not None:
                    project(i, 0)
                if t is not None:
                    turn_qk(t)
                if i is not None:
                    project(i, 1)
                if t is not None:
                    attend(t)
                    increments(t, pt)
                if i is not None:
                    project(i, 2)
                if t is not None:
                    outputs(t, pt)
                if i is not None:
                    project(i, 3)

            pipeline(pe, step)

        @block.scalar
        def _(act):
            act.wait_ge(set_up_pool, 1)
            act.activation(span[:], part[:], ACT.Tanh, scale=0.5).then_inc(set_up_act, 1)
            w.take_high_of(act, 0, 1)

            def take_x(i):
                for g in range(2):
                    act.wait_ge(x_turned, 2 * i + g + 1)
                    act.copy(hT.high[:, 4 * g:4 * g + 4, :], heads((tq, tk)[g][:], 4)).then_inc(hT_ready, 1)

            def take(i, pi, c):
                if isinstance(i, int) and i == 0 and c < 3:
                    w.take_high_of(act, c + 1, 1)
                act.wait_ge(chunk_ready, 4 * i + c + 1)
                if c in (0, 3):
                    if c == 0:
                        need(act, taken[3], i)
                    else:
                        act.wait_ge(taken[0], i + 1)
                    act.activation(tanh[:], pj[c % 2][:], ACT.Tanh, scale=0.5).then_inc(tanh_ready, 1)
                elif c == 1:
                    act.activation(tanh_f[pi][:], pj[1][:], ACT.Tanh, scale=0.5).then_inc(taken[1], 1)
                else:
                    act.copy(v[pi][:], pj[0][:]).then_inc(taken[2], 1)

            def step(i, hi, pi, t, ht, pt):
                if t is not None:
                    act.wait_ge(f_ready, t + 1)
                    act.activation(logf[:], f[:], ACT.Ln).then_inc(logf_ready, 1)
                if i is not None:
                    take_x(i)
                if t is not None:
                    act.wait_ge(cum_ready, t + 1)
                    act.activation(e_cum[:], cum_a[:], ACT.Exp)
                    act.activation(e_neg[:], cum_a[:], ACT.Exp, scale=-1.0)
                    act.activation(e_rest[:], rest_o[:], ACT.Exp)
                    act.activation(decay[:].rearrange("p h c -> p (h c)"), tot_i0[:, 0:8], ACT.Exp).then_inc(exp_ready, 1)
                if i is not None:
                    take(i, pi, 0)
                if t is not None:
                    act.wait_ge(turned_ready, t + 1)
                    act.copy(qdT[:], heads(tq[:], 4)).then_inc(qdT_ready, 1)
                if i is not None:
                    take(i, pi, 1)
                    take(i, pi, 2)
                if t is not None:
                    act.wait_ge(o_done, t + 1)
                    act.copy(o[:], rest_o[:]).then_inc(o_ready, 1)
                if i is not None:
                    take(i, pi, 3)

            pipeline(act, step)

        @block.gpsimd
        def _(pool):
            pool.memset(power[:], -0.5)
            pool.memset(S[0][:], 0.0)
            pool.wait_ge(consts_in, 16 * 7)
            pool.tensor_tensor(part[:], logits[0], logits[1], ALU.subtract).then_inc(set_up_pool, 1)
            pool.drain()

            def step(i, hi, pi, t, ht, pt):
                if t is not None:
                    pool.wait_ge(ms_ready, t + 1)
                    pool.tensor_tensor(rstd[:], ms[:], power[:], ALU.pow).then_inc(rstd_ready, 1)

            pipeline(pool, step)

        @block.vector
        def _(dve):
            dve.wait_ge(consts_in, 16 * 7)
            dve.wait_ge(set_up_act, 1)
            dve.tensor_scalar(centre[:], span[:], 0.25, 0.75, ALU.mult, ALU.add)
            dve.tensor_scalar(half_norm[:], half_norm[:], 0.5, None, ALU.mult)
            dve.drain()
            dve.tensor_scalar(span[:], span[:], -0.25, 0.25, ALU.mult, ALU.add).then_inc(set_up, 1)
            dve.drain()

            w.take_low_of(dve, 0)

            def take_low(i):
                for g in range(2):
                    dve.wait_ge(hT_ready, 2 * i + g + 1)
                    hT.take_low(dve, lambda ap: ap[:, 4 * g:4 * g + 4, :], heads((tq, tk)[g][:], 4)).then_inc(low_ready, 1)

            def gated(i, c, dst):
                dve.wait_ge(tanh_ready, 2 * i + (1 if c == 0 else 2))
                dve.scalar_tensor_tensor(dst[:], tanh[:], 1.0, pj[c % 2][:], ALU.add, ALU.mult).then_inc(taken[c], 1)

            def update(t, c):
                dve.wait_ge(inc_ready, 2 * t + c + 1)
                bank = (tot_i0, inc1)[c]
                for h in range(HG_HEADS):
                    last = dve.scalar_tensor_tensor(S[1 - c][:, h, :], S[c][:, h, :], decay[:, h, c:c + 1], bank[:, h * P:(h + 1) * P],
                                                    ALU.mult, ALU.add)
                last.then_inc((S_mid, S_end)[c], 1)

            def step(i, hi, pi, t, ht, pt):
                if t is not None:
                    dve.wait_ge(taken[1], t + 1)
                    dve.tensor_tensor(part[:], span[:], tanh_f[pt][:], ALU.mult)
                    dve.drain()
                    dve.tensor_tensor(f[:], part[:], centre[:], ALU.add).then_inc(f_ready, 1)
                    dve.tensor_tensor(k[:], span[:], part[:], ALU.subtract)
                if i is not None:
                    take_low(i)
                if t is None:
                    w.take_low_of(dve, 1)
                if t is not None:
                    dve.drain()
                    dve.wait_ge(exp_ready, t + 1)
                    dve.scalar_tensor_tensor(qd[:], q2[pt][:], 0.5, e_cum[:], ALU.mult, ALU.mult)
                    dve.tensor_tensor(kd[:], k[:], e_neg[:], ALU.mult).then_inc(dec_ready, 1)
                    dve.tensor_tensor(ks[:], k[:], e_rest[:], ALU.mult).then_inc(ks_ready, 1)
                if i is not None:
                    gated(i, 0, q2[pi])
                if t is None:
                    for c in (2, 3):
                        w.take_low_of(dve, c)
                if t is not None:
                    dve.wait_ge(turned_ready, t + 1)
                    dve.tensor_copy(kdT[:], heads(tk[:], 4)).then_inc(kdT_ready, 1)
                    dve.wait_ge(A_done, t + 1)
                    dve.tensor_tensor(A[:], heads(cum_a[:], 4), again(upto[:], 4), ALU.mult).then_inc(A_ready, 1)
                    update(t, 0)
                    dve.wait_ge(o_done, t + 1)
                    update(t, 1)
                    dve.wait_ge(o_ready, t + 1)
                    dve.tensor_tensor(sq[:], o[:], o[:], ALU.mult)
                    dve.drain()
                    dve.tensor_reduce(ms[:], heads(sq[:], HG_HEADS), AX, ALU.add)
                    dve.drain()
                    dve.tensor_scalar(ms[:], ms[:], 1.0 / P, 1e-6, ALU.mult, ALU.add).then_inc(ms_ready, 1)
                    need(dve, stored[pt], 16 * ht)
                    dve.tensor_tensor(mix[pt][:], half_norm[:], gate2[pt][:], ALU.mult)
                    dve.wait_ge(rstd_ready, t + 1)
                    dve.tensor_tensor(heads(o[:], 4), heads(o[:], 4), spread(rstd[:], P), ALU.mult)
                    dve.drain()
                    dve.tensor_tensor(mix[pt][:], mix[pt][:], o[:], ALU.mult).then_inc(mix_ready, 1)
                if i is not None:
                    gated(i, 3, gate2[pi])

            pipeline(dve, step)


SW = 512
SW_HEADS = 8
SW_DIM = 64
SW_KV = 128
QKV = SW + 2 * SW_KV
ROPE = 8
FIRST_COL = 4 * HG
ALPHA = 2.0 ** 0.25


def window_attention(nc, x, w_in, w_out, sinks, ln_g, ln_b, rope, masks, mixed, x_out):
    with ExitStack() as ctx:
        s = Stage(nc, ctx, "sw")
        sb, sem = s.sb, s.sem
        w = SplitWeights(s, [(0, SW), (SW, QKV), (QKV, QKV + SW)])
        wo = sb("wo", [P, KC, D])
        ident = sb("ident", [P, P])
        band = [sb(f"band{p}", [P, 2 * P]) for p in range(2)]
        before = sb("before", [P, P])
        sink = sb("sink", [P, SW_HEADS])
        gain, shift = sb("gain", [P, D]), sb("shift", [P, D])
        power = sb("power", [P, 1])
        xt = [sb(f"xt{p}", [P, D]) for p in range(2)]
        xres = [sb(f"xres{p}", [P, D]) for p in range(2)]
        hgm = [sb(f"hgm{p}", [P, HG]) for p in range(2)]
        cs = [sb(f"cs{p}", [P, 2 * ROPE]) for p in range(2)]
        hT = Parts(s, "hT", [P, KC, P])
        qkv = [sb(f"qkv{p}", [P, QKV]) for p in range(2)]
        gate2 = [sb(f"gate2{p}", [P, SW]) for p in range(2)]
        tanh = sb("tanh", [P, SW])
        rot = [sb(f"rot{n}", [P, 10, ROPE]) for n in range(4)]
        vr = sb("vr", [P, 2, SW_KV])
        qT = sb("qT", [P, 4, P])
        kT = sb("kT", [P, 2, P])
        sm = sb("sm", [P, SW_HEADS, 2 * P])
        top, negtop, sinkd, expsink, total, rden = (sb(n, [P, SW_HEADS]) for n in ("top", "negtop", "sinkd", "expsink", "total", "rden"))
        pT = sb("pT", [P, 2 * SW_HEADS, P])
        oa = sb("oa", [P, SW])
        mixa = sb("mixa", [P, SW])
        mixT = sb("mixT", [P, KC, P])
        z = sb("z", [P, D])
        stats = sb("stats", [P, 2, 6])
        moments = sb("moments", [P, 2])
        rstd = sb("rstd", [P, 1])
        y = [sb(f"y{p}", [P, D]) for p in range(2)]
        pj = [s.bank(f"pj{b}") for b in range(2)]
        sc = [s.bank(f"sc{b}") for b in range(2)]
        tp = [s.bank(f"tp{b}") for b in range(2)]
        ov = s.bank("ov")
        th = s.bank("th")
        turned_banks = [pj[1], th]

        consts_in, wo_here, set_up_pool, low_ready = sem("consts_in"), sem("wo_here"), sem("set_up_pool"), sem("low_ready")
        x_here, t_here, stored = ([sem(f"{n}{p}") for p in range(2)] for n in ("x_here", "t_here", "stored"))
        x_turned, hT_ready, chunk_ready, tanh_ready = sem("x_turned"), sem("hT_ready"), sem("chunk_ready"), sem("tanh_ready")
        taken = [sem(f"taken{c}") for c in range(3)]
        roped, v_kept, qk_turned, qT_ready, kT_ready = sem("roped"), sem("v_kept"), sem("qk_turned"), sem("qT_ready"), sem("kT_ready")
        scored, masked, top_ready, p_ready, den_ready = sem("scored"), sem("masked"), sem("top_ready"), sem("p_ready"), sem("den_ready")
        p_turned, pT_act, pT_dve, weighed, mixa_ready = sem("p_turned"), sem("pT_act"), sem("pT_dve"), sem("weighed"), sem("mixa_ready")
        hg_turned, hgT_ready, a_turned, aT_ready = sem("hg_turned"), sem("hgT_ready"), sem("a_turned"), sem("aT_ready")
        out_done, z_ready, var_ready, rstd_ready, y_ready = sem("out_done"), sem("z_ready"), sem("var_ready"), sem("rstd_ready"), sem("y_ready")
        y_scaled = sem("y_scaled")

        block = s.block()
        CONSTS = 7
        by_pair = lambda ap: ap.rearrange("p (j g) -> p j g", g=2)
        sink_by_pair = sink[:].rearrange("p (g j) -> p j g", g=2)

        @block.sync
        def _(sp):
            for dst, src in ((ident[:], masks["ident"]), (band[0][:], masks["band_first"]), (band[1][:], masks["band_odd"]),
                             (before[:], masks["band_odd"][:, 0:P]), (gain[:], row(ln_g, 0, D)), (shift[:], row(ln_b, 0, D)),
                             (sink[:], row(sinks, 0, SW_HEADS))):
                sp.dma_start(dst, src).then_inc(consts_in, 16)
            sp.dma_start(xt[0][:], x[0:P, :]).then_inc(x_here[0], 16)
            for c in (0, 2, 1):
                lo, hi = w.cols[c]
                w.load(sp, w_in, c, [(lo, FIRST_COL + lo, hi - lo)])
            load_columns(sp, wo, w_out, [(0, 0, D)], wo_here)

            def step(i, hi, pi, t, ht, pt):
                if i is not None:
                    need(sp, z_ready, 2 * i - 2)
                    sp.dma_start(xres[pi][:], x[bass.ds(i * P, P), :]).then_inc(t_here[pi], 16)
                    sp.dma_start(hgm[pi][:], mixed[bass.ds(i * P, P), 0:HG]).then_inc(t_here[pi], 16)
                    sp.dma_start(cs[pi][:], rope[bass.ds(i * P, P), :]).then_inc(t_here[pi], 16)
                    if not (isinstance(i, int) and i == TILES - 1):
                        need(sp, x_turned, 2 * i)
                        sp.dma_start(xt[1 - pi][:], x[bass.ds((i + 1) * P, P), :]).then_inc(x_here[1 - pi], 16)
                if t is not None:
                    sp.wait_ge(y_ready, t + 1)
                    sp.dma_start(x_out[bass.ds(t * P, P), :], y[pt][:]).then_inc(stored[pt], 16)

            pipeline(sp, step)
            for p in range(2):
                sp.wait_ge(stored[p], 16 * TILES // 2)

        @block.tensor
        def _(pe):
            pe.wait_ge(consts_in, 16 * CONSTS)
            pe.wait_ge(set_up_pool, 1)

            def turn_x(i, hi, pi):
                pe.wait_ge(x_here[pi], 16 * (hi + 1))
                need(pe, taken[1], i)
                need(pe, low_ready, 2 * i)
                for g in range(2):
                    for c in range(4):
                        last = pe.transpose(turned_banks[g][:, c * P:(c + 1) * P], xt[pi][:, (4 * g + c) * P:(4 * g + c + 1) * P], ident[:])
                    last.then_inc(x_turned, 1)

            def project(i, c, lo, hi):
                if c == 0:
                    pe.wait_ge(hT_ready, 2 * i + 2)
                if c == 0:
                    need(pe, taken[2], i)
                if isinstance(i, int) and i == 0:
                    pe.wait_ge(w.low_ready[c], 1)
                if c == 2 and lo == 0:
                    pe.wait_ge(taken[0], i + 1)
                a = w.cols[c][0]
                last = w.project(pe, pj[c % 2][:, lo:hi], hT, c, lambda: c == 0 and pe.wait_ge(low_ready, 2 * i + 2), a + lo, a + hi)
                return last

            def turn_qk(t, pt):
                pe.wait_ge(roped, t + 1)
                need(pe, aT_ready, t)
                for j in range(4):
                    pe.transpose(tp[0][:, j * P:(j + 1) * P], qkv[pt][:, j * P:(j + 1) * P], ident[:])
                pe.transpose(tp[1][:, 0:P], qkv[pt][:, SW:SW + SW_KV], ident[:]).then_inc(qk_turned, 1)

            def turn_hg(t, ht, pt):
                pe.wait_ge(t_here[pt], 16 * 3 * (ht + 1))
                for c in range(4):
                    last = pe.transpose(th[:, c * P:(c + 1) * P], hgm[pt][:, c * P:(c + 1) * P], ident[:])
                last.then_inc(hg_turned, 1)

            def score(t, r):
                if r == 0:
                    pe.wait_ge(qT_ready, t + 1)
                    pe.wait_ge(kT_ready, t + 1)
                    need(pe, z_ready, 2 * t)
                else:
                    pe.wait_ge(masked, 4 * t + 2)
                for j in range(2):
                    for g in range(2):
                        part = slice(g * SW_DIM, (g + 1) * SW_DIM)
                        last = pe.matmul(sc[g][:, j * 2 * P:(j + 1) * 2 * P], qT[part, 2 * r + j, :], kT[part, :, :], start=True, stop=True)
                last.then_inc(scored, 1)

            def project_out(t, half):
                if half == 0:
                    if isinstance(t, int) and t == 0:
                        pe.wait_ge(wo_here, 16)
                    pe.wait_ge(hgT_ready, t + 1)
                    pe.wait_ge(masked, 4 * t + 4)
                else:
                    pe.wait_ge(aT_ready, t + 1)
                for c in range(2):
                    for kc in range(4 * half, 4 * half + 4):
                        last = pe.matmul(sc[c][:], mixT[:, kc, :], wo[:, kc, c * BANK:(c + 1) * BANK], start=kc == 0, stop=kc == KC - 1)
                    if half == 1:
                        last.then_inc(out_done, 1)

            def turn_p(t, rounds):
                if 0 in rounds:
                    pe.wait_ge(p_ready, t + 1)
                for n in rounds:
                    if n >= 2:
                        pe.wait_ge((pT_act, pT_dve)[n % 2], 2 * t + 1)
                    for m in range(4):
                        k = 4 * n + m
                        last = pe.transpose(tp[n % 2][:, m * P:(m + 1) * P], sm[:, k // 2, (k % 2) * P:(k % 2 + 1) * P], ident[:])
                    last.then_inc(p_turned, 1)

            def weigh(t):
                pe.wait_ge(pT_act, 2 * t + 2)
                pe.wait_ge(pT_dve, 2 * t + 2)
                pe.wait_ge(v_kept, t + 1)
                need(pe, mixa_ready, t)
                for j in range(4):
                    for g in range(2):
                        h = 4 * g + j
                        for slot in range(2):
                            last = pe.matmul(ov[:, h * SW_DIM:(h + 1) * SW_DIM], pT[:, 2 * (2 * j + g) + slot, :],
                                             vr[:, slot, g * SW_DIM:(g + 1) * SW_DIM], start=slot == 0, stop=slot == 1)
                last.then_inc(weighed, 1)

            def turn_a(t):
                pe.wait_ge(mixa_ready, t + 1)
                for c in range(4):
                    last = pe.transpose(tp[1][:, c * P:(c + 1) * P], mixa[:, c * P:(c + 1) * P], ident[:])
                last.then_inc(a_turned, 1)

            def step(i, hi, pi, t, ht, pt):
                p, m = i is not None, t is not None
                if m:
                    turn_qk(t, pt)
                if p:
                    turn_x(i, hi, pi)
                    project(i, 0, 0, SW).then_inc(chunk_ready, 1)
                if m:
                    score(t, 0)
                    turn_hg(t, ht, pt)
                if p:
                    project(i, 2, 0, 256)
                if m:
                    score(t, 1)
                    project_out(t, 0)
                if m:
                    turn_p(t, (0, 1))
                if p:
                    project(i, 2, 256, 512).then_inc(chunk_ready, 1)
                if m:
                    turn_p(t, (2, 3))
                    weigh(t)
                if p:
                    project(i, 1, 0, 2 * SW_KV).then_inc(chunk_ready, 1)
                if m:
                    turn_a(t)
                    project_out(t, 1)

            pipeline(pe, step)

        @block.scalar
        def _(act):
            w.take_high_of(act, 0, 1)

            def step(i, hi, pi, t, ht, pt):
                p, m = i is not None, t is not None
                if m:
                    act.wait_ge(qk_turned, t + 1)
                    act.copy(qT[:], heads(tp[0][:], 4)).then_inc(qT_ready, 1)
                if p:
                    for g in range(2):
                        act.wait_ge(x_turned, 2 * i + g + 1)
                        act.copy(hT.high[:, 4 * g:4 * g + 4, :], heads(turned_banks[g][:], 4)).then_inc(hT_ready, 1)
                    if not m:
                        w.take_high_of(act, 2, 1)
                    act.wait_ge(chunk_ready, 3 * i + 1)
                    act.copy(qkv[pi][:, 0:SW].rearrange("p (j g d) -> p g j d", g=2, j=4),
                             pj[0][:].rearrange("p (g j d) -> p g j d", g=2, j=4)).then_inc(taken[0], 1)
                if m:
                    act.wait_ge(hg_turned, t + 1)
                    need(act, out_done, 2 * t)
                    act.copy(mixT[:, 0:4, :], heads(th[:], 4)).then_inc(hgT_ready, 1)
                    act.wait_ge(top_ready, t + 1)
                    for h in range(SW_HEADS):
                        act.activation(sm[:, h, :], sm[:, h, :], ACT.Exp, bias=negtop[:, h:h + 1], accum_out=total[:, h:h + 1])
                    act.activation(expsink[:], sinkd[:], ACT.Exp).then_inc(p_ready, 1)
                    for n in (0, 2):
                        act.wait_ge(p_turned, 4 * t + n + 1)
                        act.copy(pT[:, 4 * n:4 * n + 4, :], heads(tp[0][:], 4)).then_inc(pT_act, 1)
                if p:
                    if not m:
                        w.take_high_of(act, 1, 1)
                    act.wait_ge(chunk_ready, 3 * i + 2)
                    need(act, taken[2], i)
                    act.activation(tanh[:], pj[0][:], ACT.Tanh, scale=0.5).then_inc(tanh_ready, 1)
                if m:
                    act.wait_ge(a_turned, t + 1)
                    act.copy(mixT[:, 4:8, :], heads(tp[1][:], 4)).then_inc(aT_ready, 1)

            pipeline(act, step)

        @block.gpsimd
        def _(pool):
            pool.memset(power[:], -0.5)
            pool.memset(kT[:, 1, :], 0.0)
            pool.memset(vr[:, 1, :], 0.0)
            pool.drain()
            pool.memset(rstd[:], 0.0).then_inc(set_up_pool, 1)

            def rotate(t, ht, pt):
                pool.wait_ge(t_here[pt], 16 * 3 * (ht + 1))
                pool.wait_ge(taken[0], t + 1)
                pool.wait_ge(taken[1], t + 1)
                qk = qkv[pt][:, 0:SW + SW_KV].rearrange("p (h d) -> p h d", h=10)
                x1, x2 = qk[:, :, 0:ROPE], qk[:, :, ROPE:2 * ROPE]
                cos, sin = again(cs[pt][:, 0:ROPE], 10), again(cs[pt][:, ROPE:], 10)
                pool.tensor_tensor(rot[0][:], x1, cos, ALU.mult)
                pool.tensor_tensor(rot[1][:], x2, sin, ALU.mult)
                pool.tensor_tensor(rot[2][:], x2, cos, ALU.mult)
                pool.tensor_tensor(rot[3][:], x1, sin, ALU.mult)
                pool.drain()
                pool.tensor_tensor(x1, rot[0][:], rot[1][:], ALU.subtract)
                pool.tensor_tensor(x2, rot[2][:], rot[3][:], ALU.add).then_inc(roped, 1)

            def step(i, hi, pi, t, ht, pt):
                if i is not None:
                    rotate(i, hi, pi)
                if t is not None:
                    pool.wait_ge(var_ready, t + 1)
                    pool.tensor_tensor(rstd[:], moments[:, 1:2], power[:], ALU.pow).then_inc(rstd_ready, 1)
                    pool.wait_ge(y_scaled, t + 1)
                    pool.tensor_tensor(y[pt][:], y[pt][:], gain[:], ALU.mult)
                    pool.drain()
                    pool.tensor_tensor(y[pt][:], y[pt][:], shift[:], ALU.add).then_inc(y_ready, 1)

            pipeline(pool, step)

        @block.vector
        def _(dve):
            dve.wait_ge(consts_in, 16 * CONSTS)
            dve.wait_ge(set_up_pool, 1)

            w.take_low_of(dve, 0)

            def take_low(i):
                for g in range(2):
                    dve.wait_ge(hT_ready, 2 * i + g + 1)
                    hT.take_low(dve, lambda ap: ap[:, 4 * g:4 * g + 4, :], heads(turned_banks[g][:], 4)).then_inc(low_ready, 1)

            def softmax(t, pt):
                by_group = sm[:].rearrange("p (j g) k -> p j g k", g=2)
                for r in range(2):
                    dve.wait_ge(scored, 2 * t + r + 1)
                    for g in range(2):
                        dve.scalar_tensor_tensor(by_group[:, 2 * r:2 * r + 2, g, :], sc[g][:].rearrange("p (j k) -> p j k", j=2), SW_DIM ** -0.5,
                                                 again(band[pt][:], 2), ALU.mult, ALU.add).then_inc(masked, 1)
                dve.drain()
                if pt == 0:
                    dve.tensor_copy(band[0][:, P:2 * P], before[:])
                dve.tensor_reduce(top[:], sm[:], AX, ALU.max)
                dve.drain()
                dve.tensor_tensor(by_pair(top[:]), by_pair(top[:]), sink_by_pair, ALU.max)
                dve.drain()
                dve.tensor_tensor(by_pair(sinkd[:]), sink_by_pair, by_pair(top[:]), ALU.subtract)
                dve.tensor_scalar(negtop[:], top[:], -1.0, None, ALU.mult).then_inc(top_ready, 1)
                dve.wait_ge(p_ready, t + 1)
                dve.tensor_tensor(total[:], total[:], expsink[:], ALU.add)
                dve.drain()
                dve.reciprocal(rden[:], total[:])
                for n in (1, 3):
                    dve.wait_ge(p_turned, 4 * t + n + 1)
                    dve.tensor_copy(pT[:, 4 * n:4 * n + 4, :], heads(tp[1][:], 4)).then_inc(pT_dve, 1)

            def step(i, hi, pi, t, ht, pt):
                p, m = i is not None, t is not None
                if m:
                    dve.wait_ge(qk_turned, t + 1)
                    dve.tensor_copy(kT[:, pt, :], tp[1][:, 0:P]).then_inc(kT_ready, 1)
                    dve.tensor_copy(vr[:, pt, :], qkv[pt][:, SW + SW_KV:QKV]).then_inc(v_kept, 1)
                if p:
                    take_low(i)
                if not m:
                    w.take_low_of(dve, 2)
                    w.take_low_of(dve, 1)
                if m:
                    softmax(t, pt)
                    dve.drain()
                    dve.wait_ge(weighed, t + 1)
                    by_group = rden[:].rearrange("p (j g) -> p g j", g=2).unsqueeze(3).to_broadcast([P, 2, 4, SW_DIM])
                    dve.tensor_tensor(oa[:].rearrange("p (g j d) -> p g j d", g=2, j=4), ov[:].rearrange("p (g j d) -> p g j d", g=2, j=4),
                                      by_group, ALU.mult)
                    dve.drain()
                    dve.scalar_tensor_tensor(mixa[:], oa[:], 0.5, gate2[pt][:], ALU.mult, ALU.mult).then_inc(mixa_ready, 1)
                if p:
                    dve.wait_ge(tanh_ready, i + 1)
                    dve.scalar_tensor_tensor(gate2[pi][:], tanh[:], 1.0, pj[0][:], ALU.add, ALU.mult).then_inc(taken[2], 1)
                    dve.wait_ge(chunk_ready, 3 * i + 3)
                    dve.tensor_copy(qkv[pi][:, SW:QKV], pj[1][:, 0:2 * SW_KV]).then_inc(taken[1], 1)
                if m:
                    dve.wait_ge(t_here[pt], 16 * 3 * (ht + 1))
                    for c in range(2):
                        dve.wait_ge(out_done, 2 * t + c + 1)
                        cols = slice(c * BANK, (c + 1) * BANK)
                        dve.scalar_tensor_tensor(z[:, cols], xres[pt][:, cols], ALPHA, sc[c][:], ALU.mult, ALU.add).then_inc(z_ready, 1)
                    dve.drain()
                    for c in range(2):
                        dve.bn_stats(stats[:, c, :], z[:, c * BANK:(c + 1) * BANK])
                    dve.drain()
                    dve.bn_aggr(moments[:], stats[:])
                    dve.drain()
                    dve.tensor_scalar(moments[:, 1:2], moments[:, 1:2], 1e-5, None, ALU.add).then_inc(var_ready, 1)
                    need(dve, stored[pt], 16 * ht)
                    dve.wait_ge(rstd_ready, t + 1)
                    dve.tensor_scalar(y[pt][:], z[:], moments[:, 0:1], rstd[:], ALU.subtract, ALU.mult).then_inc(y_scaled, 1)

            pipeline(dve, step)


RW = 512
RW_HEADS = 8
RW_DIM = 64
PAIRS = RW_HEADS // 2
LORA = 64
RW_COLS = 3 * RW + 2 * LORA
LEVELS = 7


HALF = P // 2


def halves_of(ap, l, n):
    return ap.rearrange("p (b two w) -> p b two w", two=2, w=1 << l)[:, :, n, :]


def rwkv(nc, x, norm_g, w_in, gate_col, par, masks, mixed):
    with ExitStack() as ctx:
        s = Stage(nc, ctx, "rw")
        sb, sem = s.sb, s.sem
        w = sb("w", [P, KC, RW_COLS + RW])
        ident = sb("ident", [P, P])
        from_mid = sb("from_mid", [P, 2, P])
        halves = sb("halves", [P, 2])
        causal2 = sb("causal2", [P, 2, P])
        blocks = sb("blocks", [P, LEVELS, P])
        own_head = sb("own_head", [P, P])
        mu = sb("mu", [P, RW_COLS])
        w0, a0, k_k, k_a, r_k, gn_g, gn_b = rows = [sb(n, [P, RW]) for n in ("w0", "a0", "k_k", "k_a", "r_k", "gn_g", "gn_b")]
        up = sb("up", [P, RW])
        power = sb("power", [P, RW_HEADS])
        U = [sb(f"U{p}", [P, RW_COLS]) for p in range(2)]
        M = [sb(f"M{p}", [P, RW_COLS]) for p in range(2)]
        gate2 = [sb(f"gate2{p}", [P, RW]) for p in range(2)]
        lw, a, kk, b = (sb(n, [P, RW]) for n in ("lw", "a", "kk", "b"))
        tmp, tmp2 = sb("tmp", [P, RW]), sb("tmp2", [P, RW])
        e_in, e_ex, e_neg = (sb(n, [P, RW]) for n in ("e_in", "e_ex", "e_neg"))
        e_tot = sb("e_tot", [P, PAIRS, 2])
        ss, rss, bonus, mean, var, rstd = (sb(n, [P, RW_HEADS]) for n in ("ss", "rss", "bonus", "mean", "var", "rstd"))
        krT = sb("krT", [P, PAIRS, 2, P])
        bT = sb("bT", [P, PAIRS, P])
        kT = sb("kT", [P, PAIRS, P])
        BA = sb("BA", [P, RW_HEADS, 2, P])
        KA = sb("KA", [P, RW_HEADS, 2, P])
        X = sb("X", [P, RW_HEADS, P])
        XT = sb("XT", [P, RW_HEADS, P])
        CT = sb("CT", [P, RW_HEADS, P])
        T1 = sb("T1", [P, RW_HEADS, P])
        Z, SA, y = e_neg, e_ex, e_in
        tanh = T1[:, 0:RW // P, :].rearrange("p h t -> p (h t)")
        lowT = kT[:, 0, :]
        S = sb("S", [P, PAIRS, P])
        out = [sb(f"out{p}", [P, RW]) for p in range(2)]
        pj = [s.bank(f"pj{n}") for n in range(2)]
        B = [s.bank(f"b{n}") for n in range(6)]
        front = Normed(s, x, norm_g, ident, [pj[1], pj[0]])

        CONSTS = 16
        ident_here = sem("ident_here")
        consts_in, set_up = sem("consts_in"), sem("set_up")
        w_here = [sem(f"w_here{c}") for c in range(5)]
        shifted, stored = ([sem(f"{n}{p}") for p in range(2)] for n in ("shifted", "stored"))
        chunk_ready, tanh_ready = sem("chunk_ready"), sem("tanh_ready")
        taken = [sem(f"taken{c}") for c in range(5)]
        (mixed_in, low_ready, low_turned, lowT_ready, up_done, wa_ready, wa_tanh, lw_ready, cum_done, exp_ready) = (sem(n) for n in (
            "mixed_in", "low_ready", "low_turned", "lowT_ready", "up_done", "wa_ready", "wa_tanh", "lw_ready", "cum_done", "exp_ready"))
        ss_ready, rss_ready, dec_ready, turned4, krT_ready, bkT_ready = (sem(n) for n in (
            "ss_ready", "rss_ready", "dec_ready", "turned4", "krT_ready", "bkT_ready"))
        products, masked, first_turned, X_ready, XT_ready = (sem(n) for n in (
            "products", "masked", "first_turned", "X_ready", "XT_ready"))
        CT_ready, T1_done, T1_ready, corr_done = (sem(n) for n in ("CT_ready", "T1_done", "T1_ready", "corr_done"))
        S_in, Z_done, Z_ready, SA_done, SA_ready, y_done, y_ready, inc_done, S_out = (sem(n) for n in (
            "S_in", "Z_done", "Z_ready", "SA_done", "SA_ready", "y_done", "y_ready", "inc_done", "S_out"))
        var_ready, rstd_ready, out_ready = sem("var_ready"), sem("rstd_ready"), sem("out_ready")
        ORDER = [0, 1, 3, 2, 4]
        COLS = [(0, RW), (RW, 2 * RW), (2 * RW, 3 * RW), (3 * RW, RW_COLS), (RW_COLS, RW_COLS + RW)]

        block = s.block()

        @block.sync
        def _(sp):
            sp.dma_start(ident[:], masks["ident"]).then_inc(ident_here, 16)
            front.load(sp, 0)
            front.load_gain(sp)
            load_chunk = lambda c: load_columns(sp, w, w_in, [(COLS[c][0], gate_col if c == 4 else COLS[c][0], COLS[c][1] - COLS[c][0])], w_here[c])
            load_chunk(ORDER[0])
            small = [(from_mid[:], masks["from_mid"]), (halves[:], masks["halves"]),
                     (causal2[:], masks["causal2"]), (blocks[:], masks["blocks"]), (own_head[:], masks["own_head"]),
                     (mu[:], row(par["mu"], 0, RW_COLS)), (up[0:LORA, :], par["w_up"]), (up[LORA:P, :], par["a_up"])]
            small += [(r[:], row(par[n], 0, RW)) for r, n in zip(rows, ("w0", "a0", "k_k", "k_a", "r_k", "gn_g", "gn_b"))]
            small += [(M[0][0:1, :], masks["zeros"][:, 0:RW_COLS])]
            assert len(small) == CONSTS
            for dst, src in small:
                sp.dma_start(dst, src).then_inc(consts_in, 16)
            for c in ORDER[1:]:
                load_chunk(c)

            def shift(i, pi, first):
                for c in range(4):
                    sp.wait_ge(taken[c], i + 1)
                if not first:
                    need(sp, out_ready, i - 1)
                    sp.dma_start(M[pi][0:1, :], U[1 - pi][P - 1:P, :]).then_inc(shifted[pi], 16)
                sp.dma_start(M[pi][1:P, :], U[pi][0:P - 1, :]).then_inc(shifted[pi], 16)

            def step(i, hi, pi, t, ht, pt):
                if i is not None:
                    if not (isinstance(i, int) and i == TILES - 1):
                        front.load(sp, i + 1)
                    shift(i, pi, t is None)
                if t is not None:
                    sp.wait_ge(out_ready, t + 1)
                    sp.dma_start(mixed[bass.ds(t * P, P), 0:RW], out[pt][:]).then_inc(stored[pt], 16)

            pipeline(sp, step)
            for p in range(2):
                sp.wait_ge(stored[p], 16 * TILES // 2)

        def shift_count(ht, pt):
            return 32 * ht + (16 if pt == 0 else 32)

        @block.tensor
        def _(pe):
            pe.wait_ge(ident_here, 16)

            def project(i, c, lo=0, hi=None):
                a0_, b0_ = COLS[c]
                hi = hi or b0_ - a0_
                pos = ORDER.index(c)
                if isinstance(i, int) and i == 0:
                    pe.wait_ge(w_here[c], 16)
                if lo == 0:
                    if pos == 0:
                        pe.wait_ge(front.ready, 2 * i + 2)
                    if pos >= 2:
                        pe.wait_ge(taken[ORDER[pos - 2]], i + 1)
                for kc in range(KC):
                    last = pe.matmul(pj[pos % 2][:, lo:hi], front.hT[:, kc, :], w[:, kc, a0_ + lo:a0_ + hi], start=kc == 0, stop=kc == KC - 1)
                return last

            def turn_low(t, pt):
                pe.wait_ge(low_ready, t + 1)
                pe.transpose(B[0][:, 0:P], M[pt][:, 3 * RW:RW_COLS], ident[:]).then_inc(low_turned, 1)

            def raise_low(t):
                pe.wait_ge(lowT_ready, t + 1)
                pe.matmul(B[1][:], lowT[0:LORA], up[0:LORA, :], start=True, stop=True)
                pe.matmul(B[2][:], lowT[LORA:P], up[LORA:P, :], start=True, stop=True).then_inc(up_done, 1)

            def cumulate(t):
                pe.wait_ge(lw_ready, t + 1)
                need(pe, S_out, t)
                for n in range(2):
                    pe.matmul(B[3 + n][:], from_mid[:, n, :], lw[:], start=True, stop=True)
                for p in range(PAIRS):
                    last = pe.matmul(B[5][:, 2 * p:2 * p + 2], lw[:, p * P:(p + 1) * P], halves[:], start=True, stop=True)
                last.then_inc(cum_done, 1)

            def turn_all(t, pt):
                pe.wait_ge(dec_ready, t + 1)
                for bank, src in ((0, kk[:]), (1, M[pt][:, 0:RW]), (2, b[:]), (3, M[pt][:, RW:2 * RW])):
                    for p in range(PAIRS):
                        last = pe.transpose(B[bank][:, p * P:(p + 1) * P], src[:, p * P:(p + 1) * P], ident[:])
                    last.then_inc(turned4, 1)

            def multiply(t, r):
                if r == 0:
                    pe.wait_ge(krT_ready, 2 * t + 2)
                    pe.wait_ge(bkT_ready, 2 * t + 2)
                else:
                    pe.wait_ge(masked, 8 * t + 2)
                for n, (lhs, banks) in enumerate(((bT, ((4, 5), (2, 3))[r]), (kT, ((0, 1), (4, 5))[r]))):
                    for p in (2 * r, 2 * r + 1):
                        for o in range(2):
                            part = slice(o * RW_DIM, (o + 1) * RW_DIM)
                            cols = slice((p - 2 * r) * 2 * P, (p - 2 * r + 1) * 2 * P)
                            last = pe.matmul(B[banks[o]][:, cols], lhs[part, p, :], krT[part, p, :, :].rearrange("k n t -> k (n t)"), start=True, stop=True)
                    last.then_inc(products, 1)

            def turn_first(t, g):
                pe.wait_ge(XT_ready, 2 * LEVELS * t + g + 1)
                if g == 0:
                    pe.wait_ge(masked, 8 * t + 8)
                for h in range(4):
                    last = pe.transpose(B[3 * g][:, h * P:(h + 1) * P], XT[:, 4 * g + h, :], ident[:])
                last.then_inc(first_turned, 1)

            def level(t, l, g, stage):
                hs = range(4 * g, 4 * g + 4)
                done = 12 * t + 2 * (l - 1)
                top = l == LEVELS - 1
                if stage == 0:
                    pe.wait_ge(CT_ready, done + g + 1)
                    pe.wait_ge(X_ready, (2 * LEVELS - 2) * t + 2 * (l - 1) + g + 1)
                    width = P // 2 if top else P
                    for h in hs:
                        last = pe.matmul(B[3 * g][:, (h % 4) * P:(h % 4) * P + width], CT[:, h, :], X[:, h, 0:width], start=True, stop=True)
                    last.then_inc(T1_done, 1)
                else:
                    pe.wait_ge(T1_ready, done + g + 1)
                    pe.wait_ge(XT_ready, 2 * LEVELS * t + 2 * (l - 1) + g + 1)
                    if not top:
                        for h in hs:
                            pe.matmul(B[3 * g + 1][:, (h % 4) * HALF:(h % 4 + 1) * HALF], XT[:, h, :], halves_of(T1[:, h, :], l, 0), start=True, stop=True)
                    for h in hs:
                        lhs, rows = (T1[:, h, 0:HALF], HALF) if top else (T1[:, h, :], P)
                        last = pe.matmul(B[3 * g + 2][0:rows, (h % 4) * HALF:(h % 4 + 1) * HALF], lhs, halves_of(XT[:, h, :], l, 1), start=True, stop=True)
                    last.then_inc(corr_done, 1)

            def solve(t, pt):
                V = M[pt][:, 2 * RW:3 * RW]
                pe.wait_ge(S_in, t + 1)
                for p in range(PAIRS):
                    pe.matmul(B[0][:, p * P:(p + 1) * P], krT[:, p, 0, :], S[:, p, :], start=True, stop=False)
                    for o in range(2):
                        h = 2 * p + o
                        last = pe.matmul(B[0][:, h * RW_DIM:(h + 1) * RW_DIM], KA[:, h, 0, :], V[:, h * RW_DIM:(h + 1) * RW_DIM], start=False, stop=o == 1)
                last.then_inc(Z_done, 1)

            def read_out(t, pt):
                V = M[pt][:, 2 * RW:3 * RW]
                pe.wait_ge(XT_ready, 2 * LEVELS * t + 2 * LEVELS)
                pe.wait_ge(Z_ready, t + 1)
                for h in range(RW_HEADS):
                    cols = slice(h * RW_DIM, (h + 1) * RW_DIM)
                    last = pe.matmul(B[1][:, cols], XT[:, h, :], Z[:, cols], start=True, stop=True)
                last.then_inc(SA_done, 1)
                for p in range(PAIRS):
                    pe.matmul(B[2][:, p * P:(p + 1) * P], krT[:, p, 1, :], S[:, p, :], start=True, stop=False)
                    for o in range(2):
                        h = 2 * p + o
                        cols = slice(h * RW_DIM, (h + 1) * RW_DIM)
                        pe.matmul(B[2][:, cols], KA[:, h, 1, :], V[:, cols], start=False, stop=False)
                        if p == 0 and o == 0:
                            pe.wait_ge(SA_ready, t + 1)
                        last = pe.matmul(B[2][:, cols], BA[:, h, 1, :], SA[:, cols], start=False, stop=o == 1)
                last.then_inc(y_done, 1)
                for p in range(PAIRS):
                    cols = slice(p * P, (p + 1) * P)
                    pe.matmul(B[3][:, cols], b[:, cols], SA[:, cols], start=True, stop=False)
                    last = pe.matmul(B[3][:, cols], M[pt][:, RW + p * P:RW + (p + 1) * P], V[:, cols], start=False, stop=True)
                last.then_inc(inc_done, 1)

            def step(i, hi, pi, t, ht, pt):
                pr, m = i is not None, t is not None
                if m and isinstance(t, int) and t == 0:
                    pe.wait_ge(consts_in, 16 * CONSTS)
                if pr:
                    front.turn(pe, i, (taken[4], taken[2]))
                    project(i, 0).then_inc(chunk_ready, 1)
                if m:
                    turn_low(t, pt)
                if pr:
                    project(i, 1, 0, 256)
                if m:
                    raise_low(t)
                if pr:
                    project(i, 1, 256, 512).then_inc(chunk_ready, 1)
                    project(i, 3).then_inc(chunk_ready, 1)
                if m:
                    cumulate(t)
                if pr:
                    project(i, 2).then_inc(chunk_ready, 1)
                if m:
                    turn_all(t, pt)
                if pr:
                    project(i, 4, 0, 256)
                if m:
                    multiply(t, 0)
                    multiply(t, 1)
                if pr:
                    project(i, 4, 256, 512).then_inc(chunk_ready, 1)
                if m:
                    for g in range(2):
                        turn_first(t, g)
                    for l in range(1, LEVELS):
                        for g in range(2):
                            level(t, l, g, 0)
                        for g in range(2):
                            level(t, l, g, 1)
                    solve(t, pt)
                    read_out(t, pt)

            pipeline(pe, step)

        @block.scalar
        def _(act):
            act.wait_ge(set_up, 1)
            front.square(act, 0)

            def take(i, pi, c, t=None, ht=None, pt=None):
                pos = ORDER.index(c)
                act.wait_ge(chunk_ready, 5 * i + pos + 1)
                lo, hi = COLS[c]
                if c == 4:
                    need(act, taken[4], i)
                    act.activation(tanh, pj[0][:], ACT.Tanh, scale=0.5).then_inc(tanh_ready, 1)
                    return
                if c == 0:
                    if t is not None:
                        act.wait_ge(shifted[pt], shift_count(ht, pt))
                act.copy(U[pi][:, lo:hi], pj[pos % 2][:, 0:hi - lo]).then_inc(taken[c], 1)

            def step(i, hi, pi, t, ht, pt):
                pr, m = i is not None, t is not None
                if pr:
                    front.take(act, i)
                    take(i, pi, 0, t, ht, pt)
                if m:
                    act.wait_ge(mixed_in, t + 1)
                    act.activation(M[pt][:, 3 * RW:3 * RW + LORA], M[pt][:, 3 * RW:3 * RW + LORA], ACT.Tanh).then_inc(low_ready, 1)
                    act.wait_ge(low_turned, t + 1)
                    act.copy(lowT, B[0][:, 0:P]).then_inc(lowT_ready, 1)
                if pr:
                    take(i, pi, 1)
                if m:
                    act.wait_ge(wa_ready, t + 1)
                    act.activation(e_in[:], tmp[:], ACT.Tanh, scale=0.5)
                    act.activation(e_ex[:], tmp2[:], ACT.Tanh, scale=0.5).then_inc(wa_tanh, 1)
                if pr:
                    take(i, pi, 3)
                if m:
                    act.wait_ge(cum_done, t + 1)
                    act.wait_ge(lw_ready, t + 1)
                    act.activation(e_in[:], B[3][:], ACT.Exp)
                    act.activation(e_neg[:], B[3][:], ACT.Exp, scale=-1.0)
                    act.activation(e_ex[:], B[4][:], ACT.Exp)
                    act.activation(e_tot[:].rearrange("p h c -> p (h c)"), B[5][:, 0:2 * PAIRS], ACT.Exp).then_inc(exp_ready, 1)
                if pr:
                    take(i, pi, 2)
                if m:
                    for n in range(2):
                        act.wait_ge(turned4, 4 * t + n + 1)
                        act.copy(krT[:, :, n, :], heads(B[n][:], PAIRS)).then_inc(krT_ready, 1)
                if pr:
                    if not (isinstance(i, int) and i == TILES - 1):
                        front.square(act, i + 1)
                    take(i, pi, 4)
                if m:
                    for l in range(1, LEVELS):
                        for g in range(2):
                            act.wait_ge(T1_done, 12 * t + 2 * (l - 1) + g + 1)
                            width = HALF if l == LEVELS - 1 else P
                            act.copy(T1[:, 4 * g:4 * g + 4, 0:width], heads(B[3 * g][:], 4)[:, :, 0:width]).then_inc(T1_ready, 1)
                    act.wait_ge(Z_done, t + 1)
                    act.activation(Z[:], B[0][:], ACT.Copy, scale=-1.0).then_inc(Z_ready, 1)
                    act.wait_ge(SA_done, t + 1)
                    act.copy(SA[:], B[1][:]).then_inc(SA_ready, 1)
                    act.wait_ge(y_done, t + 1)
                    act.copy(y[:], B[2][:]).then_inc(y_ready, 1)

            pipeline(act, step)

        @block.gpsimd
        def _(pool):
            pool.memset(power[:], -0.5)
            pool.memset(front.power[:], -0.5)
            pool.memset(S[:], 0.0)
            pool.drain()
            pool.memset(rss[:], 0.0).then_inc(set_up, 1)
            front.root(pool, 0)

            def step(i, hi, pi, t, ht, pt):
                pr, m = i is not None, t is not None
                if m:
                    pool.wait_ge(ss_ready, t + 1)
                    pool.tensor_tensor(rss[:], ss[:], power[:], ALU.pow).then_inc(rss_ready, 1)
                if pr and not (isinstance(i, int) and i == TILES - 1):
                    front.root(pool, i + 1)
                if m:
                    pool.wait_ge(masked, 8 * t + 8)
                    for l in range(1, LEVELS):
                        for g in range(2):
                            if l > 1:
                                pool.wait_ge(T1_done, 12 * t + 2 * (l - 1) + g - 1)
                            pool.tensor_tensor(CT[:, 4 * g:4 * g + 4, :], BA[:, 4 * g:4 * g + 4, 0, :], again(blocks[:, l, :], 4), ALU.mult).then_inc(CT_ready, 1)
                    pool.wait_ge(var_ready, t + 1)
                    pool.tensor_tensor(rstd[:], var[:], power[:], ALU.pow).then_inc(rstd_ready, 1)

            pipeline(pool, step)

        @block.vector
        def _(dve):
            dve.wait_ge(set_up, 1)
            front.mean(dve, 0)
            front.scale(dve, 0)
            dve.wait_ge(consts_in, 16 * CONSTS)
            dve.drain()
            C2 = math.exp(-0.5) / 2

            def tt(out_, a_, b_, op):
                return dve.tensor_tensor(out_, a_, b_, op)

            def gates(t, ht, pt):
                dve.wait_ge(up_done, t + 1)
                tt(tmp[:], B[1][:], w0[:], ALU.add)
                tt(tmp2[:], B[2][:], a0[:], ALU.add).then_inc(wa_ready, 1)
                dve.wait_ge(wa_tanh, t + 1)
                dve.tensor_scalar(lw[:], e_in[:], -C2, -C2, ALU.mult, ALU.add)
                dve.tensor_scalar(a[:], e_ex[:], 0.5, 0.5, ALU.mult, ALU.add).then_inc(lw_ready, 1)

            def keys(t, pt):
                r, k = M[pt][:, 0:RW], M[pt][:, RW:2 * RW]
                tt(kk[:], k, k_k[:], ALU.mult)
                dve.drain()
                tt(tmp[:], kk[:], kk[:], ALU.mult)
                dve.scalar_tensor_tensor(tmp2[:], a[:], 1.0, k_a[:], ALU.subtract, ALU.mult)
                dve.drain()
                dve.tensor_reduce(ss[:], heads(tmp[:], RW_HEADS), AX, ALU.add)
                dve.scalar_tensor_tensor(k, tmp2[:], 1.0, k, ALU.add, ALU.mult)
                dve.drain()
                dve.tensor_scalar(ss[:], ss[:], 1e-24, None, ALU.max).then_inc(ss_ready, 1)
                tt(tmp2[:], r, k, ALU.mult)
                dve.drain()
                tt(tmp2[:], tmp2[:], r_k[:], ALU.mult)
                dve.drain()
                dve.tensor_reduce(bonus[:], heads(tmp2[:], RW_HEADS), AX, ALU.add)
                dve.wait_ge(rss_ready, t + 1)
                tt(heads(kk[:], RW_HEADS), heads(kk[:], RW_HEADS), spread(rss[:], RW_DIM), ALU.mult)
                dve.drain()
                tt(b[:], kk[:], a[:], ALU.mult)
                dve.drain()
                dve.wait_ge(exp_ready, t + 1)
                tt(kk[:], kk[:], e_ex[:], ALU.mult)
                tt(r, r, e_in[:], ALU.mult)
                tt(b[:], b[:], e_neg[:], ALU.mult)
                tt(k, k, e_neg[:], ALU.mult).then_inc(dec_ready, 1)
                for p in range(PAIRS):
                    last = dve.tensor_scalar(S[:, p, :], S[:, p, :], e_tot[:, p, 0:1], None, ALU.mult)
                last.then_inc(S_in, 1)

            def mask_products(t, r, n):
                dve.wait_ge(products, 4 * t + 2 * r + n + 1)
                banks = (((4, 5), (2, 3))[r], ((0, 1), (4, 5))[r])[n]
                dst = (BA, KA)[n]
                for o in range(2):
                    tt(dst[:, 4 * r + o:4 * r + 4:2].rearrange("p h n t -> p h (n t)"), heads(B[banks[o]][:], 2),
                       again(causal2[:].rearrange("p n t -> p (n t)"), 2), ALU.mult).then_inc(masked, 1)

            def first_level(t, g):
                hs = slice(4 * g, 4 * g + 4)
                tt(X[:, hs, :], BA[:, hs, 0, :], again(blocks[:, 0, :], 4), ALU.mult)
                dve.drain()
                tt(XT[:, hs, :], again(ident[:], 4), X[:, hs, :], ALU.subtract).then_inc(XT_ready, 1)

            def mix_shifted(i, hi, pi, part):
                if part == 0:
                    dve.wait_ge(shifted[pi], shift_count(hi, pi))
                    tt(M[pi][:], M[pi][:], U[pi][:], ALU.subtract)
                elif part == 1:
                    tt(M[pi][:], M[pi][:], mu[:], ALU.mult)
                else:
                    tt(M[pi][:], M[pi][:], U[pi][:], ALU.add).then_inc(mixed_in, 1)

            def step(i, hi, pi, t, ht, pt):
                pr, m = i is not None, t is not None
                if m:
                    gates(t, ht, pt)
                    dve.drain()
                    keys(t, pt)
                    for n in range(2):
                        dve.wait_ge(turned4, 4 * t + 3 + n)
                        dve.tensor_copy((bT, kT)[n][:], heads(B[2 + n][:], PAIRS)).then_inc(bkT_ready, 1)
                if pr and not (isinstance(i, int) and i == TILES - 1):
                    front.mean(dve, i + 1)
                    front.scale(dve, i + 1)
                if m:
                    mask_products(t, 0, 0)
                    mask_products(t, 0, 1)
                    dve.drain()
                    first_level(t, 0)
                    mask_products(t, 1, 0)
                    dve.drain()
                    first_level(t, 1)
                    mask_products(t, 1, 1)
                if pr:
                    dve.wait_ge(tanh_ready, i + 1)
                    dve.scalar_tensor_tensor(gate2[pi][:], tanh, 1.0, pj[0][:], ALU.add, ALU.mult).then_inc(taken[4], 1)
                    if not m:
                        for part in range(3):
                            mix_shifted(i, hi, pi, part)
                            dve.drain()
                if m:
                    for g in range(2):
                        if g == 0:
                            dve.drain()
                        dve.wait_ge(first_turned, 2 * t + g + 1)
                        dve.tensor_copy(X[:, 4 * g:4 * g + 4, :], heads(B[3 * g][:], 4)).then_inc(X_ready, 1)
                    for l in range(1, LEVELS):
                        for g in range(2):
                            hs = slice(4 * g, 4 * g + 4)
                            if g == 0:
                                dve.drain()
                            dve.wait_ge(corr_done, 12 * t + 2 * (l - 1) + g + 1)
                            compact = lambda bank, rows: bank[0:rows, 0:4 * HALF].rearrange("p (b w) -> p b w", w=1 << l)
                            view = lambda ap, rows, n: halves_of(ap[0:rows, hs, :].rearrange("p h t -> p (h t)"), l, n)
                            rows = HALF if l == LEVELS - 1 else P
                            if l < LEVELS - 1:
                                tt(view(X, P, 0), view(X, P, 0), compact(B[3 * g + 1], P), ALU.subtract).then_inc(X_ready, 1)
                            tt(view(XT, rows, 1), view(XT, rows, 1), compact(B[3 * g + 2], rows), ALU.subtract).then_inc(XT_ready, 1)
                        if pr and 1 <= l <= 3:
                            mix_shifted(i, hi, pi, l - 1)
                    dve.wait_ge(inc_done, t + 1)
                    tt(heads(tmp[:], PAIRS), heads(B[3][:], PAIRS), again(own_head[:], PAIRS), ALU.mult)
                    dve.drain()
                    tt(S[:], S[:], heads(tmp[:], PAIRS), ALU.add)
                    dve.drain()
                    for p in range(PAIRS):
                        last = dve.tensor_scalar(S[:, p, :], S[:, p, :], e_tot[:, p, 1:2], None, ALU.mult)
                    last.then_inc(S_out, 1)
                    H = lambda ap: heads(ap, RW_HEADS)
                    dve.wait_ge(y_ready, t + 1)
                    dve.tensor_reduce(mean[:], H(y[:]), AX, ALU.add)
                    dve.drain()
                    dve.tensor_scalar(mean[:], mean[:], 1.0 / RW_DIM, None, ALU.mult)
                    dve.drain()
                    tt(H(y[:]), H(y[:]), spread(mean[:], RW_DIM), ALU.subtract)
                    dve.drain()
                    tt(tmp[:], y[:], y[:], ALU.mult)
                    dve.drain()
                    dve.tensor_reduce(var[:], H(tmp[:]), AX, ALU.add)
                    dve.drain()
                    dve.tensor_scalar(var[:], var[:], 1.0 / RW_DIM, 64e-5, ALU.mult, ALU.add).then_inc(var_ready, 1)
                    need(dve, stored[pt], 16 * ht)
                    tt(H(tmp[:]), H(M[pt][:, 2 * RW:3 * RW]), spread(bonus[:], RW_DIM), ALU.mult)
                    dve.wait_ge(rstd_ready, t + 1)
                    tt(H(y[:]), H(y[:]), spread(rstd[:], RW_DIM), ALU.mult)
                    dve.drain()
                    tt(y[:], y[:], gn_g[:], ALU.mult)
                    tt(tmp[:], tmp[:], gn_b[:], ALU.add)
                    dve.drain()
                    tt(y[:], y[:], tmp[:], ALU.add)
                    dve.drain()
                    dve.scalar_tensor_tensor(out[pt][:], y[:], 0.5, gate2[pt][:], ALU.mult, ALU.mult).then_inc(out_ready, 1)

            pipeline(dve, step)


FX = 512
FX_HEADS = 8
FX_DIM = 64


def fox_project(nc, x, norm_g, w_in, q_g, k_g, b_f, masks, keysT, values, cum3, queries, gates):
    with ExitStack() as ctx:
        s = Stage(nc, ctx, "fp")
        sb, sem = s.sb, s.sem
        WIDTH = 4 * FX + FX_HEADS
        with ExitStack() as early:
            part = [early.enter_context(nc.sbuf_tensor(f"fp_part{n}", [FX_HEADS, SEQ], BF16)) for n in range(3)]
        w = sb("w", [P, KC, WIDTH])
        COLS = [(0, FX), (FX, 2 * FX), (2 * FX, 3 * FX), (3 * FX, 4 * FX), (4 * FX, WIDTH)]
        ident = sb("ident", [P, P])
        qk_gain = sb("qk_gain", [P, 2, FX_DIM])
        bias = sb("bias", [P, FX_HEADS])
        power = sb("power", [P, 2 * FX_HEADS])
        qk = [sb(f"qk{p}", [P, 2 * FX]) for p in range(2)]
        tanh = sb("tanh", [P, FX])
        gate2 = [sb(f"gate2{p}", [P, FX]) for p in range(2)]
        sq = sb("sq", [P, 2 * FX])
        ms, rms = sb("ms", [P, 2 * FX_HEADS]), sb("rms", [P, 2 * FX_HEADS])
        qT = [sb(f"qT{p}", [P, 4 * P]) for p in range(2)]
        forget = sb("forget", [P, TILES, FX_HEADS])
        fa, fe = sb("fa", [P, TILES, FX_HEADS]), sb("fe", [P, TILES, FX_HEADS])
        lf, cum, ones = (w[0:FX_HEADS, n, 0:SEQ] for n in (2, 3, 4))
        pj = [s.bank(f"pj{n}") for n in range(2)]
        tq = s.bank("tq")
        tf = [s.bank(f"tf{n}") for n in range(4)]
        tk = tf[0:2]
        front = Normed(s, x, norm_g, ident, [pj[1], pj[0]])

        consts_in, set_up = sem("consts_in"), sem("set_up")
        w_here = [sem(f"w_here{c}") for c in range(5)]
        chunk_ready, tanh_ready, high_ready = sem("chunk_ready"), sem("tanh_ready"), sem("high_ready")
        taken = [sem(f"taken{c}") for c in range(5)]
        ms_ready, rms_ready, qk_ready, turned, qT_ready, kT_ready = (sem(n) for n in ("ms_ready", "rms_ready", "qk_ready", "turned", "qT_ready", "kT_ready"))
        stored, gate_stored = ([sem(f"{n}{p}") for p in range(2)] for n in ("stored", "gate_stored"))
        forget_ready, exp_ready, ln_ready, soft_ready, forget_turned, parts_ready, parts_moved = (sem(n) for n in (
            "forget_ready", "exp_ready", "ln_ready", "soft_ready", "forget_turned", "parts_ready", "parts_moved"))
        block = s.block()
        CONSTS = 4

        @block.sync
        def _(sp):
            for dst, src in ((ident[:], masks["ident"]), (qk_gain[:, 0, :], row(q_g, 0, FX_DIM)),
                             (qk_gain[:, 1, :], row(k_g, 0, FX_DIM)), (bias[:], row(b_f, 0, FX_HEADS))):
                sp.dma_start(dst, src).then_inc(consts_in, 16)
            gate = RW_COLS + 3 * FX + FX_HEADS + 512
            front.load(sp, 0)
            front.load_gain(sp)
            at = RW_COLS
            for c, col in enumerate((at, at + FX, at + 2 * FX, at + 3 * FX + FX_HEADS + 512, at + 3 * FX)):
                lo, hi = COLS[c]
                load_columns(sp, w, w_in, [(lo, col, hi - lo)], w_here[c])

            def step(i, hi, pi, t, ht, pt):
                if i is not None:
                    if not (isinstance(i, int) and i == TILES - 1):
                        front.load(sp, i + 1)
                    sp.wait_ge(taken[3], i + 1)
                    sp.dma_start(gates[bass.ds(i * P, P), :], gate2[pi][:]).then_inc(gate_stored[pi], 16)
                if t is not None:
                    sp.wait_ge(qT_ready, t + 1)
                    sp.dma_start(queries[bass.ds(t * P, P), :], qT[pt][:]).then_inc(stored[pt], 16)

            pipeline(sp, step)
            sp.wait_ge(parts_ready, 1)
            for n in range(3):
                sp.dma_start(cum3[n * FX_HEADS:(n + 1) * FX_HEADS, :], part[n][:]).then_inc(parts_moved, 16)
            sp.wait_ge(parts_moved, 48)
            for p in range(2):
                sp.wait_ge(stored[p], 16 * TILES // 2)
                sp.wait_ge(gate_stored[p], 16 * TILES // 2)

        @block.tensor
        def _(pe):
            pe.wait_ge(consts_in, 16 * CONSTS)

            def project(i, c):
                lo, hi = COLS[c]
                if c == 0:
                    pe.wait_ge(front.ready, 2 * i + 2)
                if c >= 2:
                    pe.wait_ge(taken[c - 2], i + 1)
                if isinstance(i, int) and i == 0:
                    pe.wait_ge(w_here[c], 16)
                for kc in range(KC):
                    last = pe.matmul(pj[c % 2][:, 0:hi - lo], front.hT[:, kc, :], w[:, kc, lo:hi], start=kc == 0, stop=kc == KC - 1)
                last.then_inc(chunk_ready, 1)

            def step(i, hi, pi, t, ht, pt):
                if i is not None:
                    front.turn(pe, i, (taken[3], taken[4]))
                    for c in range(2):
                        project(i, c)
                if t is not None:
                    pe.wait_ge(qk_ready, t + 1)
                    for c in range(4):
                        pe.transpose(tq[:, c * P:(c + 1) * P], qk[pt][:, c * P:(c + 1) * P], ident[:])
                    for c in range(FX_HEADS):
                        last = pe.transpose(tk[c // 4][:, (c % 4) * P:(c % 4 + 1) * P], sq[:, c * P:(c + 1) * P], ident[:])
                    last.then_inc(turned, 1)
                if i is not None:
                    for c in range(2, 5):
                        project(i, c)

            pipeline(pe, step)
            pe.wait_ge(soft_ready, 1)
            for t in range(TILES):
                last = pe.transpose(tf[t // 4][0:FX_HEADS, (t % 4) * P:(t % 4 + 1) * P], forget[:, t, :], ident[:])
            last.then_inc(forget_turned, 1)

        @block.scalar
        def _(act):
            act.wait_ge(set_up, 1)
            front.square(act, 0)

            def step(i, hi, pi, t, ht, pt):
                if i is not None:
                    front.take(act, i)
                    act.wait_ge(chunk_ready, 5 * i + 1)
                    act.copy(qk[pi][:, 0:FX], pj[0][:]).then_inc(taken[0], 1)
                if t is not None:
                    act.wait_ge(turned, t + 1)
                    need(act, stored[pt], 16 * ht)
                    act.copy(qT[pt][:], tq[:]).then_inc(qT_ready, 1)
                    for n in range(2):
                        act.copy(keysT[:, 4 * n:4 * n + 4, bass.ds(t * P, P)], heads(tk[n][:], 4)).then_inc(high_ready, 1)
                if i is not None:
                    act.wait_ge(chunk_ready, 5 * i + 3)
                    act.copy(values[:, bass.ds(i, 1), :], pj[0][:].unsqueeze(1)).then_inc(taken[2], 1)
                    if not (isinstance(i, int) and i == TILES - 1):
                        front.square(act, i + 1)
                    act.wait_ge(chunk_ready, 5 * i + 4)
                    need(act, taken[3], i)
                    act.activation(tanh[:], pj[1][:], ACT.Tanh, scale=0.5).then_inc(tanh_ready, 1)

            pipeline(act, step)
            act.wait_ge(forget_ready, 1)
            act.activation(fe[:], fe[:], ACT.Exp, scale=-1.0).then_inc(exp_ready, 1)
            act.drain()
            act.activation(fe[:], fe[:], ACT.Ln, bias=1.0).then_inc(ln_ready, 1)

        @block.gpsimd
        def _(pool):
            pool.memset(power[:], -0.5)
            pool.memset(cum3[:], 0.0)
            pool.memset(front.power[:], -0.5)
            pool.drain()
            pool.memset(rms[:], 0.0).then_inc(set_up, 1)
            front.root(pool, 0)

            def step(i, hi, pi, t, ht, pt):
                if t is not None:
                    pool.wait_ge(ms_ready, t + 1)
                    pool.tensor_tensor(rms[:], ms[:], power[:], ALU.pow).then_inc(rms_ready, 1)
                if i is not None and not (isinstance(i, int) and i == TILES - 1):
                    front.root(pool, i + 1)

            pipeline(pool, step)

        @block.vector
        def _(dve):
            dve.wait_ge(consts_in, 16 * CONSTS)
            dve.wait_ge(set_up, 1)
            dve.tensor_scalar(qk_gain[:, 0, :], qk_gain[:, 0, :], FX_DIM ** -0.5, None, ALU.mult)
            dve.drain()
            front.mean(dve, 0)
            front.scale(dve, 0)
            H = 2 * FX_HEADS

            def step(i, hi, pi, t, ht, pt):
                if t is not None:
                    dve.wait_ge(taken[0], t + 1)
                    dve.tensor_tensor(sq[:], qk[pt][:], qk[pt][:], ALU.mult)
                    dve.drain()
                    dve.tensor_reduce(ms[:], heads(sq[:], H), AX, ALU.add)
                    dve.drain()
                    dve.tensor_scalar(ms[:], ms[:], 1.0 / FX_DIM, 1e-6, ALU.mult, ALU.add).then_inc(ms_ready, 1)
                    dve.wait_ge(rms_ready, t + 1)
                    dve.tensor_tensor(heads(qk[pt][:], H), heads(qk[pt][:], H), spread(rms[:], FX_DIM), ALU.mult)
                    dve.drain()
                    four = qk[pt][:].rearrange("p (n h d) -> p n h d", n=2, h=FX_HEADS)
                    q, k = four[:, 0], four[:, 1]
                    dve.tensor_tensor(q, q, again(qk_gain[:, 0, :], FX_HEADS), ALU.mult)
                    twice = [P, FX_HEADS, 2, FX_DIM]
                    dve.tensor_tensor(sq[:].rearrange("p (h n d) -> p h n d", h=FX_HEADS, n=2), k.unsqueeze(2).to_broadcast(twice),
                                      qk_gain[:, 1, :].unsqueeze(1).unsqueeze(1).to_broadcast(twice), ALU.mult).then_inc(qk_ready, 1)
                if i is not None:
                    dve.wait_ge(chunk_ready, 5 * i + 2)
                    dve.tensor_copy(qk[pi][:, FX:], pj[1][:]).then_inc(taken[1], 1)
                    dve.drain()
                if t is not None:
                    for n in range(2):
                        dve.wait_ge(high_ready, 2 * t + n + 1)
                        lower = keysT[FX_DIM:P, 4 * n:4 * n + 4, bass.ds(t * P, P)]
                        dve.tensor_tensor(lower, heads(tk[n][FX_DIM:P, :], 4), lower.bitcast(F32), ALU.subtract).then_inc(kT_ready, 1)
                if i is not None:
                    if not (isinstance(i, int) and i == TILES - 1):
                        front.mean(dve, i + 1)
                        front.scale(dve, i + 1)
                    need(dve, gate_stored[pi], 16 * hi)
                    dve.wait_ge(tanh_ready, i + 1)
                    dve.scalar_tensor_tensor(gate2[pi][:], tanh[:], 1.0, pj[1][:], ALU.add, ALU.mult).then_inc(taken[3], 1)
                    dve.wait_ge(chunk_ready, 5 * i + 5)
                    dve.tensor_copy(forget[:, bass.ds(i, 1), :], pj[0][:, 0:FX_HEADS].unsqueeze(1)).then_inc(taken[4], 1)

            pipeline(dve, step)
            dve.drain()
            dve.tensor_tensor(forget[:], forget[:], again(bias[:], TILES), ALU.add)
            dve.drain()
            dve.tensor_scalar(fa[:], forget[:], -1.0, None, ALU.mult)
            dve.drain()
            dve.tensor_tensor(fe[:], forget[:], fa[:], ALU.max).then_inc(forget_ready, 1)
            dve.tensor_scalar(fa[:], fa[:], 0.0, None, ALU.max)
            dve.drain()
            dve.wait_ge(ln_ready, 1)
            dve.tensor_tensor(forget[:], fa[:], fe[:], ALU.add).then_inc(soft_ready, 1)
            dve.wait_ge(forget_turned, 1)
            dve.memset(ones, 1.0)
            for n in range(4):
                dve.tensor_copy(lf[:, n * BANK:(n + 1) * BANK], tf[n][0:FX_HEADS, :])
            dve.drain()
            dve.tensor_tensor_scan(cum, ones, lf, 0.0, ALU.mult, ALU.add)
            dve.drain()
            for n in range(3):
                last = dve.tensor_copy(part[n][:], cum)
                dve.drain()
                if n < 2:
                    dve.tensor_tensor(cum, cum, part[n][:], ALU.subtract)
                    dve.drain()
            last.then_inc(parts_ready, 1)


GROUPS = 4
LAG = 3
UNITS = 2 * FX_HEADS
RING = 4
SPLIT_AT = (0, 4)


def forgetting_attention(nc, masks, keysT, values, cum3, queries, gates, mixed):
    with ExitStack() as ctx:
        s = Stage(nc, ctx, "fa")
        sb, sem = s.sb, s.sem
        ident = sb("ident", [P, P])
        ident16 = sb("ident16", [P, P], BF16)
        causal = sb("causal", [P, GROUPS, BANK], BF16)
        pick = sb("pick", [P, FX_HEADS, P], BF16)
        q_loaded = [sb(f"q_loaded{p}", [P, FX_HEADS, P]) for p in range(2)]
        qT = [Parts(s, f"qT{p}", [P, FX_HEADS, P]) for p in range(2)]
        gate2 = [sb(f"gate2{p}", [P, FX]) for p in range(2)]
        sm = [sb(f"sm{n}", [P, GROUPS * BANK]) for n in range(4)]
        tops, spare = ([sb(f"{name}{n}", [P, GROUPS]) for n in range(4)] for name in ("tops", "spare"))
        negtop = [sb(f"negtop{n}", [P, 1]) for n in range(4)]
        total = [sb(f"total{p}", [P, FX_HEADS]) for p in range(2)]
        rden = sb("rden", [P, FX_HEADS])
        pT = [sb(f"pT{n}", [P, 4, P]) for n in range(2)]
        o = sb("o", [P, FX])
        mix = [sb(f"mix{p}", [P, FX]) for p in range(2)]
        sc = [s.bank(f"sc{n}") for n in range(RING)]
        tp = [s.bank(f"tp{n}") for n in range(2)]
        ov = [s.bank(f"ov{n}") for n in range(2)]

        consts_in, set_up = sem("consts_in"), sem("set_up")
        q_here, q_high, q_ready, here, stored = ([sem(f"{n}{p}") for p in range(2)] for n in ("q_here", "q_high", "q_ready", "here", "stored"))
        (scored, topped, neg_ready, p_ready, p_turned, weighed, o_ready) = (sem(n) for n in (
            "scored", "topped", "neg_ready", "p_ready", "p_turned", "weighed", "o_ready"))
        pT_ready = [sem(f"pT_ready{n}") for n in range(2)]
        block = s.block()
        CONSTS = 3

        class At:

            def __init__(self, g, j):
                self.g, self.j, self.n = g, j, g + 1
                self.pair = 2 * g + j

            def unit(self, u):
                return UNITS * self.pair + u

            def chunk(self, u, c):
                return UNITS * self.g * (self.g + 1) + UNITS * self.n * self.j + self.n * u + c

            def tile(self, p):
                return 2 * self.pair + p

            def blocks(self, u, c):
                return 3 if u < FX_HEADS and c == self.n - 1 else 4

            def keys(self, u):
                return (self.n - 1) * BANK + self.blocks(u, self.n - 1) * P

        def pairs(eng, body):
            for j in range(2):
                body(At(0, j))
            for g in range(1, GROUPS):
                with eng.Fori(0, 2) as j:
                    body(At(g, j))

        def slots(at, ahead, late):
            for u in range(UNITS + LAG):
                for c in range(at.n):
                    if u < UNITS:
                        ahead(at, u, c)
                    if u >= LAG:
                        late(at, u - LAG, c)

        def turned_before(at, u, c):
            whole = UNITS // 2 * at.g * (at.g + 1) + UNITS // 2 * at.n * at.j
            return whole + (at.n * u + c) // 2

        @block.sync
        def _(sp):
            def load_q(t, p):
                rows = bass.ds(t * P, P)
                for odd in range(2):
                    src = queries[rows, :].rearrange("p (a t) -> p a t", a=4)[odd * FX_DIM:(odd + 1) * FX_DIM]
                    for copy in range(2):
                        dst = q_loaded[p][copy * FX_DIM:(copy + 1) * FX_DIM].rearrange("p (a b) t -> p a b t", b=2)[:, :, odd, :]
                        sp.dma_start(dst, src).then_inc(q_here[p], 16)

            def load(t, p):
                rows = bass.ds(t * P, P)
                sp.dma_start(gate2[p][:], gates[rows, :]).then_inc(here[p], 16)

            sp.dma_start(ident[:], masks["ident"]).then_inc(consts_in, 16)
            for n, src in enumerate((masks["causal4"], masks["pick"])):
                sp.dma_start(sm[n][:, 0:src.shape[1] * src.shape[2]], src.rearrange("p a b -> p (a b)")).then_inc(consts_in, 16)
            for p in range(2):
                load_q(p, p)
            for p in range(2):
                load(p, p)

            def finished(t, p):
                sp.wait_ge(o_ready, t + 1)
                sp.dma_start(mixed[bass.ds(t * P, P), :], mix[p][:]).then_inc(stored[p], 16)
                if t + 2 < TILES:
                    load(t + 2, p)

            for at in (At(g, j) for g in range(GROUPS) for j in range(2)):
                for p in range(2):
                    if at.tile(2) < TILES:
                        sp.wait_ge(q_ready[p], at.pair + 1)
                        load_q(at.tile(2 + p), p)
                for p in range(2):
                    finished(at.tile(p), p)
            for p in range(2):
                sp.wait_ge(stored[p], 16 * TILES // 2)

        @block.tensor
        def _(pe):
            pe.wait_ge(consts_in, 16 * CONSTS)
            pe.wait_ge(set_up, 1)

            def score(at, u, c):
                p, h = divmod(u, FX_HEADS)
                if h == 0 and c == 0:
                    pe.wait_ge(q_ready[p], at.pair + 1)
                if at.n * u + c >= RING:
                    pe.wait_ge(topped, at.chunk(u, c) - RING + 1)
                width = at.blocks(u, c) * P
                bank = sc[(at.n * u + c) % RING][:, 0:width]
                keys = slice(c * BANK, c * BANK + width)
                pe.matmul(bank, pick[:, h, :], cum3[:, keys], start=True, stop=False)
                if c == at.n - 1:
                    pe.matmul(bank, ident16[:], causal[:, bass.ds(2 * at.j + p, 1), 0:width].rearrange("q a k -> q (a k)"), start=False, stop=False)
                pe.matmul(bank, qT[p].high[:, h, :], keysT[:, h, keys], start=False, stop=False)
                pe.matmul(bank, qT[p].low[:, h, :], keysT[:, h, keys], start=False, stop=True).then_inc(scored, 1)

            def weigh(at, u, c):
                if c == 0:
                    pe.wait_ge(p_ready, at.unit(u) + 1)
                k = (at.n * u + c) % 2
                need(pe, pT_ready[k], turned_before(at, u, c))
                for m in range(at.blocks(u, c)):
                    last = pe.transpose(tp[k][:, m * P:(m + 1) * P], sm[u % 4][:, (4 * c + m) * P:(4 * c + m + 1) * P], ident[:])
                last.then_inc(p_turned, 1)
                if at.n * u + c > 0:
                    apply(at, *divmod(at.n * u + c - 1, at.n))
                if u == UNITS - 1 and c == at.n - 1:
                    apply(at, u, c)

            def apply(at, u, c):
                p, h = divmod(u, FX_HEADS)
                k = (at.n * u + c) % 2
                pe.wait_ge(pT_ready[k], turned_before(at, u, c) + 1)
                blocks = at.blocks(u, c)
                for m in range(blocks):
                    last = pe.matmul(ov[p][:, h * FX_DIM:(h + 1) * FX_DIM], pT[k][:, m, :],
                                     values[:, 4 * c + m, h * FX_DIM:(h + 1) * FX_DIM], start=c == 0 and m == 0, stop=c == at.n - 1 and m == blocks - 1)
                if c == at.n - 1:
                    last.then_inc(weighed, 1)

            pairs(pe, lambda at: slots(at, score, weigh))

        @block.scalar
        def _(act):
            def high(at, p):
                need(act, scored, at.chunk(0, 0))
                act.wait_ge(q_here[p], 64 * (at.pair + 1))
                act.copy(qT[p].high[:], q_loaded[p][:]).then_inc(q_high[p], 1)

            def soft(at, u, c):
                if u in SPLIT_AT and c == 0:
                    high(at, SPLIT_AT.index(u))
                if c == at.n - 1:
                    act.wait_ge(neg_ready, at.unit(u) + 1)
                    p, h = divmod(u, FX_HEADS)
                    view = sm[u % 4][:, 0:at.keys(u)]
                    act.activation(view, view, ACT.Exp, bias=negtop[u % 4][:], accum_out=total[p][:, h:h + 1]).then_inc(p_ready, 1)

            def nothing(at, u, c):
                pass

            pairs(act, lambda at: slots(at, soft, nothing))

        @block.vector
        def _(dve):
            dve.wait_ge(consts_in, 16 * CONSTS)
            dve.tensor_copy(ident16[:], ident[:])
            dve.tensor_copy(causal[:].rearrange("p a b -> p (a b)"), sm[0][:])
            dve.tensor_copy(pick[:].rearrange("p a b -> p (a b)"), sm[1][:, 0:FX_HEADS * P]).then_inc(set_up, 1)
            dve.drain()

            def low(at, p):
                dve.wait_ge(q_high[p], at.pair + 1)
                qT[p].take_low(dve, lambda ap: ap[:], q_loaded[p][:]).then_inc(q_ready[p], 1)

            def top(at, u, c):
                if u in SPLIT_AT and c == 0:
                    low(at, SPLIT_AT.index(u))
                if u >= 4 and c == 0:
                    dve.wait_ge(p_turned, at.chunk(u - 3, 0))
                dve.wait_ge(scored, at.chunk(u, c) + 1)
                width = at.blocks(u, c) * P
                dst, bank = sm[u % 4][:, c * BANK:c * BANK + width], sc[(at.n * u + c) % RING][:, 0:width]
                dve.tensor_scalar(dst, bank, 0.0, NEG, ALU.add, ALU.max, accum_out=tops[u % 4][:, c:c + 1]).then_inc(topped, 1)
                if c == at.n - 1:
                    dve.drain()
                    dve.tensor_scalar(spare[u % 4][:, 0:at.n], tops[u % 4][:, 0:at.n], -1.0, -NEG, ALU.mult, ALU.min, accum_out=negtop[u % 4][:]).then_inc(neg_ready, 1)

            def take_p(at, u, c):
                k = (at.n * u + c) % 2
                dve.wait_ge(p_turned, at.chunk(u, c) + 1)
                width = at.blocks(u, c)
                dve.tensor_copy(pT[k][:, 0:width, :], heads(tp[k][:], 4)[:, 0:width, :]).then_inc(pT_ready[k], 1)
                if u == FX_HEADS and c == 0:
                    finish(at, 0)
                if u == UNITS - 1 and c == at.n - 1:
                    finish(at, 1)

            def finish(at, p):
                dve.wait_ge(here[p], 16 * (at.pair + 1))
                need(dve, stored[p], 16 * at.pair)
                dve.wait_ge(p_ready, at.unit(FX_HEADS * (p + 1)))
                dve.reciprocal(rden[:], total[p][:])
                dve.drain()
                dve.wait_ge(weighed, at.unit(FX_HEADS * (p + 1)))
                dve.tensor_tensor(heads(o[:], FX_HEADS), heads(ov[p][:], FX_HEADS), spread(rden[:], FX_DIM), ALU.mult)
                dve.drain()
                dve.scalar_tensor_tensor(mix[p][:], o[:], 0.5, gate2[p][:], ALU.mult, ALU.mult).then_inc(o_ready, 1)

            pairs(dve, lambda at: slots(at, top, take_p))




def project_block(nc, name, x, w_out, blocks, final_g, masks, first_half, second_half, x_out):
    with ExitStack() as ctx:
        s = Stage(nc, ctx, name)
        sb, sem = s.sb, s.sem
        w = SplitWeights(s, [(0, BANK), (BANK, D)])
        ident = sb("ident", [P, P])
        gain = sb("gain", [P, D])
        power = sb("power", [P, 1])
        mix = [sb(f"mix{p}", [P, D]) for p in range(2)]
        xres = [sb(f"xres{p}", [P, D]) for p in range(2)]
        mixT = [Parts(s, f"mixT{p}", [P, KC, P]) for p in range(2)]
        z, square = sb("z", [P, D]), sb("square", [P, D])
        sq_sum, ms, rms = sb("sq_sum", [P, 1]), sb("ms", [P, 1]), sb("rms", [P, 1])
        y = [sb(f"y{p}", [P, D]) for p in range(2)]
        turned_banks = [s.bank(f"turned{g}") for g in range(2)]
        out = [[s.bank(f"out{p}{c}") for c in range(2)] for p in range(2)]
        ident_here, gain_here, set_up = sem("ident_here"), sem("gain_here"), sem("set_up")
        here, x_here, stored = ([sem(f"{n}{p}") for p in range(2)] for n in ("here", "x_here", "stored"))
        turned, high_ready, low_ready, out_done, z_ready, squared, ms_ready, rms_ready, y_ready = (sem(n) for n in (
            "turned", "high_ready", "low_ready", "out_done", "z_ready", "squared", "ms_ready", "rms_ready", "y_ready"))
        block = s.block()

        def tiles(eng, step):
            def pair(j):
                for p in range(2):
                    step(2 * j + p, j, p)
            pair(0)
            with eng.Fori(1, TILES // 2 - 1) as j:
                pair(j)
            pair(TILES // 2 - 1)

        def last(i):
            return isinstance(i, int) and i == TILES - 1

        @block.sync
        def _(sp):
            def load_mix(rows, p):
                sp.dma_start(mix[p][:, 0:BANK], first_half[rows, :]).then_inc(here[p], 16)
                sp.dma_start(mix[p][:, BANK:D], second_half[rows, :]).then_inc(here[p], 16)

            def load_x(rows, p):
                sp.dma_start(xres[p][:], x[rows, :]).then_inc(x_here[p], 16)

            sp.dma_start(ident[:], masks["ident"]).then_inc(ident_here, 16)
            load_mix(bass.ds(0, P), 0)
            for c, (lo, hi) in enumerate(w.cols):
                at = 0
                for src, n in blocks:
                    load_columns(sp, w.loaded[:, at:at + n, :], w_out[src * P:(src + n) * P, :], [(lo, lo, hi - lo)], w.here[c])
                    at += n
            load_mix(bass.ds(P, P), 1)
            for p in range(2):
                load_x(bass.ds(p * P, P), p)
            sp.dma_start(gain[:], row(final_g, 0, D)).then_inc(gain_here, 16)

            def step(i, hi, pi):
                rows = rows_of(sp, i)
                more = not (isinstance(i, int) and i >= TILES - 2)
                if more:
                    later = bass.ds((i + 2) * P if isinstance(i, int) else sp.snap((i + 2) * P), P)
                if more:
                    sp.wait_ge(turned, 2 * i + 2)
                    load_mix(later, pi)
                sp.wait_ge(y_ready, i + 1)
                sp.dma_start(x_out[rows, :], y[pi][:]).then_inc(stored[pi], 16)
                if more:
                    load_x(later, pi)

            tiles(sp, step)
            for p in range(2):
                sp.wait_ge(stored[p], 16 * TILES // 2)

        @block.tensor
        def _(pe):
            pe.wait_ge(ident_here, 16)

            def turn(i, hi, pi):
                pe.wait_ge(here[pi], 32 * (hi + 1))
                need(pe, low_ready, 2 * i)
                for g in range(2):
                    for c in range(4):
                        one = pe.transpose(turned_banks[g][:, c * P:(c + 1) * P], mix[pi][:, (4 * g + c) * P:(4 * g + c + 1) * P], ident[:])
                    one.then_inc(turned, 1)

            def step(i, hi, pi):
                if not last(i):
                    turn(i + 1, hi + pi, 1 - pi)
                pe.wait_ge(high_ready, 2 * i + 2)
                need(pe, z_ready, 2 * i - 2)
                for c in range(2):
                    if isinstance(i, int) and i == 0:
                        pe.wait_ge(w.low_ready[c], 1)
                    w.project(pe, out[pi][c][:], mixT[pi], c, lambda: c == 0 and pe.wait_ge(low_ready, 2 * i + 2)).then_inc(out_done, 1)

            turn(0, 0, 0)
            tiles(pe, step)

        @block.scalar
        def _(act):
            def take_high(i, pi):
                for g in range(2):
                    act.wait_ge(turned, 2 * i + g + 1)
                    act.copy(mixT[pi].high[:, 4 * g:4 * g + 4, :], heads(turned_banks[g][:], 4)).then_inc(high_ready, 1)

            def step(i, hi, pi):
                if not last(i):
                    take_high(i + 1, 1 - pi)
                if isinstance(i, int) and i == 0:
                    w.take_high_of(act, 1, len(blocks))
                act.wait_ge(z_ready, 2 * i + 2)
                act.activation(square[:], z[:], ACT.Square, accum_out=sq_sum[:]).then_inc(squared, 1)

            take_high(0, 0)
            w.take_high_of(act, 0, len(blocks))
            tiles(act, step)

        @block.gpsimd
        def _(pool):
            pool.memset(power[:], -0.5)
            pool.drain()
            pool.memset(rms[:], 0.0).then_inc(set_up, 1)

            def step(i, hi, pi):
                pool.wait_ge(ms_ready, i + 1)
                pool.tensor_tensor(rms[:], ms[:], power[:], ALU.pow).then_inc(rms_ready, 1)

            tiles(pool, step)

        @block.vector
        def _(dve):
            def take_low(i, pi):
                for g in range(2):
                    dve.wait_ge(high_ready, 2 * i + g + 1)
                    mixT[pi].take_low(dve, lambda ap: ap[:, 4 * g:4 * g + 4, :], heads(turned_banks[g][:], 4)).then_inc(low_ready, 1)

            def step(i, hi, pi):
                if not last(i):
                    take_low(i + 1, 1 - pi)
                if isinstance(i, int) and i == 0:
                    w.take_low_of(dve, 1)
                    dve.wait_ge(gain_here, 16)
                dve.wait_ge(x_here[pi], 16 * (hi + 1))
                for c in range(2):
                    dve.wait_ge(out_done, 2 * i + c + 1)
                    cols = slice(c * BANK, (c + 1) * BANK)
                    dve.tensor_tensor(z[:, cols], xres[pi][:, cols], out[pi][c][:], ALU.add).then_inc(z_ready, 1)
                dve.wait_ge(squared, i + 1)
                dve.tensor_scalar(ms[:], sq_sum[:], 1.0 / D, 1e-6, ALU.mult, ALU.add).then_inc(ms_ready, 1)
                need(dve, stored[pi], 16 * hi)
                dve.wait_ge(rms_ready, i + 1)
                dve.scalar_tensor_tensor(y[pi][:], z[:], rms[:], gain[:], ALU.mult, ALU.mult).then_inc(y_ready, 1)
                dve.drain()

            dve.wait_ge(set_up, 1)
            take_low(0, 0)
            w.take_low_of(dve, 0)
            tiles(dve, step)


BR = 256
A_COL, P_COL = 0, 1808
POOLS = 4
POOL_DIM = 64
A_TAPS = 3


def short_mixers(nc, x, norm_w, w_in, conv_w, pool_w, pool_scale, masks, mixed):
    with ExitStack() as ctx:
        s = Stage(nc, ctx, "sh")
        sb, sem = s.sb, s.sem
        w = SplitWeights(s, [(c * BANK, (c + 1) * BANK) for c in range(3)])
        ident = sb("ident", [P, P])
        taps = sb("taps", [P, A_TAPS, BR])
        scale = sb("scale", [P, BR])
        pw = sb("pw", [P, 2, POOL_DIM])
        window = sb("window", [P, POOLS, P])
        window_later = sb("window_later", [P, POOLS, P])
        window_prev = sb("window_prev", [P, POOLS, P])
        tmp_c = sb("tmp_c", [P, BR])
        tanh = sb("tanh", [P, 2, BR])
        U = [sb(f"U{p}", [P, BR]) for p in range(2)]
        back = [sb(f"back{n}", [P, BR]) for n in range(1, A_TAPS)]
        GB = [sb(f"GB{p}", [P, BR]) for p in range(2)]
        PU = [sb(f"PU{p}", [P, BR]) for p in range(2)]
        PG = [sb(f"PG{p}", [P, BR]) for p in range(2)]
        pu_prev = sb("pu_prev", [P, BR])
        zeros4 = sb("zeros4", [P, POOLS, P])
        part = [sb(f"part{n}", [P, BR]) for n in range(A_TAPS)]
        pooledT = sb("pooledT", [P, 2, P])
        out = [sb(f"out{p}", [P, 2 * BR]) for p in range(2)]
        pj = [s.bank(f"pj{n}") for n in range(2)]
        pooled = s.bank("pooled")
        mx = [s.bank(f"mx{n}") for n in range(2)]
        turned_banks = [s.bank(f"turned{n}") for n in range(2)]
        front = Normed(s, x, norm_w, ident, turned_banks, split=True)

        CONSTS = 11
        consts_in, set_up = sem("consts_in"), sem("set_up")
        chunk_ready, c_ready, tanh_b, b_free = (sem(n) for n in ("chunk_ready", "c_ready", "tanh_b", "b_free"))
        tanh_p, u_taken = sem("tanh_p"), sem("u_taken")
        taken = [sem(f"taken{c}") for c in range(3)]
        shifted, stored = ([sem(f"{n}{p}") for p in range(2)] for n in ("shifted", "stored"))
        conved, pool_done, pooledT_ready, mx_done, prev_kept, out_ready = (sem(n) for n in (
            "conved", "pool_done", "pooledT_ready", "mx_done", "prev_kept", "out_ready"))
        block = s.block()

        def shift_count(ht, pt):
            return 64 * ht + (32 if pt == 0 else 64)

        @block.sync
        def _(sp):
            small = [(ident[:], masks["ident"]), (scale[:], row(pool_scale, 0, BR)),
                     (window[:], masks["window_first"]), (window_later[:], masks["window"]), (window_prev[:], masks["window_prev"]),
                     (back[0][0:1, :], masks["zeros"][:, 0:BR]), (back[1][0:2, :], masks["zeros"][:, 0:2 * BR].rearrange("a (b c) -> (a b) c", b=2)),
                     (pw[:], pool_w.rearrange("(q o) c d -> (o c) q d", q=2))]
            small += [(taps[:, n, :], conv_w[n:n + 1, :].to_broadcast([P, BR])) for n in range(A_TAPS)]
            assert len(small) == CONSTS
            for dst, src in small:
                sp.dma_start(dst, src).then_inc(consts_in, 16)
            front.load(sp, 0)
            front.load_gain(sp)
            for c, (first, second) in enumerate(((A_COL, A_COL + 2 * BR), (A_COL + BR, A_COL + 3 * BR), (P_COL, P_COL + BR))):
                w.load(sp, w_in, c, [(c * BANK, first, BR), (c * BANK + BR, second, BR)])
            sp.wait_ge(consts_in, 16 * CONSTS)

            def shift(i, pi, first):
                if not first:
                    sp.wait_ge(conved, i)
                sp.wait_ge(taken[0], i + 1)
                for n in range(1, A_TAPS):
                    if not first:
                        sp.dma_start(back[n - 1][0:n, :], U[1 - pi][P - n:P, :]).then_inc(shifted[pi], 16)
                    sp.dma_start(back[n - 1][n:P, :], U[pi][0:P - n, :]).then_inc(shifted[pi], 16)

            def step(i, hi, pi, t, ht, pt):
                if i is not None:
                    if not (isinstance(i, int) and i == TILES - 1):
                        front.load(sp, i + 1)
                    shift(i, pi, t is None)
                if t is not None:
                    rows = rows_of(sp, t)
                    sp.wait_ge(out_ready, t + 1)
                    sp.dma_start(mixed[rows, 0:2 * BR], out[pt][:]).then_inc(stored[pt], 16)

            pipeline(sp, step)
            for p in range(2):
                sp.wait_ge(stored[p], 16 * TILES // 2)

        @block.tensor
        def _(pe):
            pe.wait_ge(consts_in, 16 * CONSTS)

            def project(i, c):
                if c == 0:
                    pe.wait_ge(front.ready, 2 * i + 2)
                need(pe, (taken[2], taken[1], taken[0])[c], (i, i, i + 1)[c])
                if isinstance(i, int) and i == 0:
                    pe.wait_ge(w.low_ready[c], 1)
                last = w.project(pe, pj[c % 2][:], front.parts, c, lambda: c == 0 and pe.wait_ge(front.low_ready, 2 * i + 2))
                last.then_inc(chunk_ready, 1)

            def pool_windows(t, pt):
                pe.wait_ge(u_taken, t + 1)
                pe.wait_ge(prev_kept, t + 1)
                for g in range(POOLS):
                    o, q = g % 2, g // 2
                    dst = pooled[o * POOL_DIM:(o + 1) * POOL_DIM, q * P:(q + 1) * P]
                    cols = slice(g * POOL_DIM, (g + 1) * POOL_DIM)
                    pe.matmul(dst, PU[pt][:, cols], window[:, g, :], start=True, stop=False)
                    last = pe.matmul(dst, pu_prev[:, cols], window_prev[:, g, :], start=False, stop=True)
                last.then_inc(pool_done, 1)

            def mix_pools(t):
                pe.wait_ge(pooledT_ready, t + 1)
                need(pe, out_ready, t)
                for q in range(2):
                    for o in range(2):
                        half = slice(o * POOL_DIM, (o + 1) * POOL_DIM)
                        last = pe.matmul(mx[o][:, q * POOL_DIM:(q + 1) * POOL_DIM], pooledT[half, q, :], pw[half, q, :], start=True, stop=True)
                last.then_inc(mx_done, 1)

            def step(i, hi, pi, t, ht, pt):
                pr, m = i is not None, t is not None
                if m:
                    pool_windows(t, pt)
                if pr:
                    front.turn(pe, i)
                    project(i, 0)
                if m:
                    mix_pools(t)
                if pr:
                    project(i, 1)
                    project(i, 2)

            pipeline(pe, step)

        @block.scalar
        def _(act):
            act.wait_ge(set_up, 1)
            front.square(act, 0)
            w.take_high_of(act, 0, 2)

            def step(i, hi, pi, t, ht, pt):
                pr, m = i is not None, t is not None
                if m:
                    act.wait_ge(pool_done, t + 1)
                    act.copy(pooledT[:], pooled[:, 0:2 * P].rearrange("p (q t) -> p q t", q=2)).then_inc(pooledT_ready, 1)
                if pr:
                    front.take(act, i)
                    if not m:
                        w.take_high_of(act, 1, 2)
                    act.wait_ge(chunk_ready, 3 * i + 1)
                    need(act, taken[0], i)
                    act.copy(tmp_c[:], pj[0][:, BR:]).then_inc(c_ready, 1)
                    if not (isinstance(i, int) and i == TILES - 1):
                        front.square(act, i + 1)
                    if not m:
                        w.take_high_of(act, 2, 2)
                    act.wait_ge(chunk_ready, 3 * i + 2)
                    need(act, taken[1], i)
                    act.activation(tanh[:, 0, :], pj[1][:, BR:], ACT.Tanh, scale=0.5).then_inc(tanh_b, 1)
                    act.wait_ge(chunk_ready, 3 * i + 3)
                    act.copy(PU[pi][:], pj[0][:, 0:BR]).then_inc(u_taken, 1)
                    need(act, taken[2], i)
                    act.activation(tanh[:, 1, :], pj[0][:, BR:], ACT.Tanh, scale=0.5).then_inc(tanh_p, 1)

            pipeline(act, step)

        @block.gpsimd
        def _(pool):
            pool.memset(front.power[:], -0.5)
            pool.drain()
            pool.memset(pu_prev[:], 0.0).then_inc(set_up, 1)
            pool.wait_ge(consts_in, 16 * CONSTS)
            front.root(pool, 0)

            def step(i, hi, pi, t, ht, pt):
                if i is not None and not (isinstance(i, int) and i == TILES - 1):
                    front.root(pool, i + 1)
                if t is not None:
                    pool.wait_ge(pool_done, t + 1)
                    if pt == 0:
                        pool.tensor_tensor(window[:], window_later[:], zeros4[:], ALU.add)
                    pool.tensor_tensor(pu_prev[:], PU[pt][:], zeros4[:, 0:2, :].rearrange("p a b -> p (a b)"), ALU.add).then_inc(prev_kept, 1)

            pool.memset(zeros4[:], 0.0)
            pool.drain()
            pool.memset(pu_prev[:], 0.0).then_inc(prev_kept, 1)
            pipeline(pool, step)

        @block.vector
        def _(dve):
            dve.wait_ge(consts_in, 16 * CONSTS)
            dve.wait_ge(set_up, 1)
            dve.tensor_scalar(scale[:], scale[:], 0.5, None, ALU.mult)
            dve.tensor_scalar(taps[:], taps[:], 0.5, None, ALU.mult)
            dve.drain()
            front.mean(dve, 0)
            front.scale(dve, 0)
            w.take_low_of(dve, 0)

            def step(i, hi, pi, t, ht, pt):
                pr, m = i is not None, t is not None
                if pr:
                    front.take_low(dve, i)
                if not m:
                    w.take_low_of(dve, 1)
                if m:
                    dve.wait_ge(shifted[pt], shift_count(ht, pt))
                    for n in range(A_TAPS):
                        src = U[pt] if n == 0 else back[n - 1]
                        last = dve.tensor_tensor(part[n][:], src[:], taps[:, A_TAPS - 1 - n, :], ALU.mult)
                    last.then_inc(conved, 1)
                    dve.drain()
                    dve.tensor_tensor(part[0][:], part[0][:], part[1][:], ALU.add)
                    dve.drain()
                    dve.tensor_tensor(part[0][:], part[0][:], part[2][:], ALU.add)
                    dve.drain()
                    need(dve, stored[pt], 16 * ht)
                    dve.tensor_tensor(out[pt][:, 0:BR], part[0][:], GB[pt][:], ALU.mult)
                if pr:
                    dve.wait_ge(c_ready, i + 1)
                    dve.tensor_tensor(U[pi][:], pj[0][:, 0:BR], tmp_c[:], ALU.mult).then_inc(taken[0], 1)
                if not m:
                    w.take_low_of(dve, 2)
                if m:
                    dve.wait_ge(mx_done, t + 1)
                    four = lambda ap: ap.rearrange("p (q o d) -> p q o d", q=2, o=2)
                    for o in range(2):
                        last = dve.tensor_tensor(four(out[pt][:, BR:])[:, :, o, :], mx[o][:, 0:2 * POOL_DIM].rearrange("p (q d) -> p q d", q=2),
                                                 four(PG[pt][:])[:, :, o, :], ALU.mult)
                    last.then_inc(out_ready, 1)
                if pr:
                    if not (isinstance(i, int) and i == TILES - 1):
                        front.mean(dve, i + 1)
                        front.scale(dve, i + 1)
                    dve.wait_ge(tanh_b, i + 1)
                    dve.scalar_tensor_tensor(GB[pi][:], tanh[:, 0, :], 1.0, pj[1][:, BR:], ALU.add, ALU.mult)
                    dve.drain()
                    dve.tensor_tensor(GB[pi][:], GB[pi][:], pj[1][:, 0:BR], ALU.mult).then_inc(taken[1], 1)
                    dve.wait_ge(tanh_p, i + 1)
                    dve.scalar_tensor_tensor(PG[pi][:], tanh[:, 1, :], 1.0, pj[0][:, BR:], ALU.add, ALU.mult).then_inc(taken[2], 1)
                    dve.drain()
                    dve.tensor_tensor(PG[pi][:], PG[pi][:], scale[:], ALU.mult)

            pipeline(dve, step)


GLA_K = 128
GLA_HEADS, GLA_V = 4, 64
RANK = 16
SSD_HEADS, SSD_DIM = 4, 64
XBC = 3 * BR
TAPS = 4
LOGS = GLA_K + SSD_HEADS
WIDE = XBC + RANK + SSD_HEADS
QKV_COL, LR_COL, GZ_COL, SZ_COL, XBC_COL, DT_COL = 1024, 1536, 1552, 2320, 2576, 3344


def recurrences(nc, x, norm_w, w_in, par, masks, mixed):
    with ExitStack() as ctx:
        s = Stage(nc, ctx, "rc")
        sb, sem = s.sb, s.sem
        COLS = [(0, BANK), (BANK, 2 * BANK), (2 * BANK, 3 * BANK), (3 * BANK, 2 * BANK + WIDE)]
        w = SplitWeights(s, COLS)
        ident = sb("ident", [P, P])
        after, halves = sb("after", [P, P]), sb("halves", [P, 2])
        chunk_ones = sb("chunk_ones", [P, 2, P])
        state_mask = sb("state_mask", [P, BANK])
        taps, conv_b = sb("taps", [P, TAPS, XBC]), sb("conv_b", [P, XBC])
        gate_w, gate_b = sb("gate_w", [RANK, GLA_K]), sb("gate_b", [P, GLA_K])
        dt_bias, rate, skip = sb("dt_bias", [P, SSD_HEADS]), sb("rate", [P, LOGS]), sb("skip", [P, SSD_HEADS])
        gla_norm, ssd_norm = sb("gla_norm", [P, GLA_V]), sb("ssd_norm", [P, BR])
        gla_gain = sb("gla_gain", [P, BR])
        power = sb("power", [P, GLA_HEADS + 1])
        QKV = [sb(f"QKV{p}", [P, BANK]) for p in range(2)]
        tanh = sb("tanh", [P, BANK])
        G2 = [sb(f"G2{p}", [P, BANK]) for p in range(2)]
        XB = [sb(f"XB{p}", [P, WIDE]) for p in range(2)]
        back = [sb(f"back{n}", [P, XBC]) for n in range(1, TAPS)]
        conv = sb("conv", [P, XBC])
        prod = sb("prod", [P, XBC])
        th = prod
        qT = sb("qT", [P, P])
        lrT = sb("lrT", [RANK, P])
        CT = sb("CT", [P, 2, P])
        la, neg, mag, soft = (sb(n, [P, LOGS]) for n in ("la", "neg", "mag", "soft"))
        e_rest = sb("e_rest", [P, LOGS])
        e_tot = sb("e_tot", [P, 2 + 2 * SSD_HEADS])
        kd, wx, wgt = sb("kd", [P, GLA_K]), sb("wx", [P, BR]), sb("wgt", [P, SSD_HEADS])
        upd = sb("upd", [P, BANK])
        S = [sb(f"S{c}", [P, BANK]) for c in range(2)]
        o, sq = sb("o", [P, BANK]), sb("sq", [P, BANK])
        ms, rms = sb("ms", [P, GLA_HEADS + 1]), sb("rms", [P, GLA_HEADS + 1])
        mix = [sb(f"mix{p}", [P, BANK]) for p in range(2)]
        pj = [s.bank(f"pj{n}") for n in range(2)]
        B = [s.bank(f"b{n}") for n in range(6)]
        front = Normed(s, x, norm_w, ident, [B[3], B[4]], split=True)

        ident_here = sem("ident_here")
        consts_in, set_up = sem("consts_in"), sem("set_up")
        chunk_ready, tanh_ready, rate_ready = sem("chunk_ready"), sem("tanh_ready"), sem("rate_ready")
        taken = [sem(f"taken{c}") for c in range(4)]
        shifted, stored = ([sem(f"{n}{p}") for p in range(2)] for n in ("shifted", "stored"))
        (small_turned, small_ready, q_ready, logit_done, neg_ready, soft_in, exp_ready, ln_ready, la_ready, rest_done, rest_ready) = (sem(n) for n in (
            "small_turned", "small_ready", "q_ready", "logit_done", "neg_ready", "soft_in", "exp_ready", "ln_ready", "la_ready", "rest_done", "rest_ready"))
        conv_used, conv_ready, th_ready, xbc_ready, C_turned, CT_ready, wx_ready, upd_done, S_ready = (sem(n) for n in (
            "conv_used", "conv_ready", "th_ready", "xbc_ready", "C_turned", "CT_ready", "wx_ready", "upd_done", "S_ready"))
        o_done, o_ready, ms_ready, rms_ready, mix_ready = (sem(n) for n in (
            "o_done", "o_ready", "ms_ready", "rms_ready", "mix_ready"))
        block = s.block()

        def shift_count(ht, pt):
            return 96 * ht + (48 if pt == 0 else 96)

        small = [(after[:], masks["chunk_after"]), (halves[:], masks["halves"]),
                 (chunk_ones[:], masks["chunk_ones"]), (state_mask[:], masks["state_mask"]), (conv_b[:], row(par["conv_b"], 0, XBC)),
                 (gate_w[:], par["gate_w"]), (gate_b[:], row(par["gate_b"], 0, GLA_K)), (dt_bias[:], row(par["dt_bias"], 0, SSD_HEADS)),
                 (rate[:, GLA_K:], row(par["a_log"], 0, SSD_HEADS)), (skip[:], row(par["d"], 0, SSD_HEADS)),
                 (gla_norm[:], row(par["gla_norm"], 0, GLA_V)), (ssd_norm[:], row(par["ssd_norm"], 0, BR))]
        small += [(taps[:, n, :], par["conv_w"][n:n + 1, :].to_broadcast([P, XBC])) for n in range(TAPS)]
        small += [(back[n - 1][0:n, :], masks["zeros"][:, 0:n * XBC].rearrange("a (b c) -> (a b) c", b=n)) for n in range(1, TAPS)]
        CONSTS = len(small)
        pieces = [[(0, QKV_COL, BANK)], [(BANK, GZ_COL, BR), (BANK + BR, SZ_COL, BR)], [(2 * BANK, XBC_COL, BANK)],
                  [(3 * BANK, XBC_COL + BANK, XBC - BANK), (2 * BANK + XBC, LR_COL, RANK), (2 * BANK + XBC + RANK, DT_COL, SSD_HEADS)]]

        @block.sync
        def _(sp):
            sp.dma_start(ident[:], masks["ident"]).then_inc(ident_here, 16)
            front.load(sp, 0)
            front.load_gain(sp)
            w.load(sp, w_in, 0, pieces[0])
            for dst, src in small:
                sp.dma_start(dst, src).then_inc(consts_in, 16)
            for c in range(1, 4):
                w.load(sp, w_in, c, pieces[c])
            sp.wait_ge(consts_in, 16 * CONSTS)

            def shift(i, pi, first):
                if not first:
                    sp.wait_ge(conv_used, i)
                sp.wait_ge(taken[2], i + 1)
                sp.wait_ge(taken[3], i + 1)
                for n in range(1, TAPS):
                    if not first:
                        sp.dma_start(back[n - 1][0:n, :], XB[1 - pi][P - n:P, 0:XBC]).then_inc(shifted[pi], 16)
                    sp.dma_start(back[n - 1][n:P, :], XB[pi][0:P - n, 0:XBC]).then_inc(shifted[pi], 16)

            def step(i, hi, pi, t, ht, pt):
                if i is not None:
                    if not (isinstance(i, int) and i == TILES - 1):
                        front.load(sp, i + 1)
                    shift(i, pi, t is None)
                if t is not None:
                    rows = rows_of(sp, t)
                    sp.wait_ge(mix_ready, 2 * t + 2)
                    sp.dma_start(mixed[rows, :], mix[pt][:]).then_inc(stored[pt], 16)

            pipeline(sp, step)
            for p in range(2):
                sp.wait_ge(stored[p], 16 * TILES // 2)

        @block.tensor
        def _(pe):
            pe.wait_ge(ident_here, 16)

            def project(i, c):
                lo, hi = COLS[c]
                if c < 2:
                    need(pe, taken[c + 2], i)
                else:
                    pe.wait_ge(taken[c - 2], i + 1)
                if c == 0:
                    pe.wait_ge(front.ready, 2 * i + 2)
                if isinstance(i, int) and i == 0:
                    pe.wait_ge(w.low_ready[c], 1)
                last = w.project(pe, pj[c % 2][:, 0:hi - lo], front.parts, c, lambda: c == 0 and pe.wait_ge(front.low_ready, 2 * i + 2))
                last.then_inc(chunk_ready, 1)

            def turn_small(t, pt):
                pe.wait_ge(taken[0], t + 1)
                pe.wait_ge(taken[3], t + 1)
                need(pe, o_ready, t)
                pe.transpose(B[0][:, 0:P], QKV[pt][:, 0:GLA_K], ident[:])
                pe.transpose(B[0][0:RANK, P:2 * P], XB[pt][:, XBC:XBC + RANK], ident[:]).then_inc(small_turned, 1)

            def logits(t):
                pe.wait_ge(small_ready, t + 1)
                pe.matmul(B[1][:, 0:GLA_K], lrT[:], gate_w[:], start=True, stop=True).then_inc(logit_done, 1)

            def rest(t):
                pe.wait_ge(la_ready, t + 1)
                pe.matmul(B[2][:, 0:LOGS], after[:], la[:], start=True, stop=True)
                pe.matmul(B[2][:, LOGS:LOGS + 2], la[:, 0:GLA_K], halves[:], start=True, stop=True)
                for c in range(2):
                    at = LOGS + 2 + c * SSD_HEADS
                    last = pe.matmul(B[2][:, at:at + SSD_HEADS], chunk_ones[:, c, :], la[:, GLA_K:], start=True, stop=True)
                last.then_inc(rest_done, 1)

            def turn_C(t):
                pe.wait_ge(xbc_ready, t + 1)
                for g in range(2):
                    last = pe.transpose(B[3][:, g * P:(g + 1) * P], conv[:, 2 * BR + g * P:2 * BR + (g + 1) * P], ident[:])
                last.then_inc(C_turned, 1)

            def update(t, pt):
                pe.wait_ge(wx_ready, t + 1)
                need(pe, S_ready, 2 * t)
                for c in range(2):
                    r = slice(c * CHUNK, (c + 1) * CHUNK)
                    bank = B[4 + c]
                    pe.matmul(bank[:, 0:BR], kd[r, :], QKV[pt][r, 2 * GLA_K:], start=True, stop=True)
                    for g in range(2):
                        last = pe.matmul(bank[:, BR + g * P:BR + (g + 1) * P], conv[r, BR + g * P:BR + (g + 1) * P], wx[r, g * P:(g + 1) * P], start=True, stop=True)
                    last.then_inc(upd_done, 1)

            def read_out(t):
                pe.wait_ge(CT_ready, t + 1)
                pe.wait_ge(q_ready, t + 1)
                for c in range(2):
                    pe.wait_ge(S_ready, 2 * t + c + 1)
                    r = slice(c * CHUNK, (c + 1) * CHUNK)
                    pe.matmul(B[0][r, 0:BR], qT[:, r], S[c][:, 0:BR], start=True, stop=True)
                    for g in range(2):
                        last = pe.matmul(B[0][r, BR + g * P:BR + (g + 1) * P], CT[:, g, r], S[c][:, BR + g * P:BR + (g + 1) * P], start=True, stop=True)
                last.then_inc(o_done, 1)

            def step(i, hi, pi, t, ht, pt):
                pr, m = i is not None, t is not None
                if m and isinstance(t, int) and t == 0:
                    pe.wait_ge(consts_in, 16 * CONSTS)
                if m:
                    turn_small(t, pt)
                if pr:
                    front.turn(pe, i)
                if m:
                    logits(t)
                if pr:
                    project(i, 0)
                if m:
                    rest(t)
                if pr:
                    project(i, 1)
                if pr:
                    project(i, 2)
                if m:
                    turn_C(t)
                    update(t, pt)
                if pr:
                    project(i, 3)
                if m:
                    read_out(t)

            pipeline(pe, step)

        @block.scalar
        def _(act):
            act.wait_ge(set_up, 1)
            front.square(act, 0)
            w.take_high_of(act, 0, len(pieces[0]))
            act.wait_ge(consts_in, 16 * CONSTS)
            act.activation(rate[:, GLA_K:], rate[:, GLA_K:], ACT.Exp).then_inc(rate_ready, 1)

            def step(i, hi, pi, t, ht, pt):
                pr, m = i is not None, t is not None
                if m:
                    act.wait_ge(small_turned, t + 1)
                    act.copy(lrT[:], B[0][0:RANK, P:2 * P]).then_inc(small_ready, 1)
                    act.copy(qT[:], B[0][:, 0:P]).then_inc(q_ready, 1)
                if pr:
                    front.take(act, i)
                if m:
                    act.wait_ge(soft_in, t + 1)
                    act.activation(mag[:], mag[:], ACT.Exp, scale=-1.0)
                    act.drain()
                    act.activation(mag[:], mag[:], ACT.Ln, bias=1.0).then_inc(ln_ready, 1)
                if pr:
                    if not m:
                        w.take_high_of(act, 1, len(pieces[1]))
                    act.wait_ge(chunk_ready, 4 * i + 1)
                    act.activation(QKV[pi][:, 0:GLA_K], pj[0][:, 0:GLA_K], ACT.Copy, scale=(GLA_K // GLA_HEADS) ** -0.5)
                    act.copy(QKV[pi][:, GLA_K:], pj[0][:, GLA_K:]).then_inc(taken[0], 1)
                if m:
                    act.wait_ge(rest_done, t + 1)
                    act.activation(e_rest[:], B[2][:, 0:LOGS], ACT.Exp)
                    act.activation(e_tot[:], B[2][:, LOGS:LOGS + 10], ACT.Exp).then_inc(rest_ready, 1)
                    act.wait_ge(conv_ready, t + 1)
                    act.activation(th[:], conv[:], ACT.Tanh).then_inc(th_ready, 1)
                if pr:
                    if not m:
                        w.take_high_of(act, 2, len(pieces[2]))
                    act.wait_ge(chunk_ready, 4 * i + 2)
                    need(act, taken[1], i)
                    act.activation(tanh[:], pj[1][:], ACT.Tanh, scale=0.5).then_inc(tanh_ready, 1)
                if pr:
                    if not m:
                        w.take_high_of(act, 3, len(pieces[3]))
                    act.wait_ge(chunk_ready, 4 * i + 3)
                    if t is not None:
                        act.wait_ge(shifted[pt], shift_count(ht, pt))
                    act.copy(XB[pi][:, 0:BANK], pj[0][:]).then_inc(taken[2], 1)
                if m:
                    act.wait_ge(C_turned, t + 1)
                    act.copy(CT[:], B[3][:, 0:BR].rearrange("p (g t) -> p g t", g=2)).then_inc(CT_ready, 1)
                if pr:
                    if not (isinstance(i, int) and i == TILES - 1):
                        front.square(act, i + 1)
                if pr:
                    act.wait_ge(chunk_ready, 4 * i + 4)
                    act.copy(XB[pi][:, BANK:WIDE], pj[1][:, 0:WIDE - BANK]).then_inc(taken[3], 1)
                if m:
                    act.wait_ge(o_done, t + 1)
                    need(act, mix_ready, 2 * t)
                    act.copy(o[:], B[0][:]).then_inc(o_ready, 1)

            pipeline(act, step)

        @block.gpsimd
        def _(pool):
            pool.memset(power[:], -0.5)
            pool.memset(rate[:, 0:GLA_K], 1.0 / 16.0)
            pool.memset(S[1][:], 0.0)
            pool.memset(front.power[:], -0.5)
            pool.drain()
            pool.memset(rms[:], 0.0).then_inc(set_up, 1)
            front.root(pool, 0)

            def step(i, hi, pi, t, ht, pt):
                pr, m = i is not None, t is not None
                if pr and not (isinstance(i, int) and i == TILES - 1):
                    front.root(pool, i + 1)
                if m:
                    pool.wait_ge(ms_ready, t + 1)
                    pool.tensor_tensor(rms[:], ms[:], power[:], ALU.pow)
                    pool.drain()
                    need(pool, stored[pt], 16 * ht)
                    pool.tensor_tensor(heads(o[:, 0:BR], 4), heads(o[:, 0:BR], 4), spread(rms[:, 0:4], GLA_V), ALU.mult)
                    pool.tensor_scalar(o[:, BR:], o[:, BR:], rms[:, 4:5], None, ALU.mult)
                    pool.tensor_tensor(G2[pt][:, 0:BR], G2[pt][:, 0:BR], gla_gain[:], ALU.mult)
                    pool.drain()
                    pool.tensor_tensor(mix[pt][:, 0:BR], o[:, 0:BR], G2[pt][:, 0:BR], ALU.mult).then_inc(mix_ready, 1)
                    pool.tensor_tensor(mix[pt][:, BR:], o[:, BR:], ssd_norm[:], ALU.mult).then_inc(mix_ready, 1)

            pipeline(pool, step)

        @block.vector
        def _(dve):
            dve.wait_ge(set_up, 1)
            front.mean(dve, 0)
            front.scale(dve, 0)
            w.take_low_of(dve, 0)
            dve.wait_ge(consts_in, 16 * CONSTS)
            dve.tensor_scalar(taps[:], taps[:], 0.5, None, ALU.mult)
            dve.tensor_scalar(conv_b[:], conv_b[:], 0.5, None, ALU.mult)
            dve.tensor_scalar(heads(gla_gain[:], 4), again(gla_norm[:], 4), 0.5, None, ALU.mult)
            dve.wait_ge(rate_ready, 1)
            dve.tensor_scalar(rate[:], rate[:], -1.0, None, ALU.mult)
            dve.drain()

            def softplus(t, pt):
                dve.wait_ge(logit_done, t + 1)
                dve.tensor_tensor(neg[:, 0:GLA_K], B[1][:, 0:GLA_K], gate_b[:], ALU.add).then_inc(neg_ready, 1)
                dve.tensor_tensor(neg[:, GLA_K:], XB[pt][:, XBC + RANK:WIDE], dt_bias[:], ALU.add)
                dve.drain()
                dve.tensor_scalar(neg[:, 0:GLA_K], neg[:, 0:GLA_K], -1.0, None, ALU.mult)
                dve.drain()
                dve.scalar_tensor_tensor(mag[:], neg[:], -1.0, neg[:], ALU.mult, ALU.max).then_inc(soft_in, 1)
                dve.wait_ge(ln_ready, t + 1)
                dve.scalar_tensor_tensor(soft[:], neg[:], 0.0, mag[:], ALU.max, ALU.add)
                dve.drain()
                dve.tensor_tensor(la[:], soft[:], rate[:], ALU.mult).then_inc(la_ready, 1)

            def convolve(t, ht, pt):
                dve.wait_ge(shifted[pt], shift_count(ht, pt))
                dve.tensor_tensor(conv[:], XB[pt][:, 0:XBC], taps[:, TAPS - 1, :], ALU.mult)
                dve.drain()
                dve.tensor_tensor(conv[:], conv[:], conv_b[:], ALU.add)
                for n in range(1, TAPS):
                    last = dve.tensor_tensor(prod[:], back[n - 1][:], taps[:, TAPS - 1 - n, :], ALU.mult)
                    if n == TAPS - 1:
                        last.then_inc(conv_used, 1)
                    dve.drain()
                    last = dve.tensor_tensor(conv[:], conv[:], prod[:], ALU.add)
                    if n < TAPS - 1:
                        dve.drain()
                last.then_inc(conv_ready, 1)

            def step(i, hi, pi, t, ht, pt):
                pr, m = i is not None, t is not None
                if pr:
                    front.take_low(dve, i)
                if not m:
                    for c in range(1, 4):
                        w.take_low_of(dve, c)
                if m:
                    softplus(t, pt)
                    convolve(t, ht, pt)
                    dve.wait_ge(th_ready, t + 1)
                    dve.scalar_tensor_tensor(conv[:], th[:], 1.0, conv[:], ALU.add, ALU.mult).then_inc(xbc_ready, 1)
                    dve.drain()
                    dve.wait_ge(rest_ready, t + 1)
                    dve.tensor_tensor(wgt[:], e_rest[:, GLA_K:], soft[:, GLA_K:], ALU.mult)
                    dve.tensor_tensor(kd[:], QKV[pt][:, GLA_K:2 * GLA_K], e_rest[:, 0:GLA_K], ALU.mult)
                    dve.drain()
                    dve.tensor_tensor(heads(wx[:], 4), heads(conv[:, 0:BR], 4), spread(wgt[:], SSD_DIM), ALU.mult).then_inc(wx_ready, 1)
                    dve.tensor_tensor(heads(sq[:, BR:], 4), heads(conv[:, 0:BR], 4), spread(skip[:], SSD_DIM), ALU.mult)
                if pr:
                    dve.wait_ge(tanh_ready, i + 1)
                    if m:
                        need(dve, mix_ready, 2 * t)
                    dve.scalar_tensor_tensor(G2[pi][:], tanh[:], 1.0, pj[1][:], ALU.add, ALU.mult).then_inc(taken[1], 1)
                if m:
                    for c in range(2):
                        dve.wait_ge(upd_done, 2 * t + c + 1)
                        dve.tensor_tensor(upd[:], B[4 + c][:], state_mask[:], ALU.mult)
                        src, dst = S[1 - c], S[c]
                        if c == 1:
                            need(dve, o_done, t)
                        dve.tensor_scalar(dst[:, 0:BR], src[:, 0:BR], e_tot[:, c:c + 1], None, ALU.mult)
                        dve.tensor_tensor(heads(dst[:, BR:], 4), heads(src[:, BR:], 4),
                                          spread(e_tot[:, 2 + 4 * c:6 + 4 * c], SSD_DIM), ALU.mult)
                        dve.drain()
                        dve.tensor_tensor(dst[:], dst[:], upd[:], ALU.add).then_inc(S_ready, 1)
                        dve.drain()
                if pr and not (isinstance(i, int) and i == TILES - 1):
                    front.mean(dve, i + 1)
                    front.scale(dve, i + 1)
                if m:
                    dve.wait_ge(o_ready, t + 1)
                    dve.tensor_tensor(o[:, BR:], o[:, BR:], sq[:, BR:], ALU.add)
                    dve.drain()
                    dve.scalar_tensor_tensor(o[:, BR:], o[:, BR:], 0.5, G2[pt][:, BR:], ALU.mult, ALU.mult)
                    dve.drain()
                    dve.tensor_tensor(sq[:], o[:], o[:], ALU.mult)
                    dve.drain()
                    dve.tensor_reduce(ms[:, 0:4], heads(sq[:, 0:BR], 4), AX, ALU.add)
                    dve.tensor_reduce(ms[:, 4:5], sq[:, BR:], AX, ALU.add)
                    dve.drain()
                    dve.tensor_scalar(ms[:, 0:4], ms[:, 0:4], 1.0 / GLA_V, 1e-6, ALU.mult, ALU.add)
                    dve.tensor_scalar(ms[:, 4:5], ms[:, 4:5], 1.0 / BR, 1e-6, ALU.mult, ALU.add)
                    dve.drain()
                    dve.tensor_copy(ms[:, 0:1], ms[:, 0:1]).then_inc(ms_ready, 1)

            pipeline(dve, step)


def constants():
    f32 = np.float32
    a = np.arange(P)
    s, t = a[:, None], a[None, :]
    same = (s // CHUNK) == (t // CHUNK)
    m = {"ident": np.eye(P), "chunk_upto": (s <= t) & same, "chunk_after": (s > t) & same,
         "halves": np.stack([a < P // 2, a >= P // 2], 1)}
    own = np.where(t <= s, 0.0, NEG)
    earlier = np.where(t > s, 0.0, NEG)
    m["band_first"] = np.concatenate([own, np.full((P, P), NEG)], 1)
    m["band_odd"] = np.concatenate([earlier, own], 1)
    freq = f32(500000.0) ** (-np.arange(0, 2 * ROPE, 2, dtype=f32) / f32(2 * ROPE))
    angle = np.arange(SEQ, dtype=f32)[:, None] * freq[None].astype(f32)
    m["rope"] = np.concatenate([np.cos(angle), np.sin(angle)], 1)
    first = (s < P // 2).astype(f32)
    m["from_mid"] = np.stack([(s <= t) - first, (s < t) - first], 1)
    m["causal2"] = np.stack([s < t, s <= t], 1)
    m["blocks"] = np.stack([((s >> (n + 1)) == (t >> (n + 1))) & ((s >> n) % 2 == 0) & ((t >> n) % 2 == 1) for n in range(LEVELS)], 1)
    m["own_head"] = (s // RW_DIM) == (t // RW_DIM)
    k = np.arange(BANK)[None]
    m["causal4"] = np.stack([np.where(k <= P * r + s, 0.0, NEG) for r in range(GROUPS)], 1)
    pick = np.zeros((3, FX_HEADS, FX_HEADS, P))
    for h in range(FX_HEADS):
        pick[:, h, h] = 1
    m["pick"] = np.concatenate([pick.reshape(3 * FX_HEADS, FX_HEADS, P), np.zeros((P - 3 * FX_HEADS, FX_HEADS, P))])
    sizes = (2, 4, 8, 16)
    def windows(count):
        return np.stack([((s <= t) & (s > t - n)) / count(n) - (s == t) for n in sizes], 1)
    m["window_first"] = windows(lambda n: np.minimum(t + 1, n))
    m["window"] = windows(lambda n: n)
    m["window_prev"] = np.stack([(s - P > t - n) / n for n in sizes], 1)
    m["chunk_ones"] = np.stack([np.broadcast_to(s < CHUNK, (P, P)), np.broadcast_to(s >= CHUNK, (P, P))], 1)
    v = np.arange(BR)[None]
    m["state_mask"] = np.concatenate([s // (GLA_K // GLA_HEADS) == v // GLA_V, np.ones((P, BR), bool)], 1)
    m["zeros"] = np.zeros((1, 4 * D))
    return {n: np.ascontiguousarray(c.astype(f32)) for n, c in m.items()}


def build_program(nc, a, c, out):
    x = a["x"][0]

    def scratch(name, shape):
        return nc.dram_tensor(name, shape, F32, kind="Internal").ap()

    x1, x2 = scratch("x1_dram", [SEQ, D]), scratch("x2_dram", [SEQ, D])
    mixed, queries, gates = (scratch(f"{n}_dram", [SEQ, BANK]) for n in ("mixed", "queries", "gates"))
    second_mix = scratch("second_mix_dram", [SEQ, BANK])
    hgrn(nc, x, a["w_in"][0], a["lb_logits"], a["hg_norm_w"], c, mixed)
    window_attention(nc, x, a["w_in"][0], a["w_out"][0], a["sinks"], a["ln_g"], a["ln_b"], c["rope"], c, mixed, x1)
    par = {n: a[f"rw_{n}_2"] for n in ("mu", "w0", "a0", "k_k", "k_a", "gn_g", "gn_b")}
    par |= {"w_up": a["rw_w_up_2"][0], "a_up": a["rw_a_up_2"][0], "r_k": a["rw_r_k_2"].rearrange("a h d -> a (h d)")}
    rwkv(nc, x1, a["norm_g_2"], a["w_in_2"][0], RW_COLS + 3 * FX + FX_HEADS, par, c, mixed)
    with ExitStack() as ctx:
        keysT = ctx.enter_context(nc.sbuf_tensor("keysT", [P, FX_HEADS, SEQ], F32R))
        values = ctx.enter_context(nc.sbuf_tensor("values", [P, TILES, FX], F32))
        cum3 = ctx.enter_context(nc.sbuf_tensor("cum3", [P, SEQ], BF16))
        fox_project(nc, x1, a["norm_g_2"], a["w_in_2"][0], a["fox_q_g_2"], a["fox_k_g_2"], a["fox_b_f_2"], c, keysT, values, cum3, queries, gates)
        forgetting_attention(nc, c, keysT, values, cum3, queries, gates, second_mix)
    project_block(nc, "po", x1, a["w_out_2"][0], ((0, KC),), a["final_g_2"].rearrange("(a d) -> a d", a=1), c, mixed, second_mix, x2)
    short_mixers(nc, x2, a["norm_w_3"], a["w_in_3"][0], a["conv_a_w_3"][0], a["pool_w_3"][0], a["pool_scale_3"], c, mixed)
    par = {"conv_w": a["ssd_conv_w_3"][0], "conv_b": a["ssd_conv_b_3"], "gate_w": a["gla_gate_w_3"][0], "gate_b": a["gla_gate_b_3"],
           "dt_bias": a["ssd_dt_bias_3"], "a_log": a["ssd_a_log_3"], "d": a["ssd_d_3"], "gla_norm": a["gla_norm_w_3"],
           "ssd_norm": a["ssd_norm_w_3"]}
    recurrences(nc, x2, a["norm_w_3"], a["w_in_3"][0], par, c, second_mix)
    project_block(nc, "pl", x2, a["w_out_3"][0], ((0, 2), (4, 2), (2, 2), (6, 2)), a["final_norm_w_3"].rearrange("(a d) -> a d", a=1),
                  c, mixed, second_mix, out[0])


INPUTS = ["x", "w_in", "lb_logits", "hg_norm_w", "sinks", "w_out", "ln_g", "ln_b", "norm_g_2", "w_in_2", "rw_mu_2", "rw_w_up_2",
          "rw_w0_2", "rw_a_up_2", "rw_a0_2", "rw_k_k_2", "rw_k_a_2", "rw_r_k_2", "rw_gn_g_2", "rw_gn_b_2", "fox_q_g_2", "fox_k_g_2",
          "fox_b_f_2", "w_out_2", "final_g_2", "norm_w_3", "w_in_3", "conv_a_w_3", "gla_gate_w_3", "gla_gate_b_3", "gla_norm_w_3",
          "pool_w_3", "pool_scale_3", "ssd_conv_w_3", "ssd_conv_b_3", "ssd_dt_bias_3", "ssd_a_log_3", "ssd_d_3", "ssd_norm_w_3",
          "w_out_3", "final_norm_w_3"]


def kernel(**inputs):
    import concourse.bacc as bacc
    from concourse.bass_utils import run_bass_kernel_spmd

    nc = bacc.Bacc("TRN2", target_bir_lowering=False, num_devices=1)
    arrays, a, c = {}, {}, {}
    for name in INPUTS:
        v = np.ascontiguousarray(inputs[name])
        arrays[f"in_{name}"] = v
        a[name] = nc.dram_tensor(f"in_{name}", v.shape, mybir.dt.from_np(v.dtype), kind="ExternalInput").ap()
    for name, v in constants().items():
        arrays[f"const_{name}"] = v
        c[name] = nc.dram_tensor(f"const_{name}", v.shape, F32, kind="ExternalInput").ap()
    out = nc.dram_tensor("out_dram", [1, SEQ, D], F32, kind="ExternalOutput").ap()
    build_program(nc, a, c, out)
    r = run_bass_kernel_spmd(nc, [arrays], core_ids=[0])
    return r.results[0]["out_dram"]
```
